# Optimizing a Trainium2 kernel written in Bass

```python
import math
import jax, jax.numpy as jnp
from jax import lax
import numpy as np

D_MODEL = 1024
BATCH = 1
SEQ = 256
DEPTH = 1

CONV_DIM = 512
CONV_WIDTH = 31
CONV_GROUPS = 8
N_HEADS = 8
HEAD_DIM = 64
ATTN_DIM = N_HEADS * HEAD_DIM
Q_BLOCK = 128
N_EXPERTS = 64
TOP_K = 8
N_GROUPS = 8
TOPK_GROUPS = 4
EXPERT_DIM = 256
SHARED_DIM = 256
ROUTED_SCALE = 2.5
TOKEN_CHUNK_MAX = 1024
EPS = 1e-6

OFF_CONV = 0
OFF_Q = OFF_CONV + 2 * CONV_DIM
OFF_K = OFF_Q + ATTN_DIM
OFF_V = OFF_K + ATTN_DIM
OFF_F = OFF_V + ATTN_DIM
OFF_GC = OFF_F + N_HEADS
OFF_GA = OFF_GC + D_MODEL
IN_COLS = OFF_GA + D_MODEL

kernel_name = "hybrid_conformer_fox_moe_block"

def rms_norm(x, g):
    xf = x.astype(jnp.float32)
    y = xf * lax.rsqrt(jnp.mean(xf * xf, axis=-1, keepdims=True) + EPS)
    return (y * g).astype(x.dtype)

def group_norm(u, g, b):
    B, S, C = u.shape
    uf = u.astype(jnp.float32).reshape(B, S, CONV_GROUPS, C // CONV_GROUPS)
    mu = jnp.mean(uf, axis=-1, keepdims=True)
    var = jnp.mean(jnp.square(uf - mu), axis=-1, keepdims=True)
    y = ((uf - mu) * lax.rsqrt(var + EPS)).reshape(B, S, C)
    return (y * g + b).astype(u.dtype)

def conformer_conv(a, gate, w_dw, b_dw, gn_g, gn_b, w_conv_out):
    u = a * jax.nn.sigmoid(gate)
    u = lax.conv_general_dilated(
        u, w_dw[:, None, :].astype(u.dtype), window_strides=(1,),
        padding=[(CONV_WIDTH - 1, 0)],
        dimension_numbers=('NWC', 'WIO', 'NWC'),
        feature_group_count=CONV_DIM) + b_dw
    u = jax.nn.silu(group_norm(u, gn_g, gn_b))
    return u @ w_conv_out

def forgetting_attention(q, k, v, log_f):
    S = q.shape[2]
    cum = jnp.cumsum(log_f, axis=-1)
    scale = HEAD_DIM ** -0.5
    neg = jnp.finfo(jnp.float32).min
    outs = []
    for i in range(S // Q_BLOCK):
        q0, q1 = i * Q_BLOCK, (i + 1) * Q_BLOCK
        s = jnp.einsum('bhqd,bhkd->bhqk', q[:, :, q0:q1], k[:, :, :q1],
                       preferred_element_type=jnp.float32) * scale
        s = s + cum[:, :, q0:q1, None] - cum[:, :, None, :q1]
        causal = (q0 + jnp.arange(Q_BLOCK))[:, None] >= jnp.arange(q1)[None, :]
        p = jax.nn.softmax(jnp.where(causal, s, neg), axis=-1)
        outs.append(jnp.einsum('bhqk,bhkd->bhqd', p.astype(v.dtype), v[:, :, :q1]))
    return jnp.concatenate(outs, axis=2)

def mixer_sublayer(h, w_in, w_dw, b_dw, gn_g, gn_b, w_conv_out, q_norm_g, k_norm_g,
                   b_forget, w_attn_out, w_out):
    B, S, _ = h.shape
    p = h @ w_in
    y_conv = conformer_conv(p[..., OFF_CONV:OFF_CONV + CONV_DIM],
                            p[..., OFF_CONV + CONV_DIM:OFF_Q],
                            w_dw, b_dw, gn_g, gn_b, w_conv_out)
    q = rms_norm(p[..., OFF_Q:OFF_K].reshape(B, S, N_HEADS, HEAD_DIM), q_norm_g)
    k = rms_norm(p[..., OFF_K:OFF_V].reshape(B, S, N_HEADS, HEAD_DIM), k_norm_g)
    v = p[..., OFF_V:OFF_F].reshape(B, S, N_HEADS, HEAD_DIM)
    log_f = jax.nn.log_sigmoid((p[..., OFF_F:OFF_GC] + b_forget).astype(jnp.float32))
    o = forgetting_attention(q.transpose(0, 2, 1, 3), k.transpose(0, 2, 1, 3),
                             v.transpose(0, 2, 1, 3), log_f.transpose(0, 2, 1))
    y_attn = o.transpose(0, 2, 1, 3).reshape(B, S, ATTN_DIM) @ w_attn_out
    merged = (jax.nn.sigmoid(p[..., OFF_GC:OFF_GA]) * y_conv
              + jax.nn.sigmoid(p[..., OFF_GA:IN_COLS]) * y_attn)
    return merged @ w_out

def moe_sublayer(h, w_router, router_bias, w_experts_gate_up, w_experts_down,
                 w_shared_gate_up, w_shared_down):
    B, S, D = h.shape
    T = B * S
    t = h.reshape(T, D)
    scores = jax.nn.sigmoid((t @ w_router).astype(jnp.float32))
    biased = scores + router_bias.astype(jnp.float32)
    grp = biased.reshape(T, N_GROUPS, N_EXPERTS // N_GROUPS)
    grp_score = lax.top_k(grp, 2)[0].sum(-1)
    _, gidx = lax.top_k(grp_score, TOPK_GROUPS)
    gmask = jax.nn.one_hot(gidx, N_GROUPS, dtype=jnp.float32).sum(1) > 0
    emask = jnp.repeat(gmask, N_EXPERTS // N_GROUPS, axis=-1)
    _, eidx = lax.top_k(jnp.where(emask, biased, -jnp.inf), TOP_K)
    w = jnp.take_along_axis(scores, eidx, axis=-1)
    w = w / jnp.sum(w, axis=-1, keepdims=True) * ROUTED_SCALE
    combine = jnp.sum(jax.nn.one_hot(eidx, N_EXPERTS, dtype=jnp.float32) * w[..., None],
                      axis=1).astype(h.dtype)
    chunk = math.gcd(T, TOKEN_CHUNK_MAX)

    def expert_chunk(args):
        tc, cc = args
        gu = jnp.einsum('cd,edf->cef', tc, w_experts_gate_up)
        act = jax.nn.silu(gu[..., :EXPERT_DIM]) * gu[..., EXPERT_DIM:] * cc[..., None]
        return jnp.einsum('cef,efd->cd', act, w_experts_down)

    routed = lax.map(expert_chunk, (t.reshape(T // chunk, chunk, D),
                                    combine.reshape(T // chunk, chunk, N_EXPERTS))).reshape(T, D)
    sgu = t @ w_shared_gate_up
    shared = (jax.nn.silu(sgu[:, :SHARED_DIM]) * sgu[:, SHARED_DIM:]) @ w_shared_down
    return (routed + shared).reshape(B, S, D)

def setup_inputs(seed: int = 0) -> dict:
    key = jax.random.key(seed)
    ks = jax.random.split(key, 24)
    L, D = DEPTH, D_MODEL
    f32 = jnp.float32

    def nrm(k, shape, scale):
        return jax.random.normal(k, shape, f32) * scale

    return {
        "x": nrm(ks[0], (BATCH, SEQ, D), 1.0),
        "c": nrm(ks[1], (BATCH, D), 1.0),
        "w_ada": nrm(ks[2], (L, D, 6 * D), 0.1 * D ** -0.5),
        "b_ada": nrm(ks[3], (L, 6 * D), 0.02),
        "norm1_g": 1.0 + nrm(ks[4], (L, D), 0.02),
        "w_in": nrm(ks[5], (L, D, IN_COLS), D ** -0.5),
        "w_dw": nrm(ks[6], (L, CONV_WIDTH, CONV_DIM), CONV_WIDTH ** -0.5),
        "b_dw": nrm(ks[7], (L, CONV_DIM), 0.02),
        "conv_gn_g": 1.0 + nrm(ks[8], (L, CONV_DIM), 0.02),
        "conv_gn_b": nrm(ks[9], (L, CONV_DIM), 0.02),
        "w_conv_out": nrm(ks[10], (L, CONV_DIM, D), CONV_DIM ** -0.5),
        "q_norm_g": 1.0 + nrm(ks[11], (L, HEAD_DIM), 0.02),
        "k_norm_g": 1.0 + nrm(ks[12], (L, HEAD_DIM), 0.02),
        "b_forget": 2.0 + nrm(ks[13], (L, N_HEADS), 0.1),
        "w_attn_out": nrm(ks[14], (L, ATTN_DIM, D), ATTN_DIM ** -0.5),
        "w_out": nrm(ks[15], (L, D, D), D ** -0.5),
        "norm2_g": 1.0 + nrm(ks[16], (L, D), 0.02),
        "w_router": nrm(ks[17], (L, D, N_EXPERTS), D ** -0.5),
        "router_bias": nrm(ks[18], (L, N_EXPERTS), 0.01),
        "w_experts_gate_up": nrm(ks[19], (L, N_EXPERTS, D, 2 * EXPERT_DIM), D ** -0.5),
        "w_experts_down": nrm(ks[20], (L, N_EXPERTS, EXPERT_DIM, D), EXPERT_DIM ** -0.5),
        "w_shared_gate_up": nrm(ks[21], (L, D, 2 * SHARED_DIM), D ** -0.5),
        "w_shared_down": nrm(ks[22], (L, SHARED_DIM, D), SHARED_DIM ** -0.5),
    }

def reference(x, c, w_ada, b_ada, norm1_g, w_in, w_dw, b_dw, conv_gn_g, conv_gn_b,
              w_conv_out, q_norm_g, k_norm_g, b_forget, w_attn_out, w_out, norm2_g,
              w_router, router_bias, w_experts_gate_up, w_experts_down,
              w_shared_gate_up, w_shared_down):
    for l in range(DEPTH):
        mod = jax.nn.silu(c) @ w_ada[l] + b_ada[l]
        shift1, scale1, gate1, shift2, scale2, gate2 = jnp.split(mod[:, None, :], 6, axis=-1)
        h = rms_norm(x, norm1_g[l]) * (1.0 + scale1) + shift1
        x = x + gate1 * mixer_sublayer(h, w_in[l], w_dw[l], b_dw[l], conv_gn_g[l], conv_gn_b[l],
                                       w_conv_out[l], q_norm_g[l], k_norm_g[l], b_forget[l],
                                       w_attn_out[l], w_out[l])
        h = rms_norm(x, norm2_g[l]) * (1.0 + scale2) + shift2
        x = x + gate2 * moe_sublayer(h, w_router[l], router_bias[l], w_experts_gate_up[l],
                                     w_experts_down[l], w_shared_gate_up[l], w_shared_down[l])
    return x


_drawn_inputs = setup_inputs


def setup_inputs(seed=0):
    import zlib

    import numpy as np

    out = dict(_drawn_inputs(seed))
    spreads = {}
    factors = {'b_ada': 3.036,
     'norm1_g': 8.0,
     'w_dw': 2.863,
     'b_dw': 8.0,
     'conv_gn_g': 8.0,
     'conv_gn_b': 8.0,
     'q_norm_g': 8.0,
     'k_norm_g': 8.0,
     'b_forget': 8.0,
     'w_attn_out': 3.801,
     'norm2_g': 8.0,
     'router_bias': 6.606}
    for name, (base, spread) in spreads.items():
        noise = np.random.default_rng([zlib.crc32(name.encode()), seed]).standard_normal(out[name].shape)
        drawn = base * np.exp(spread * noise) if base else spread * noise
        out[name] = __import__('jax').numpy.asarray(drawn.astype(out[name].dtype))
    for name, factor in factors.items():
        out[name] = (out[name] * factor).astype(out[name].dtype)
    return out
```

```python
import concourse.bass as bass
from concourse import mybir
from contextlib import ExitStack


def hybrid_conformer_fox_moe_block(
    nc, x, c, w_ada, b_ada, norm1_g, w_in, w_dw, b_dw, conv_gn_g, conv_gn_b, w_conv_out, q_norm_g,
    k_norm_g, b_forget, w_attn_out, w_out, norm2_g, w_router, router_bias, w_experts_gate_up,
    w_experts_down, w_shared_gate_up, w_shared_down, out,
):
    fp32, i32 = mybir.dt.float32, mybir.dt.int32
    ALU = mybir.AluOpType
    ACT = mybir.ActivationFunctionType
    AX = mybir.AxisListType.X

    PART = 128
    SEQ, D = x.shape[1], x.shape[2]
    TH = SEQ // PART
    KD = D // PART
    TAPS, CONV = w_dw.shape[1], w_dw.shape[2]
    KC = CONV // PART
    HEADS, HD = b_forget.shape[1], q_norm_g.shape[1]
    E, F = w_experts_gate_up.shape[1], w_experts_down.shape[2]
    KF = F // PART
    ATT = HEADS * HD
    OFF_Q = 2 * CONV
    OFF_F = OFF_Q + 3 * ATT
    OFF_G = OFF_F + HEADS
    GROUPS, EPG, TOPG, TOPK = 8, 8, 4, 8
    ROUTED_SCALE = 2.5
    EPS = 1e-6
    W = 512
    SLOTS = SEQ * TOPK
    PADDED = SLOTS + PART
    ITEMS = E + SLOTS // PART + 1
    NSLOT = 4
    SLOTW = KD * 2 * F + KF * D
    NBUF = 5
    BUFW = KD * W
    NEG = -1.0e30
    LOWEST = -87.0

    ctx = ExitStack()
    with ctx:
        def sb(name, shape, dt=fp32):
            return ctx.enter_context(nc.sbuf_tensor(name, shape, dt))

        def sem(name):
            return ctx.enter_context(nc.semaphore(name))

        ring = sb("ring", [PART, NSLOT * SLOTW])
        work = sb("work", [PART, KD * PADDED])
        xs = sb("xs", [PART, TH, D])
        gate2 = sb("gate2", [PART, D])
        misc = sb("misc", [PART, 2 * D])
        SI = sb("SI", [PART, TH, PART])
        ST = sb("ST", [PART, SEQ])
        iota = sb("iota", [PART, PADDED])
        sg = sb("sg", [PART, F])
        actT = sb("actT", [PART, KF, PART])
        ident = sb("ident", [PART, PART])
        before = sb("before", [PART, PART])
        ones = sb("ones", [PART, PART])
        blk = sb("blk", [PART, PART])
        causal = sb("causal", [PART, 2 * PART])
        headsum = sb("headsum", [PART, 8, 16])
        headrow = sb("headrow", [16, 8, PART])
        lower8 = sb("lower8", [PART, GROUPS, GROUPS])
        slotm = sb("slotm", [PART, TH, E])
        wt = sb("wt", [PART, TH, E])
        tab = sb("tab", [1, E + 1 + 2 * ITEMS], i32)
        freeat = sb("freeat", [1, E], i32)
        wf = sb("wf", [PART, KD, HEADS])
        convc = sb("convc", [PART, KC, TAPS + 3])
        qkg = sb("qkg", [PART, 2])
        bf = sb("bf", [HEADS, 1])
        sc = sb("sc", [PART, KD])
        st2 = sb("st2", [PART, 16])
        enum = sb("enum", [E, 1])
        wcol = sb("wcol", [PART, 1])

        def view(t, at, n, k=None):
            v = t[:, at:at + n]
            return v if k is None else v.rearrange("p (k n) -> p k n", k=k)

        TAIL = NBUF * BUFW
        h1T = view(work, 0, 2048, KD)
        gates = view(work, 2048, 4096, 2 * KD)
        upad = view(work, 6144, KC * 288, KC)
        gsig = view(work, 7296, 1024, KC)
        cacc = view(work, 8320, 1024, KC)
        sqb = view(work, 9344, 1024, KC)
        qk = view(work, 10368, 2048, 2 * KC)
        qksq = view(work, 12416, 2048, 2 * KC)
        v_sb = view(work, 14464, 1024, TH)
        oT = view(work, 15488, 1024, KC)
        router = view(work, 16512, KD * E, KD)
        small = view(work, 17024, 384)
        convrow = work[0:TAPS + 3, 0:CONV]
        qkrow = work[0:2, 512:640]
        crow = work[0:KD, 640:768]
        shift1, G1 = view(ring, TAIL, D), view(ring, TAIL + D, D)
        h1 = view(ring, TAIL + 2 * D, 2 * D, TH)
        gate1, shift2 = view(ring, TAIL, D), view(ring, TAIL + D, D)
        h2 = view(ring, TAIL + 2 * D, 2 * D, TH)
        G2, n2g = view(work, 0, D), view(work, D, D)
        bada = view(misc, 0, 1536, 3)
        sc_rep = view(iota, 0, 1024, KD)
        AU = view(misc, 0, 1024, KC)
        BU = view(misc, 1024, 1024, KC)
        zf = work[0:HEADS, 9344:9600]
        za = work[0:HEADS, 9600:9856]
        zl = work[0:HEADS, 9856:10112]
        cum = small[0:HEADS, 0:256]
        rs16 = ST[0:16, :]
        prob = view(work, 12416, 768, 2)
        probT = view(work, 13184, 768, 2)
        h2T = view(work, 10368, 2048, KD)
        shT = view(work, 2048, 512, 2)
        shg = view(work, 2560, 512, 2)
        r = {n: work[:, 3072 + 128 * i:3200 + 128 * i].rearrange("p (t e) -> p t e", t=TH)
             for i, n in enumerate(("z", "s", "b", "e", "pre", "m", "rep", "sel"))}
        rbias = work[:, 4096:4096 + E]
        top2 = work[:, 4160:4288].rearrange("p (t g e) -> p t g e", t=TH, g=GROUPS)
        gs = work[:, 4288:4304].rearrange("p (t g) -> p t g", t=TH)
        grank = work[:, 4304:4320].rearrange("p (t g) -> p t g", t=TH)
        gmask = work[:, 4320:4336].rearrange("p (t g) -> p t g", t=TH)
        top8 = work[:, 4336:4352].rearrange("p (t e) -> p t e", t=TH)
        cmp1 = work[:, 4352:4480].rearrange("p (t g h) -> p t g h", t=TH, g=GROUPS)
        cmp2 = work[:, 4480:4608].rearrange("p (t g h) -> p t g h", t=TH, g=GROUPS)
        cnt = work[:, 4608:4672]
        incl = work[:, 4672:4736]
        first = work[:, 4736:4800]
        nit = work[:, 4800:4864]
        cumi = work[:, 4864:4930]
        ecol = work[0:E, 4930:4932]
        ecum = work[0:E, 4932:4934]
        ecol2 = work[0:E, 4934:4938]
        slotT = SI[0:E, :, :].rearrange("p t s -> p (t s)")
        jt = work[0:E, 5200:5200 + 5 * ITEMS].rearrange("p (k j) -> p k j", k=5)
        Emat = ring[0:E, TAIL:TAIL + SLOTS]
        SS = misc[:, :].rearrange("p (b t s) -> p b t s", b=2, t=TH)
        hs = work[:, :].rearrange("p (k s) -> p k s", k=KD)
        y = view(misc, 0, D)
        hTi = view(misc, D, D, KD)
        act = sg

        bank = [ctx.enter_context(nc.psum_tensor(f"bank{i}", [PART, W], fp32)) for i in range(8)]
        acc = bank[4:8]
        psU, psY, psM = bank[0], bank[1:3], bank[3]

        def cols(w, n):
            return w[0, :, n:n + W].rearrange("(k p) n -> p k n", p=PART)

        pieces = [cols(w_ada, W * j) for j in range(4)]
        pieces += [cols(w_in, n) for n in (OFF_Q, OFF_Q + ATT, OFF_Q + 2 * ATT, CONV, 0)]
        pieces += [cols(w_in, OFF_G + W * j) for j in range(4)]
        pieces += [cols(w_ada, W * j) for j in range(4, 12)]
        pieces += [w_conv_out[0].rearrange("(k p) n -> p k n", p=PART),
                   w_attn_out[0].rearrange("(k p) n -> p k n", p=PART)]
        pieces += [cols(w_out, 0), cols(w_out, W), cols(w_shared_gate_up, 0),
                   w_shared_down[0].rearrange("(k p) n -> p k n", p=PART)]
        (ADA1, QP, KP, VP, GP, AP_, GATEP, ADA2, COUT, AOUT, WOUT, SHGU, SHD) = (
            0, 4, 5, 6, 7, 8, 9, 13, 21, 22, 23, 25, 26)

        def used_by():
            users = [(ada_done, j + 1) for j in range(4)]
            users += [(unit_done, 2 * j + 2) for j in range(9)]
            users += [(ada_done, j + 1) for j in range(4, 12)]
            return users + [(yc_done, 4), (ya_done, 4), (mo_done, 3), (mo_done, 4), (sgu_done, 2), (down_done, 1)]

        def piece(n):
            k, m = pieces[n].shape[1:]
            return view(ring, (n % NBUF) * BUFW, k * m, k)

        def expert_gu(b):
            return view(ring, b * SLOTW, KD * 2 * F, KD)

        def expert_dn(b):
            return view(ring, b * SLOTW + KD * 2 * F, KF * D, KF)

        piece_in = [sem(f"piece_in{i}") for i in range(NBUF)]
        expert_in = [sem(f"expert_in{i}") for i in range(NSLOT)]
        x_in, row_in, n1_in, n2_in, bada_in, wf_in, bf_in, rw_in, rb_in, out_done = map(sem, (
            "x_in", "row_in", "n1_in", "n2_in", "bada_in", "wf_in", "bf_in", "rw_in", "rb_in", "out_done"))
        upad_zero = sem("upad_zero")
        cst, pool_chain, sel_ready, aug_zero, iota_ready, pad_ready = map(sem, (
            "cst", "pool_chain", "sel_ready", "aug_zero", "iota_ready", "pad_ready"))
        dve_chain, act_chain = sem("dve_chain"), sem("act_chain")
        rowsT, rows_out, sc_ready, screp_ready = map(sem, ("rowsT", "rows_out", "sc_ready", "screp_ready"))
        ada_done, ada1_out, ada2_out = map(sem, ("ada_done", "ada1_out", "ada2_out"))
        ss_ready, sqrt_in, sqrt_out, h1_ready, h1T_ps, h1T_ready = map(sem, (
            "ss_ready", "sqrt_in", "sqrt_out", "h1_ready", "h1T_ps", "h1T_ready"))
        unit_done, unit_out_dve, unit_out_act, f_done = map(sem, (
            "unit_done", "unit_out_dve", "unit_out_act", "f_done"))
        qk_raw, qksq_ready, qkstat, qkrstd, qkb_done, qk_ready = map(sem, (
            "qk_raw", "qksq_ready", "qkstat", "qkrstd", "qkb_done", "qk_ready"))
        gsig_ready, u_ready, conv_step, f_step = map(sem, ("gsig_ready", "u_ready", "conv_step", "f_step"))
        zf_ready, lf_ready, aug_ready = map(sem, ("zf_ready", "lf_ready", "aug_ready"))
        s_done, max_done, exp_done, p_ready, pT_done, pT_out, o_done, o_out = map(sem, (
            "s_done", "max_done", "exp_done", "p_ready", "pT_done", "pT_out", "o_done", "o_out"))
        mean_done, dmu_ready, csq_ready, var_done, crstd, cb_done, yn_ready, cT_ready = map(sem, (
            "mean_done", "dmu_ready", "csq_ready", "var_done", "crstd", "cb_done", "yn_ready", "cT_ready"))
        yc_done, yc_out, ya_done, ya_out, merged, mo_done, x1_ready = map(sem, (
            "yc_done", "yc_out", "ya_done", "ya_out", "merged", "mo_done", "x1_ready"))
        h2_ready, h2T_ps, h2T_ready, logit_done, sgu_done, shg_ready, shT_ready = map(sem, (
            "h2_ready", "h2T_ps", "h2T_ready", "logit_done", "sgu_done", "shg_ready", "shT_ready"))
        z_ready, ez_ready, sel_out, rank_done, ecol_out, ecum_done, tabs_ps_in, tabs_ps, slotT_ps, slotT_out = map(sem, (
            "z_ready", "ez_ready", "sel_out", "rank_done", "ecol_out", "ecum_done", "tabs_ps_in", "tabs_ps",
            "slotT_ps", "slotT_out"))
        E_ready, m1_done, SS_ready, gather_ps, gather_out_act, gather_out_dve, tabs_ready = map(sem, (
            "E_ready", "m1_done", "SS_ready", "gather_ps", "gather_out_act", "gather_out_dve", "tabs_ready"))
        hT_ready, up_done, silu_done, act_ready, t_done, actT_ready, si_ready, sit_done, st_ready, down_done, y_ready, all_done, fin = map(sem, (
            "hT_ready", "up_done", "silu_done", "act_ready", "t_done", "actT_ready", "si_ready", "sit_done",
            "st_ready", "down_done", "y_ready", "all_done", "fin"))

        ADA_B = [1, 2, 3, 4]
        H1T_B = [5, 6, 7, 0]
        UNIT_B = [1, 2, 3, 4]
        UNITS = ["q", "q", "k", "k", "v", "v", "g", "g", "a", "a"] + ["m"] * 8
        S_B, PT_B, O_B = [0, 1], [2, 3], [4, 5]

        block = ctx.enter_context(nc.Block())

        @block.sync
        def _(sp):
            sp.dma_start(crow, c[0].rearrange("(k p) -> k p", p=PART)).then_inc(row_in, 16)
            users = used_by()
            for n in range(len(pieces)):
                if n >= NBUF:
                    sp.wait_ge(*users[n - NBUF])
                    sp.wait_ge(piece_in[n % NBUF], 16 * (n // NBUF))
                sp.dma_start(piece(n), pieces[n]).then_inc(piece_in[n % NBUF], 16)
                if n == 0:
                    sp.dma_start(xs[:, :, :], x[0].rearrange("(t p) d -> p t d", p=PART)).then_inc(x_in, 16)

            def load_expert(e, b):
                sp.dma_start(expert_gu(b), w_experts_gate_up[0, bass.ds(e, 1), :, :].rearrange(
                    "o (k p) n -> p (o k) n", p=PART)).then_inc(expert_in[b], 16)
                sp.dma_start(expert_dn(b), w_experts_down[0, bass.ds(e, 1), :, :].rearrange(
                    "o (k p) n -> p (o k) n", p=PART)).then_inc(expert_in[b], 16)

            sp.wait_ge(*users[WOUT])
            sp.wait_ge(*users[WOUT + 1])
            load_expert(2, 2)
            sp.wait_ge(*users[SHGU])
            sp.wait_ge(*users[SHD])
            load_expert(0, 0)
            load_expert(1, 1)
            sp.wait_ge(gather_ps, 4 * KD)
            sp.wait_ge(m1_done, 4)
            load_expert(3, 3)
            sp.wait_ge(tabs_ready, 1)
            with sp.Fori(1, E // NSLOT) as g:
                for b in range(NSLOT):
                    e = g * NSLOT + b
                    free = sp.value_load(freeat[0:1, bass.ds(e - NSLOT, 1)], min_val=1, max_val=ITEMS)
                    sp.wait_ge(expert_in[b], g * 32)
                    sp.wait_ge(down_done, free)
                    load_expert(e, b)
            for t in range(TH):
                for n in range(2):
                    sp.wait_ge(fin, t * 2 + n + 1)
                    sp.dma_start(out[0, t * PART:(t + 1) * PART, n * W:(n + 1) * W],
                                 xs[:, t, n * W:(n + 1) * W]).then_inc(out_done, 16)
            sp.wait_ge(out_done, 16 * TH * 2)

        @block.gpsimd
        def _(pool):
            chain = [0]

            def link(ins):
                chain[0] += 1
                ins.then_inc(pool_chain, 1)
                pool.wait_ge(pool_chain, chain[0])

            link(pool.memset(ident[:, :], 0.0))
            pool.affine_select(out=ident[:, :], in_=ident[:, :], compare_op=ALU.not_equal, fill=1.0, base=0,
                               pattern=[[-1, PART]], channel_multiplier=1).then_inc(cst, 1)
            pool.memset(ones[:, :], 1.0).then_inc(cst, 1)
            link(pool.memset(headsum[:, :, :], 0.0))
            link(pool.memset(headrow[:, :, :], 0.0))
            for half in range(2):
                hr = headrow[:, :, half * HD:(half + 1) * HD]
                link(pool.affine_select(out=headsum[half * HD:(half + 1) * HD, :, :],
                                        in_=headsum[half * HD:(half + 1) * HD, :, :],
                                        compare_op=ALU.not_equal, fill=1.0 / HD, base=half,
                                        pattern=[[2, 8], [-1, 16]], channel_multiplier=0))
                link(pool.affine_select(out=hr, in_=hr, compare_op=ALU.not_equal, fill=1.0, base=-half,
                                        pattern=[[-2, 8], [0, HD]], channel_multiplier=1))
            link(pool.memset(blk[:, :], 0.0))
            for half in range(2):
                link(pool.memset(blk[half * HD:(half + 1) * HD, half * HD:(half + 1) * HD], 1.0 / HD))
            pool.memset(upad[:, :, 0:TAPS - 1], 0.0).then_inc(upad_zero, 1)
            link(pool.memset(causal[:, :], 0.0))
            link(pool.affine_select(out=causal[:, :], in_=causal[:, :], compare_op=ALU.is_ge, fill=NEG, base=PART,
                                    pattern=[[-1, 2 * PART]], channel_multiplier=1))
            link(pool.memset(before[:, :], 0.0))
            link(pool.affine_select(out=before[:, :], in_=before[:, :], compare_op=ALU.is_ge, fill=1.0, base=0,
                                    pattern=[[-1, PART]], channel_multiplier=1))
            link(pool.iota(enum[:, :], pattern=[[0, 1]], base=0, channel_multiplier=1,
                           allow_small_or_imprecise_dtypes=True))
            link(pool.memset(lower8[:, :, :], 0.0))
            pool.affine_select(out=lower8[:, :, :], in_=lower8[:, :, :], compare_op=ALU.is_ge, fill=1.0, base=0,
                               pattern=[[-1, GROUPS], [1, GROUPS]], channel_multiplier=0).then_inc(sel_ready, 1)
            pool.wait_ge(sel_ready, 1)
            pool.wait_ge(ada_done, 12)
            link(pool.memset(misc[:, :], 0.0))
            for t, rows in ((AU, 32), (BU, 0)):
                for par in range(2):
                    a = t[64 * par + rows:64 * par + rows + HEADS, :, :]
                    pool.affine_select(out=a, in_=a, compare_op=ALU.not_equal, fill=1.0, base=-par,
                                       pattern=[[-2, KC], [0, SEQ]], channel_multiplier=1).then_inc(aug_zero, 1)
                    pool.wait_ge(aug_zero, (1 if t is BU else 0) * 2 + par + 1)
            pool.iota(iota[:, :], pattern=[[1, PADDED]], base=0, channel_multiplier=0,
                      allow_small_or_imprecise_dtypes=True).then_inc(iota_ready, 1)
            pool.wait_ge(iota_ready, 1)
            pool.wait_ge(SS_ready, 8)
            pool.wait_ge(tabs_ready, 1)
            pool.memset(hs[:, :, SLOTS:PADDED], 0.0).then_inc(pad_ready, 1)

        @block.scalar
        def _(a):
            chain = [0]

            def link(ins):
                chain[0] += 1
                ins.then_inc(act_chain, 1)
                a.wait_ge(act_chain, chain[0])

            for i, (src, n) in enumerate(((w_dw[0], TAPS), (b_dw, 1), (conv_gn_g, 1), (conv_gn_b, 1))):
                a.dma_start(convrow[(0, TAPS, TAPS + 1, TAPS + 2)[i]:(0, TAPS, TAPS + 1, TAPS + 2)[i] + n, :],
                            src).then_inc(row_in, 16)
            for i, g in enumerate((q_norm_g, k_norm_g)):
                for half in range(2):
                    a.dma_start(qkrow[i:i + 1, half * HD:(half + 1) * HD], g).then_inc(row_in, 16)
            for q in range(4):
                a.dma_start(bada[32 * q:32 * q + 1, :, :],
                            b_ada[0:1, q * 1536:(q + 1) * 1536].rearrange("o (k n) -> o k n", k=3)).then_inc(bada_in, 16)
            a.dma_start(G1, norm1_g.broadcast_to([PART, D])).then_inc(n1_in, 16)
            a.dma_start(bf[:, :], b_forget[0].rearrange("(h o) -> h o", o=1)).then_inc(bf_in, 16)
            with nc.allow_non_contiguous_dma(reason="eight columns of w_in"):
                a.dma_start(wf[:, :, :], w_in[0, :, OFF_F:OFF_F + HEADS].rearrange("(k p) n -> p k n", p=PART)).then_inc(wf_in, 16)
            a.dma_start(router, w_router[0].rearrange("(k p) n -> p k n", p=PART)).then_inc(rw_in, 16)

            a.wait_ge(rowsT, 1)
            a.activation(sc[:, :], bank[0][:, 0:KD], ACT.Silu).then_inc(sc_ready, 1)
            a.wait_ge(x_in, 16)
            for t in range(TH):
                a.activation(h1[:, t, :], xs[:, t, :], ACT.Square, accum_out=st2[:, t:t + 1]).then_inc(ss_ready, 1)
            a.wait_ge(sqrt_in, 1)
            a.activation(st2[:, 4:6], st2[:, 2:4], ACT.Sqrt).then_inc(sqrt_out, 1)
            for i in range(4):
                a.wait_ge(h1T_ps, i + 1)
                a.activation(h1T[:, 2 * i:2 * i + 2, :], bank[H1T_B[i]][:, :].rearrange("p (k n) -> p k n", k=2),
                             ACT.Copy).then_inc(h1T_ready, 1)
            for u in range(4):
                a.wait_ge(qk_raw, u + 1)
                a.activation(qksq[:, 2 * u:2 * u + 2, :], qk[:, 2 * u:2 * u + 2, :], ACT.Square).then_inc(qksq_ready, 1)
            for u in (4, 5):
                a.wait_ge(unit_done, u + 1)
                a.activation(v_sb[:, u - 4, :], bank[UNIT_B[u % 4]][:, :], ACT.Copy).then_inc(unit_out_act, 1)
            for u in (6, 7):
                a.wait_ge(unit_done, u + 1)
                a.activation(gsig[:, 2 * (u - 6):2 * (u - 6) + 2, :],
                             bank[UNIT_B[u % 4]][:, :].rearrange("p (k n) -> p k n", k=2), ACT.Sigmoid).then_inc(unit_out_act, 1)
            for u in range(10, 18):
                a.wait_ge(unit_done, u + 1)
                a.activation(gates[:, 2 * (u - 10):2 * (u - 10) + 2, :],
                             bank[UNIT_B[u % 4]][:, :].rearrange("p (k n) -> p k n", k=2), ACT.Sigmoid).then_inc(unit_out_act, 1)
            a.wait_ge(qkstat, 2)
            a.activation(rs16[:, :], rs16[:, :], ACT.Sqrt).then_inc(qkrstd, 1)
            a.wait_ge(zf_ready, 1)
            link(a.activation(za, zf, ACT.Abs))
            link(a.activation(za, za, ACT.Exp, scale=-1.0))
            a.activation(zl, za, ACT.Ln, bias=1.0).then_inc(lf_ready, 1)
            for j in range(8):
                dst = (gate1, shift2, G2, gate2[:, :])[j // 2][:, (j % 2) * W:(j % 2) * W + W]
                a.wait_ge(ada_done, 4 + j + 1)
                if j == 0:
                    a.wait_ge(h1T_ps, 4)
                a.activation(dst, bank[5 + j % 2][:, :], ACT.Identity if j // 2 == 2 else ACT.Copy,
                             bias=1.0 if j // 2 == 2 else 0.0).then_inc(ada2_out, 1)
            a.dma_start(n2g, norm2_g.broadcast_to([PART, D])).then_inc(n2_in, 16)
            for h in range(HEADS):
                a.wait_ge(max_done, 2 * h + 2)
                if h >= 2:
                    a.wait_ge(pT_done, h - 1)
                ps = bank[S_B[h % 2]]
                a.activation(prob[:, h % 2, 0:PART], ps[:, 0:PART], ACT.Exp, bias=st2[:, 6:7] if h % 2 == 0 else st2[:, 10:11],
                             accum_out=st2[:, 8:9] if h % 2 == 0 else st2[:, 12:13])
                a.activation(prob[:, h % 2, PART:3 * PART], ps[:, PART:3 * PART], ACT.Exp,
                             bias=st2[:, 7:8] if h % 2 == 0 else st2[:, 11:12],
                             accum_out=st2[:, 9:10] if h % 2 == 0 else st2[:, 13:14]).then_inc(exp_done, 1)
            a.wait_ge(dmu_ready, 2)
            a.activation(sqb, gsig, ACT.Square).then_inc(csq_ready, 1)
            a.wait_ge(crstd, 1)
            a.activation(rs16[0:8, :], rs16[0:8, :], ACT.Sqrt).then_inc(crstd, 1)
            for k in range(KC):
                a.wait_ge(yn_ready, k // 2 + 1)
                a.activation(cacc[:, k, :], sqb[:, k, :], ACT.Silu, scale=convc[:, k, TAPS + 1:TAPS + 2],
                             bias=convc[:, k, TAPS + 2:TAPS + 3]).then_inc(cT_ready, 1)
            for t in range(TH):
                a.wait_ge(x1_ready, 2 * t + 2)
                a.activation(h2[:, t, :], xs[:, t, :], ACT.Square, accum_out=st2[:, t:t + 1]).then_inc(ss_ready, 1)
            a.dma_start(rbias, router_bias.broadcast_to([PART, E])).then_inc(rb_in, 16)
            a.wait_ge(sqrt_in, 2)
            a.activation(st2[:, 4:6], st2[:, 2:4], ACT.Sqrt).then_inc(sqrt_out, 1)
            for i in range(4):
                a.wait_ge(h2T_ps, i + 1)
                a.activation(h2T[:, 2 * i:2 * i + 2, :], bank[i][:, :].rearrange("p (k n) -> p k n", k=2),
                             ACT.Copy).then_inc(h2T_ready, 1)
            a.wait_ge(z_ready, 1)
            a.activation(r["e"], r["z"], ACT.Exp, scale=-1.0).then_inc(ez_ready, 1)
            a.wait_ge(sgu_done, 1)
            a.activation(shg[:, :, :], bank[1][:, :].rearrange("p (k n) -> p k n", k=2), ACT.Silu).then_inc(shg_ready, 1)
            for i in range(0, 4 * KD, 2):
                a.wait_ge(gather_ps, i + 1)
                if i == 0:
                    a.wait_ge(tabs_ready, 1)
                a.activation(hs[:, i % KD, (i // KD) * W:(i // KD) * W + W], bank[0][:, :], ACT.Copy).then_inc(gather_out_act, 1)
            a.wait_ge(gather_out_dve, 2 * KD)
            a.wait_ge(gather_out_act, 2 * KD)
            a.wait_ge(pad_ready, 1)
            total = a.value_load(tab[0:1, E:E + 1], min_val=1, max_val=ITEMS - 1)
            p0 = a.value_load(tab[0:1, E + 1:E + 2], min_val=0, max_val=SLOTS)
            a.activation(hTi, hs[:, :, bass.ds(p0, PART)], ACT.Copy).then_inc(hT_ready, 1)
            with a.Fori(0, total) as i:
                a.wait_ge(up_done, i + 1)
                a.activation(sg[:, :], psU[:, 0:F], ACT.Silu).then_inc(silu_done, 1)
                p = a.value_load(tab[0:1, bass.ds(E + 2 + i, 1)], min_val=0, max_val=SLOTS)
                a.activation(hTi, hs[:, :, bass.ds(p, PART)], ACT.Copy).then_inc(hT_ready, 1)
                a.wait_ge(down_done, i + 2)
                a.wait_ge(st_ready, i + 2)
                a.activation(y[:, 0:W], psY[0][:, :], ACT.Copy, scale=wcol[:, 0:1]).then_inc(y_ready, 1)

        @block.vector
        def _(v):
            chain = [0]

            def link(ins):
                chain[0] += 1
                ins.then_inc(dve_chain, 1)
                v.wait_ge(dve_chain, chain[0])

            v.wait_ge(sc_ready, 1)
            v.tensor_copy(sc_rep, sc[:, :].unsqueeze(2).broadcast_to([PART, KD, PART])).then_inc(screp_ready, 1)
            v.tensor_copy(convc[:, :, :], bank[0][:, 64:64 + KC * (TAPS + 3)].rearrange("p (k n) -> p k n", k=KC))
            v.tensor_copy(qkg[:, 1:2], bank[0][:, 241:242])
            v.tensor_scalar(qkg[:, 0:1], bank[0][:, 240:241], HD ** -0.5, None, ALU.mult).then_inc(rows_out, 1)

            def rstd():
                v.tensor_scalar(st2[:, 2:4], st2[:, 0:2], 1.0 / D, EPS, ALU.mult, ALU.add).then_inc(sqrt_in, 1)

            def rstd2(n):
                v.wait_ge(sqrt_out, n)
                link(v.reciprocal(st2[:, 6:8], st2[:, 4:6]))
                link(v.tensor_tensor(st2[:, 8:10], st2[:, 6:8], st2[:, 6:8], ALU.mult))
                link(v.tensor_tensor(st2[:, 8:10], st2[:, 8:10], st2[:, 2:4], ALU.mult))
                link(v.tensor_scalar(st2[:, 8:10], st2[:, 8:10], -0.5, 1.5, ALU.mult, ALU.add))
                link(v.tensor_tensor(st2[:, 14:16], st2[:, 6:8], st2[:, 8:10], ALU.mult))

            v.wait_ge(ss_ready, TH)
            rstd()
            for j in range(4):
                v.wait_ge(ada_done, j + 1)
                dst = (shift1, G1)[j // 2][:, (j % 2) * W:(j % 2) * W + W]
                if j < 2:
                    v.tensor_copy(dst, bank[ADA_B[j]][:, :]).then_inc(ada1_out, 1)
                else:
                    v.wait_ge(n1_in, 16)
                    v.scalar_tensor_tensor(dst, bank[ADA_B[j]][:, :], 1.0, dst, ALU.add, ALU.mult).then_inc(ada1_out, 1)
            rstd2(1)
            v.wait_ge(ada1_out, 4)
            for t in range(TH):
                link(v.scalar_tensor_tensor(h1[:, t, :], xs[:, t, :], st2[:, 14 + t:15 + t], G1, ALU.mult, ALU.mult))
                v.tensor_tensor(h1[:, t, :], h1[:, t, :], shift1, ALU.add).then_inc(h1_ready, 1)
            for u in range(4):
                v.wait_ge(unit_done, u + 1)
                v.tensor_copy(qk[:, 2 * u:2 * u + 2, :], bank[UNIT_B[u % 4]][:, :].rearrange("p (k n) -> p k n", k=2)).then_inc(qk_raw, 1)
            v.wait_ge(f_done, 1)
            v.wait_ge(bf_in, 16)
            v.tensor_scalar(zf, bank[5][0:HEADS, 0:SEQ], bf[:, 0:1], None, ALU.add).then_inc(zf_ready, 1)
            for u in (8, 9):
                v.wait_ge(unit_done, u + 1)
                v.wait_ge(unit_out_act, u - 6 + 1)
                if u == 8:
                    v.wait_ge(upad_zero, 1)
                k = 2 * (u - 8)
                v.tensor_tensor(upad[:, k:k + 2, TAPS - 1:TAPS - 1 + SEQ],
                                bank[UNIT_B[u % 4]][:, :].rearrange("p (k n) -> p k n", k=2),
                                gsig[:, k:k + 2, :], ALU.mult).then_inc(unit_out_dve, 1)
            v.wait_ge(qkstat, 1)
            v.tensor_scalar(rs16[:, :], bank[6][0:16, 0:SEQ], EPS, None, ALU.add).then_inc(qkstat, 1)
            v.wait_ge(rows_out, 1)
            v.wait_ge(unit_out_dve, 2)
            for k in range(KC):
                v.tensor_scalar(cacc[:, k, :], upad[:, k, 0:SEQ], convc[:, k, 0:1], convc[:, k, TAPS:TAPS + 1],
                                ALU.mult, ALU.add).then_inc(conv_step, 1)
            with v.Fori(1, TAPS) as j:
                for k in range(KC):
                    v.wait_ge(conv_step, (j - 1) * KC + k + 1)
                    v.scalar_tensor_tensor(cacc[:, k, :], upad[:, k, bass.ds(j, SEQ)], convc[:, k, bass.ds(j, 1)],
                                           cacc[:, k, :], ALU.mult, ALU.add).then_inc(conv_step, 1)
            v.wait_ge(qkrstd, 1)
            v.reciprocal(rs16[:, :], rs16[:, :]).then_inc(qkrstd, 1)
            for i in range(4):
                v.wait_ge(qkb_done, i + 1)
                v.scalar_tensor_tensor(qk[:, 2 * i:2 * i + 2, :], qk[:, 2 * i:2 * i + 2, :],
                                       qkg[:, i // 2:i // 2 + 1],
                                       bank[UNIT_B[i % 4]][:, :].rearrange("p (k n) -> p k n", k=2),
                                       ALU.mult, ALU.mult).then_inc(qk_ready, 1)
            v.wait_ge(lf_ready, 1)
            link(v.tensor_scalar(za, zf, 0.0, None, ALU.min))
            link(v.tensor_tensor(zl, za, zl, ALU.subtract))
            link(v.memset(za, 1.0))
            link(v.tensor_tensor_scan(cum, za, zl, 0.0, ALU.mult, ALU.add))
            v.wait_ge(aug_zero, 4)
            for par in range(2):
                v.tensor_copy(AU[64 * par:64 * par + HEADS, :, :], cum.unsqueeze(1).broadcast_to([HEADS, KC, SEQ]))
                ins = v.tensor_scalar(BU[64 * par + 32:64 * par + 32 + HEADS, :, :],
                                      cum.unsqueeze(1).broadcast_to([HEADS, KC, SEQ]), -1.0, None, ALU.mult)
            ins.then_inc(aug_ready, 1)

            def head_max(h):
                ps = bank[S_B[h % 2]]
                v.wait_ge(s_done, h + 1)
                o = 6 if h % 2 == 0 else 10
                v.tensor_reduce(st2[:, o:o + 1], ps[:, 0:PART], AX, ALU.max, negate=True).then_inc(max_done, 1)
                v.tensor_reduce(st2[:, o + 1:o + 2], ps[:, PART:3 * PART], AX, ALU.max, negate=True).then_inc(max_done, 1)

            def head_norm(h):
                o = 8 if h % 2 == 0 else 12
                v.wait_ge(exp_done, h + 1)
                link(v.reciprocal(st2[:, o:o + 2], st2[:, o:o + 2]))
                v.tensor_scalar(prob[:, h % 2, 0:PART], prob[:, h % 2, 0:PART], st2[:, o:o + 1], None, ALU.mult)
                v.tensor_scalar(prob[:, h % 2, PART:3 * PART], prob[:, h % 2, PART:3 * PART], st2[:, o + 1:o + 2],
                                None, ALU.mult).then_inc(p_ready, 1)

            def head_pT(h):
                v.wait_ge(pT_done, h + 1)
                if h >= 2:
                    v.wait_ge(o_done, h - 1)
                v.tensor_copy(probT[:, h % 2, :], bank[PT_B[h % 2]][:, 0:3 * PART]).then_inc(pT_out, 1)

            def head_out(h):
                if h % 2 == 1:
                    v.wait_ge(o_done, h + 1)
                    v.tensor_copy(oT[:, h // 2, :], bank[O_B[(h // 2) % 2]][:, 0:SEQ]).then_inc(o_out, 1)

            v.wait_ge(qksq_ready, 4)
            for step in range(HEADS + 1):
                if step < HEADS:
                    head_max(step)
                if step >= 1:
                    head_norm(step - 1)
                    head_pT(step - 1)
                    if step >= 2:
                        head_out(step - 2)
            head_out(HEADS - 1)
            for i in range(2):
                v.wait_ge(mean_done, i + 1)
                v.tensor_tensor(gsig[:, 2 * i:2 * i + 2, :], cacc[:, 2 * i:2 * i + 2, :],
                                bank[6 + i][:, :].rearrange("p (k n) -> p k n", k=2), ALU.subtract).then_inc(dmu_ready, 1)
            v.wait_ge(var_done, 1)
            v.tensor_scalar(rs16[0:8, :], bank[0][0:8, 0:SEQ], EPS, None, ALU.add).then_inc(crstd, 1)
            v.wait_ge(crstd, 2)
            v.reciprocal(rs16[0:8, :], rs16[0:8, :]).then_inc(crstd, 1)
            for i in range(2):
                v.wait_ge(cb_done, i + 1)
                v.tensor_tensor(sqb[:, 2 * i:2 * i + 2, :], gsig[:, 2 * i:2 * i + 2, :],
                                bank[1 + i][:, :].rearrange("p (k n) -> p k n", k=2), ALU.mult).then_inc(yn_ready, 1)
            for i in range(4):
                v.wait_ge(ya_done, i + 1)
                v.tensor_tensor(gates[:, KD + 2 * i:KD + 2 * i + 2, :], gates[:, KD + 2 * i:KD + 2 * i + 2, :],
                                bank[3 + i][:, :].rearrange("p (k n) -> p k n", k=2), ALU.mult).then_inc(ya_out, 1)
            for i in range(4):
                v.wait_ge(yc_done, i + 1)
                g = gates[:, 2 * i:2 * i + 2, :]
                v.tensor_tensor(g, g, bank[3 + i][:, :].rearrange("p (k n) -> p k n", k=2), ALU.mult).then_inc(yc_out, 1)
                v.wait_ge(yc_out, i + 1)
                v.tensor_tensor(g, g, gates[:, KD + 2 * i:KD + 2 * i + 2, :], ALU.add).then_inc(merged, 1)
            v.wait_ge(ada2_out, 8)
            for t in range(TH):
                for n in range(2):
                    i = 2 * t + n
                    v.wait_ge(mo_done, i + 1)
                    link(v.tensor_tensor(cacc[:, 0:2, :].rearrange("p k n -> p (k n)"), bank[i][:, :],
                                         gate1[:, n * W:(n + 1) * W], ALU.mult))
                    v.tensor_tensor(xs[:, t, n * W:(n + 1) * W], xs[:, t, n * W:(n + 1) * W],
                                    cacc[:, 0:2, :].rearrange("p k n -> p (k n)"), ALU.add).then_inc(x1_ready, 1)
                    v.wait_ge(x1_ready, i + 1)
            v.wait_ge(n2_in, 16)
            link(v.tensor_tensor(G2, G2, n2g, ALU.mult))
            v.wait_ge(ss_ready, 2 * TH)
            rstd()
            rstd2(2)
            for t in range(TH):
                link(v.scalar_tensor_tensor(h2[:, t, :], xs[:, t, :], st2[:, 14 + t:15 + t], G2, ALU.mult, ALU.mult))
                v.tensor_tensor(h2[:, t, :], h2[:, t, :], shift2, ALU.add).then_inc(h2_ready, 1)
            v.wait_ge(logit_done, 1)
            v.tensor_scalar(r["z"], bank[0][:, 0:TH * E].rearrange("p (t e) -> p t e", t=TH), LOWEST, None,
                            ALU.max).then_inc(z_ready, 1)
            v.wait_ge(ez_ready, 1)
            link(v.tensor_scalar(r["e"], r["e"], 1.0, None, ALU.add))
            link(v.reciprocal(r["s"], r["e"]))
            v.wait_ge(rb_in, 16)
            link(v.tensor_tensor(r["b"], r["s"], rbias.unsqueeze(1).broadcast_to([PART, TH, E]), ALU.add))
            for t in range(TH):
                for g in range(GROUPS):
                    ins = v.max(top2[:, t, g, :], r["b"][:, t, g * EPG:(g + 1) * EPG])
            link(ins)
            link(v.tensor_tensor(gs, top2[:, :, :, 0], top2[:, :, :, 1], ALU.add))
            mine = gs.unsqueeze(3).broadcast_to([PART, TH, GROUPS, GROUPS])
            theirs = gs.unsqueeze(2).broadcast_to([PART, TH, GROUPS, GROUPS])
            v.wait_ge(sel_ready, 1)
            for t in range(TH):
                v.tensor_tensor(cmp1[:, t], theirs[:, t], mine[:, t], ALU.is_gt)
                ins = v.tensor_tensor(cmp2[:, t], theirs[:, t], mine[:, t], ALU.is_equal)
            link(ins)
            link(v.tensor_tensor(cmp2, cmp2, lower8[:, :, :].unsqueeze(1).broadcast_to([PART, TH, GROUPS, GROUPS]), ALU.mult))
            link(v.tensor_tensor(cmp1, cmp1, cmp2, ALU.add))
            link(v.tensor_reduce(grank, cmp1, AX, ALU.add))
            link(v.tensor_scalar(gmask, grank, float(TOPG), None, ALU.is_lt))
            em = gmask.unsqueeze(3).broadcast_to([PART, TH, GROUPS, EPG])
            grp = {n: r[n].rearrange("p t (g e) -> p t g e", g=GROUPS) for n in ("b", "m", "pre")}
            for t in range(TH):
                v.tensor_tensor(grp["m"][:, t], grp["b"][:, t], em[:, t], ALU.mult)
                ins = v.tensor_scalar(grp["pre"][:, t], em[:, t], -NEG, NEG, ALU.mult, ALU.add)
            link(ins)
            link(v.tensor_tensor(r["m"], r["m"], r["pre"], ALU.add))
            for t in range(TH):
                ins = v.max(top8[:, t, :], r["m"][:, t, :])
            link(ins)
            for t in range(TH):
                ins = v.match_replace(r["rep"][:, t, :], top8[:, t, :], r["m"][:, t, :], 2.0 * NEG)
            link(ins)
            v.tensor_tensor(r["sel"], r["rep"], r["m"], ALU.not_equal).then_inc(sel_out, 1)
            v.wait_ge(sel_out, 1)
            link(v.tensor_tensor(wt[:, :, :], r["s"], r["sel"], ALU.mult))
            link(v.tensor_reduce(st2[:, 0:2], wt[:, :, :], AX, ALU.add))
            link(v.reciprocal(st2[:, 0:2], st2[:, 0:2]))
            for t in range(TH):
                ins = v.tensor_scalar(wt[:, t, :], wt[:, t, :], st2[:, t:t + 1], ROUTED_SCALE, ALU.mult, ALU.mult)
            link(ins)
            v.wait_ge(rank_done, 1)
            link(v.tensor_copy(cnt, bank[0][:, 128:128 + E]))
            link(v.tensor_tensor_scan(incl, ones[:, 0:E], cnt, 0.0, ALU.mult, ALU.add))
            link(v.tensor_tensor(first, incl, cnt, ALU.subtract))
            link(v.tensor_tensor(slotm[:, :, :], bank[0][:, 256:256 + TH * E].rearrange("p (t e) -> p t e", t=TH),
                                 first.unsqueeze(1).broadcast_to([PART, TH, E]), ALU.add))
            link(v.scalar_tensor_tensor(slotm[:, :, :], slotm[:, :, :], 1.0, r["sel"], ALU.add, ALU.mult))
            v.tensor_scalar(slotm[:, :, :], slotm[:, :, :], -1.0, None, ALU.add).then_inc(slotT_out, 1)
            link(v.tensor_copy(ecol[:, 0:1], bank[0][0:E, 448:449]))
            link(v.tensor_scalar(ecol2[:, 0:1], ecol[:, 0:1], 0.0, None, ALU.is_gt))
            link(v.tensor_scalar(ecol2[:, 1:2], ecol[:, 0:1], float(PART), None, ALU.is_gt))
            v.tensor_tensor(ecol[:, 1:2], ecol2[:, 0:1], ecol2[:, 1:2], ALU.add).then_inc(ecol_out, 1)
            v.wait_ge(ecum_done, 1)
            v.wait_ge(slotT_ps, 1)
            link(v.tensor_copy(ecum, bank[3][0:E, 256:258]))
            link(v.tensor_copy(slotT, bank[3][0:E, 0:SEQ]))
            link(v.tensor_tensor(ecol2[:, 2:4], ecum, ecol, ALU.add))
            v.wait_ge(iota_ready, 1)
            v.wait_ge(h2_ready, TH)
            link(v.tensor_scalar(Emat, iota[0:E, 0:SLOTS], ecol2[:, 2:3], None, ALU.is_ge))
            v.scalar_tensor_tensor(Emat, iota[0:E, 0:SLOTS], ecum[:, 0:1], Emat, ALU.is_ge, ALU.subtract).then_inc(E_ready, 1)
            j = iota[0:E, 0:ITEMS]
            link(v.tensor_scalar(jt[:, 0, :], j, ecum[:, 1:2], None, ALU.is_ge))
            link(v.scalar_tensor_tensor(jt[:, 1, :], j, ecol2[:, 3:4], jt[:, 0, :], ALU.is_lt, ALU.mult))
            link(v.tensor_scalar(jt[:, 0, :], j, ecum[:, 1:2], float(PART), ALU.subtract, ALU.mult))
            v.scalar_tensor_tensor(jt[:, 2, :], jt[:, 0, :], ecum[:, 0:1], jt[:, 1, :], ALU.add, ALU.mult).then_inc(tabs_ps_in, 1)
            link(v.tensor_scalar(nit[:, :], cnt, 0.0, None, ALU.is_gt))
            link(v.scalar_tensor_tensor(nit[:, :], cnt, float(PART), nit[:, :], ALU.is_gt, ALU.add))
            link(v.memset(cumi[:, 0:1], 0.0))
            link(v.tensor_tensor_scan(cumi[:, 1:E + 1], ones[:, 0:E], nit[:, :], 0.0, ALU.mult, ALU.add))
            link(v.tensor_copy(tab[0:1, 0:E + 1], cumi[0:1, 0:E + 1]))
            link(v.tensor_scalar(freeat[0:1, :], cumi[0:1, 1:E + 1], 1.0, None, ALU.add))
            v.wait_ge(tabs_ps, 1)
            v.tensor_copy(tab[0:1, E + 1:E + 1 + 2 * ITEMS], bank[3][0:1, 0:2 * ITEMS]).then_inc(tabs_ready, 1)
            v.wait_ge(shg_ready, 1)
            v.wait_ge(sgu_done, 2)
            v.tensor_tensor(shT, shg, bank[2][:, :].rearrange("p (k n) -> p k n", k=2), ALU.mult).then_inc(shT_ready, 1)

            def select(q):
                for t in range(TH):
                    v.wait_ge(m1_done, 2 * q + t + 1)
                    if q >= 2:
                        v.wait_ge(gather_ps, KD * (q - 1))
                    v.tensor_tensor(SS[:, q % 2, t, :], bank[2 + t][:, :], iota[:, q * W:(q + 1) * W],
                                    ALU.is_equal).then_inc(SS_ready, 1)

            select(0)
            for q in range(4):
                if q < 3:
                    select(q + 1)
                for i in range(KD * q + 1, KD * (q + 1), 2):
                    v.wait_ge(gather_ps, i + 1)
                    v.tensor_copy(hs[:, i % KD, q * W:(q + 1) * W], bank[1][:, :]).then_inc(gather_out_dve, 1)
            v.wait_ge(gather_ps, 4 * KD)
            v.memset(ST[:, :], 0.0).then_inc(st_ready, 1)
            v.memset(y[:, :], 0.0).then_inc(y_ready, 2)
            total = v.value_load(tab[0:1, E:E + 1], min_val=1, max_val=ITEMS - 1)

            def build_si(n):
                p = v.value_load(tab[0:1, bass.ds(n + (E + 1), 1)], min_val=0, max_val=SLOTS)
                e = v.value_load(tab[0:1, bass.ds(n + (E + 1 + ITEMS), 1)], min_val=0, max_val=E - 1)
                for t in range(TH):
                    ins = v.tensor_scalar(SI[:, t, :], iota[:, bass.ds(p, PART)], slotm[:, t, bass.ds(e, 1)],
                                          wt[:, t, bass.ds(e, 1)], ALU.is_equal, ALU.mult)
                ins.then_inc(si_ready, 1)

            build_si(0)
            with v.Fori(0, total) as i:
                v.wait_ge(silu_done, i + 1)
                v.tensor_tensor(act[:, :], sg[:, :], psU[:, F:2 * F], ALU.mult).then_inc(act_ready, 1)
                v.wait_ge(t_done, i + 1)
                v.tensor_copy(actT[:, :, :], psM[:, 0:F].rearrange("p (k n) -> p k n", k=KF)).then_inc(actT_ready, 1)
                v.wait_ge(sit_done, i + 1)
                v.tensor_scalar(ST[:, :], psU[:, 0:SEQ], 0.0, None, ALU.is_gt)
                v.reduce_sum(wcol[:, 0:1], psU[:, 0:SEQ], AX).then_inc(st_ready, 1)
                build_si(i + 1)
                v.wait_ge(down_done, i + 2)
                v.wait_ge(st_ready, i + 2)
                v.tensor_scalar(y[:, W:2 * W], psY[1][:, :], wcol[:, 0:1], None, ALU.mult).then_inc(y_ready, 1)
            v.wait_ge(all_done, 1)
            for t in range(TH):
                for n in range(2):
                    link(v.tensor_tensor(misc[:, 0:W], acc[2 * t + n][:, :], gate2[:, n * W:(n + 1) * W], ALU.mult))
                    xo = xs[:, t, n * W:(n + 1) * W]
                    v.tensor_tensor(xo, xo, misc[:, 0:W], ALU.add).then_inc(fin, 1)
                    v.wait_ge(fin, 2 * t + n + 1)

        @block.tensor
        def _(pe):
            mm, tr = nc.tensor.matmul, nc.tensor.transpose

            def arrived(n):
                pe.wait_ge(piece_in[n % NBUF], 16 * (n // NBUF + 1))
                return piece(n)

            pe.wait_ge(cst, 2)
            pe.wait_ge(row_in, 16 * 9)
            tr(bank[0][:, 0:KD], crow, ident[0:KD, 0:KD])
            n = TAPS + 3
            for k in range(KC):
                tr(bank[0][:, 64 + n * k:64 + n * (k + 1)], convrow[:, k * PART:(k + 1) * PART], ident[0:n, 0:n])
            tr(bank[0][:, 240:242], qkrow, ident[0:2, 0:2]).then_inc(rowsT, 1)

            def ada(j, n, b):
                w = arrived(n)
                for k in range(KD):
                    mm(b[:, :], sc_rep[:, k, :], w[:, k, :], start=(k == 0), stop=False)
                q = j // 3
                mm(b[:, :], ones[32 * q:32 * q + 1, :], bada[32 * q:32 * q + 1, j % 3, :], start=False,
                   stop=True).then_inc(ada_done, 1)

            pe.wait_ge(screp_ready, 1)
            pe.wait_ge(bada_in, 64)
            for j in range(4):
                ada(j, ADA1 + j, bank[ADA_B[j]])
            for i in range(4):
                for kk in range(2):
                    for t in range(TH):
                        if i == 0 and kk == 0:
                            pe.wait_ge(h1_ready, TH)
                            pe.wait_ge(rows_out, 1)
                        k = 2 * i + kk
                        ins = tr(bank[H1T_B[i]][:, kk * SEQ + t * PART:kk * SEQ + (t + 1) * PART],
                                 h1[:, t, k * PART:(k + 1) * PART], ident[:, :])
                ins.then_inc(h1T_ps, 1)
            pe.wait_ge(h1T_ready, 4)
            pe.wait_ge(ada1_out, 4)
            starts = {0: QP, 2: KP, 4: VP, 6: GP, 8: AP_, 10: GATEP, 12: GATEP + 1, 14: GATEP + 2, 16: GATEP + 3}
            for u, kind in enumerate(UNITS):
                b = bank[UNIT_B[u % 4]]
                if u >= 4:
                    p = u - 4
                    if p < 4:
                        pe.wait_ge(qk_raw, p + 1)
                    elif p in (8, 9):
                        pe.wait_ge(unit_out_dve, p - 7)
                    else:
                        pe.wait_ge(unit_out_act, p - 3 if p < 8 else p - 5)
                if u in starts:
                    w = arrived(starts[u])
                if kind == "v":
                    for k in range(KD):
                        ins = mm(b[:, :], h1T[:, k, (u % 2) * PART:(u % 2 + 1) * PART], w[:, k, :],
                                 start=(k == 0), stop=(k == KD - 1))
                else:
                    for kk in range(2):
                        m = 2 * (u % 2) + kk
                        for k in range(KD):
                            ins = mm(b[:, kk * SEQ:(kk + 1) * SEQ], w[:, k, m * PART:(m + 1) * PART],
                                     h1T[:, k, :], start=(k == 0), stop=(k == KD - 1))
                ins.then_inc(unit_done, 1)
                if u == 5:
                    pe.wait_ge(wf_in, 16)
                    for k in range(KD):
                        ins = mm(bank[5][0:HEADS, 0:SEQ], wf[:, k, :], h1T[:, k, :], start=(k == 0), stop=(k == KD - 1))
                    ins.then_inc(f_done, 1)
                if u == 9:
                    pe.wait_ge(qksq_ready, 4)
                    pe.wait_ge(sel_ready, 1)
                    for k in range(2 * KC):
                        ins = mm(bank[6][0:16, 0:SEQ], headsum[:, k, :], qksq[:, k, :], start=(k == 0), stop=(k == 2 * KC - 1))
                    ins.then_inc(qkstat, 1)
            pe.wait_ge(zf_ready, 1)
            pe.wait_ge(qkstat, 2)
            for j in range(8):
                if j >= 2:
                    pe.wait_ge(ada2_out, j - 1)
                ada(4 + j, ADA2 + j, bank[5 + j % 2])
            pe.wait_ge(qkrstd, 2)
            for i in range(4):
                p = 14 + i
                pe.wait_ge(unit_out_act, 12 if i == 0 else 12)
                for kk in range(2):
                    ins = mm(bank[UNIT_B[i % 4]][:, kk * SEQ:(kk + 1) * SEQ], headrow[:, 2 * i + kk, :], rs16[:, :],
                             start=True, stop=True)
                ins.then_inc(qkb_done, 1)

            def scores(h):
                b, base, j = bank[S_B[h % 2]], 64 * (h % 2), h // 2
                if h >= 2:
                    pe.wait_ge(exp_done, h - 1)
                for q, o, keys in ((0, 0, PART), (1, PART, SEQ)):
                    qs = slice(q * PART, (q + 1) * PART)
                    mm(b[:, o:o + keys], qk[base:base + HD, j, qs], qk[base:base + HD, KC + j, 0:keys], start=True, stop=False)
                    mm(b[:, o:o + keys], AU[base:base + 40, j, qs], BU[base:base + 40, j, 0:keys], start=False, stop=False)
                    ins = mm(b[:, o:o + keys], ident[:, :], causal[:, 2 * PART - keys:], start=False, stop=True)
                ins.then_inc(s_done, 1)

            def transposes(h):
                pe.wait_ge(p_ready, h + 1)
                if h >= 2:
                    pe.wait_ge(pT_out, h - 1)
                for i in range(3):
                    o = (0, 1, 2)[i] * PART
                    ins = tr(bank[PT_B[h % 2]][:, o:o + PART], prob[:, h % 2, o:o + PART], ident[:, :])
                ins.then_inc(pT_done, 1)

            def values(h):
                base, j = 64 * (h % 2), h // 2
                pe.wait_ge(pT_out, h + 1)
                if h % 2 == 0 and h >= 4:
                    pe.wait_ge(o_out, j - 1)
                b = bank[O_B[j % 2]]
                mm(b[base:base + HD, 0:PART], v_sb[:, 0, h * HD:(h + 1) * HD], probT[:, h % 2, 0:PART], start=True, stop=True)
                mm(b[base:base + HD, PART:SEQ], v_sb[:, 0, h * HD:(h + 1) * HD], probT[:, h % 2, PART:SEQ], start=True, stop=False)
                mm(b[base:base + HD, PART:SEQ], v_sb[:, 1, h * HD:(h + 1) * HD], probT[:, h % 2, SEQ:3 * PART],
                   start=False, stop=True).then_inc(o_done, 1)

            pe.wait_ge(qk_ready, 4)
            pe.wait_ge(ada2_out, 8)
            pe.wait_ge(aug_ready, 1)
            pe.wait_ge(unit_out_act, 4)
            scores(0)
            for h in range(HEADS):
                if h + 1 < HEADS:
                    scores(h + 1)
                transposes(h)
                values(h)
            pe.wait_ge(conv_step, TAPS * KC)
            for i in range(2):
                for kk in range(2):
                    ins = mm(bank[6 + i][:, kk * SEQ:(kk + 1) * SEQ], blk[:, :], cacc[:, 2 * i + kk, :], start=True, stop=True)
                ins.then_inc(mean_done, 1)
            pe.wait_ge(csq_ready, 1)
            pe.wait_ge(exp_done, HEADS)
            for k in range(KC):
                ins = mm(bank[0][0:8, 0:SEQ], headsum[:, k, 0:8], sqb[:, k, :], start=(k == 0), stop=(k == KC - 1))
            ins.then_inc(var_done, 1)
            w = arrived(COUT)
            wa = arrived(AOUT)
            pe.wait_ge(o_out, 4)
            pe.wait_ge(dmu_ready, 2)

            def project(w, src, done, out_sem):
                for i in range(4):
                    if out_sem is not None:
                        pe.wait_ge(out_sem, i + 1)
                    for kk in range(2):
                        m = 2 * i + kk
                        for k in range(KC):
                            ins = mm(bank[3 + i][:, kk * SEQ:(kk + 1) * SEQ], w[:, k, m * PART:(m + 1) * PART],
                                     src[:, k, :], start=(k == 0), stop=(k == KC - 1))
                    ins.then_inc(done, 1)

            project(wa, oT, ya_done, None)
            pe.wait_ge(crstd, 3)
            for i in range(2):
                for kk in range(2):
                    ins = mm(bank[1 + i][:, kk * SEQ:(kk + 1) * SEQ], headrow[0:8, 2 * i + kk, :], rs16[0:8, :], start=True, stop=True)
                ins.then_inc(cb_done, 1)
            pe.wait_ge(cT_ready, KC)
            project(w, cacc, yc_done, ya_out)
            pe.wait_ge(merged, 4)
            for t in range(TH):
                for n in range(2):
                    w = arrived(WOUT + n)
                    for k in range(KD):
                        ins = mm(bank[2 * t + n][:, :], gates[:, k, t * PART:(t + 1) * PART], w[:, k, :],
                                 start=(k == 0), stop=(k == KD - 1))
                    ins.then_inc(mo_done, 1)
            pe.wait_ge(h2_ready, TH)
            for i in range(4):
                for kk in range(2):
                    for t in range(TH):
                        k = 2 * i + kk
                        ins = tr(bank[i][:, kk * SEQ + t * PART:kk * SEQ + (t + 1) * PART],
                                 h2[:, t, k * PART:(k + 1) * PART], ident[:, :])
                ins.then_inc(h2T_ps, 1)
            pe.wait_ge(h2T_ready, 4)
            pe.wait_ge(rw_in, 16)
            for t in range(TH):
                for k in range(KD):
                    ins = mm(bank[0][:, t * E:(t + 1) * E], h2T[:, k, t * PART:(t + 1) * PART], router[:, k, :],
                             start=(k == 0), stop=(k == KD - 1))
            ins.then_inc(logit_done, 1)
            w = arrived(SHGU)
            for m in range(2 * KF):
                for k in range(KD):
                    ins = mm(bank[1 + m // 2][:, (m % 2) * SEQ:(m % 2 + 1) * SEQ], w[:, k, m * PART:(m + 1) * PART],
                             h2T[:, k, :], start=(k == 0), stop=(k == KD - 1))
                if m % 2 == 1:
                    ins.then_inc(sgu_done, 1)
            pe.wait_ge(sel_out, 1)
            sel = r["sel"]
            for t in range(TH):
                mm(bank[0][:, 128:128 + E], ones[:, :], sel[:, t, :], start=(t == 0), stop=(t == TH - 1))
            for t in range(TH):
                for s in range(t):
                    mm(bank[0][:, 256 + t * E:256 + (t + 1) * E], ones[:, :], sel[:, s, :], start=(s == 0), stop=False)
                mm(bank[0][:, 256 + t * E:256 + (t + 1) * E], before[:, :], sel[:, t, :], start=(t == 0), stop=True)
            for t in range(TH):
                ins = mm(bank[0][0:E, 448:449], sel[:, t, :], ones[:, 0:1], start=(t == 0), stop=(t == TH - 1))
            ins.then_inc(rank_done, 1)
            pe.wait_ge(slotT_out, 1)
            for t in range(TH):
                ins = tr(bank[3][0:E, t * PART:(t + 1) * PART], slotm[:, t, :], ident[:, :])
            ins.then_inc(slotT_ps, 1)
            pe.wait_ge(ecol_out, 1)
            mm(bank[3][0:E, 256:258], before[0:E, 0:E], ecol, start=True, stop=True).then_inc(ecum_done, 1)
            pe.wait_ge(tabs_ps_in, 1)
            mm(bank[3][0:1, 0:ITEMS], ones[0:E, 0:1], jt[:, 2, :], start=True, stop=True)
            mm(bank[3][0:1, ITEMS:2 * ITEMS], enum[:, :], jt[:, 1, :], start=True, stop=True).then_inc(tabs_ps, 1)
            w = arrived(SHD)
            pe.wait_ge(shT_ready, 1)
            for t in range(TH):
                for n in range(2):
                    for k in range(KF):
                        ins = mm(acc[2 * t + n][:, :], shT[:, k, t * PART:(t + 1) * PART], w[:, k, n * W:(n + 1) * W],
                                 start=(k == 0), stop=False)
            ins.then_inc(down_done, 1)

            pe.wait_ge(E_ready, 1)
            pe.wait_ge(tabs_ready, 1)

            def select(q):
                for t in range(TH):
                    if q >= 1:
                        pe.wait_ge(SS_ready, 2 * (q - 1) + t + 1)
                    mm(bank[2 + t][:, :], slotT[:, t * PART:(t + 1) * PART], Emat[:, q * W:(q + 1) * W],
                       start=True, stop=True).then_inc(m1_done, 1)

            select(0)
            for q in range(4):
                if q < 3:
                    select(q + 1)
                pe.wait_ge(SS_ready, 2 * q + 2)
                for k in range(KD):
                    i = q * KD + k
                    if i >= 2:
                        pe.wait_ge((gather_out_act, gather_out_dve)[i % 2], i // 2)
                    for t in range(TH):
                        ins = mm(bank[i % 2][:, :], h2[:, t, k * PART:(k + 1) * PART], SS[:, q % 2, t, :],
                                 start=(t == 0), stop=(t == TH - 1))
                    ins.then_inc(gather_ps, 1)
            pe.wait_ge(gather_out_act, 2 * KD)
            pe.wait_ge(gather_out_dve, 2 * KD)

            def scatter():
                for t in range(TH):
                    for n in range(2):
                        mm(acc[2 * t + n][:, :], ST[:, t * PART:(t + 1) * PART], y[:, n * W:(n + 1) * W],
                           start=False, stop=False)

            with pe.Fori(0, E // NSLOT) as g:
                for b in range(NSLOT):
                    gu, dn = expert_gu(b), expert_dn(b)
                    e = g * NSLOT + b
                    lo = pe.value_load(tab[0:1, bass.ds(e, 1)], min_val=0, max_val=ITEMS - 1)
                    hi = pe.value_load(tab[0:1, bass.ds(e + 1, 1)], min_val=0, max_val=ITEMS - 1)
                    with pe.If(hi > lo):
                        with pe.Fori(lo, hi) as i:
                            pe.wait_ge(expert_in[b], g * 32 + 32)
                            pe.wait_ge(hT_ready, i + 1)
                            pe.wait_ge(st_ready, i + 1)
                            for k in range(KD):
                                ins = mm(psU[:, :], hTi[:, k, :], gu[:, k, :], start=(k == 0), stop=(k == KD - 1))
                            ins.then_inc(up_done, 1)
                            pe.wait_ge(y_ready, i * 2 + 2)
                            scatter()
                            pe.wait_ge(act_ready, i + 1)
                            for k in range(KF):
                                ins = tr(psM[:, k * PART:(k + 1) * PART], act[:, k * PART:(k + 1) * PART], ident[:, :])
                            ins.then_inc(t_done, 1)
                            pe.wait_ge(si_ready, i + 1)
                            for t in range(TH):
                                ins = tr(psU[:, t * PART:(t + 1) * PART], SI[:, t, :], ident[:, :])
                            ins.then_inc(sit_done, 1)
                            pe.wait_ge(actT_ready, i + 1)
                            for n in range(2):
                                for k in range(KF):
                                    ins = mm(psY[n][:, :], actT[:, k, :], dn[:, k, n * W:(n + 1) * W],
                                             start=(k == 0), stop=(k == KF - 1))
                            ins.then_inc(down_done, 1)
                    pe.nop()
            total = pe.value_load(tab[0:1, E:E + 1], min_val=1, max_val=ITEMS - 1)
            pe.wait_ge(st_ready, total + 1)
            pe.wait_ge(y_ready, total * 2 + 2)
            for t in range(TH):
                for n in range(2):
                    ins = mm(acc[2 * t + n][:, :], ST[:, t * PART:(t + 1) * PART], y[:, n * W:(n + 1) * W],
                             start=False, stop=True)
            ins.then_inc(all_done, 1)


_INS = ["x", "c", "w_ada", "b_ada", "norm1_g", "w_in", "w_dw", "b_dw", "conv_gn_g", "conv_gn_b", "w_conv_out",
        "q_norm_g", "k_norm_g", "b_forget", "w_attn_out", "w_out", "norm2_g", "w_router", "router_bias",
        "w_experts_gate_up", "w_experts_down", "w_shared_gate_up", "w_shared_down"]


def kernel(**inputs):
    import numpy as _np
    import concourse.bacc as _bacc
    from concourse import mybir as _mybir
    from concourse.bass_utils import run_bass_kernel_spmd as _run

    nc = _bacc.Bacc("TRN2", target_bir_lowering=False, num_devices=1)
    arrays, args = {}, []
    for name in _INS:
        a = _np.ascontiguousarray(inputs[name])
        arrays[f"in_{name}_dram"] = a
        args.append(nc.dram_tensor(f"in_{name}_dram", a.shape, _mybir.dt.from_np(a.dtype), kind="ExternalInput").ap())
    out = nc.dram_tensor("out_dram", inputs["x"].shape, _mybir.dt.float32, kind="ExternalOutput").ap()
    hybrid_conformer_fox_moe_block(nc, *args, out)
    return _run(nc, [arrays], core_ids=[0]).results[0]["out_dram"]
```

```python
import concourse.bass as bass
from concourse import mybir
from contextlib import ExitStack


def hybrid_conformer_fox_moe_block(
    nc, x, c, w_ada, b_ada, norm1_g, w_in, w_dw, b_dw, conv_gn_g, conv_gn_b, w_conv_out, q_norm_g,
    k_norm_g, b_forget, w_attn_out, w_out, norm2_g, w_router, router_bias, w_experts_gate_up,
    w_experts_down, w_shared_gate_up, w_shared_down, out,
):
    fp32, fp32r, i32 = mybir.dt.float32, mybir.dt.float32r, mybir.dt.int32
    ALU = mybir.AluOpType
    ACT = mybir.ActivationFunctionType
    AX = mybir.AxisListType.X

    PART = 128
    SEQ, D = x.shape[1], x.shape[2]
    TH = SEQ // PART
    KD = D // PART
    TAPS, CONV = w_dw.shape[1], w_dw.shape[2]
    KC = CONV // PART
    HEADS, HD = b_forget.shape[1], q_norm_g.shape[1]
    E, F = w_experts_gate_up.shape[1], w_experts_down.shape[2]
    KF = F // PART
    ATT = HEADS * HD
    OFF_Q = 2 * CONV
    OFF_F = OFF_Q + 3 * ATT
    OFF_G = OFF_F + HEADS
    GROUPS, EPG, TOPG, TOPK = 8, 8, 4, 8
    ROUTED_SCALE = 2.5
    EPS = 1e-6
    W = 512
    SLOTS = SEQ * TOPK
    PADDED = SLOTS + PART
    ITEMS = E + SLOTS // PART
    GU, DN = KD * 2 * F, KF * D
    SLOTW = GU + DN
    QW = GU // 4
    NBUF = 5
    BUFW = KD * W
    NEG = -1.0e30
    LOWEST = -87.0

    ctx = ExitStack()
    with ctx:
        def sb(name, shape, dt=fp32):
            return ctx.enter_context(nc.sbuf_tensor(name, shape, dt))

        def sem(name):
            return ctx.enter_context(nc.semaphore(name))

        with nc.sbuf_tensor("ring", [PART, 4 * SLOTW], fp32) as ring:
            pass
        raw = sb("raw", [PART, 2 * SLOTW])
        split = sb("split", [PART, 2 * SLOTW], fp32r)
        with ExitStack() as early:
            def sbe(name, shape):
                return early.enter_context(nc.sbuf_tensor(name, shape, fp32))

            misc = sbe("misc", [PART, 2 * D])
            blk = sbe("blk", [PART, PART])
            causal = sbe("causal", [PART, 2 * PART])
            headsum = sbe("headsum", [PART, 8, 16])
            headrow = sbe("headrow", [16, 8, PART])
            wf = sbe("wf", [PART, KD, HEADS])
            convc = sbe("convc", [PART, KC, TAPS + 3])
            qkg = sbe("qkg", [PART, 2])
            bf = sbe("bf", [HEADS, 1])
            sc = sbe("sc", [PART, KD])
            before = sbe("before", [PART, PART])
            ones = sbe("ones", [PART, PART])
            lower8 = sbe("lower8", [PART, GROUPS, GROUPS])
            enum = sbe("enum", [E, 1])
        y2 = sb("y2", [PART, 2, D], fp32r)
        hT2 = sb("hT2", [PART, 2, KD, PART], fp32r)
        aT2 = sb("aT2", [PART, 2, KF, PART], fp32r)
        work = sb("work", [PART, KD * PADDED])
        xs = sb("xs", [PART, TH, D])
        gate2 = sb("gate2", [PART, D])
        SI = sb("SI", [PART, TH, PART])
        ST = sb("ST", [PART, SEQ], fp32r)
        iota = sb("iota", [PART, PADDED])
        sg = sb("sg", [PART, F])
        ident = sb("ident", [PART, PART])
        slotm = sb("slotm", [PART, TH, E])
        wt = sb("wt", [PART, TH, E])
        tab = sb("tab", [1, 1 + 2 * ITEMS], i32)
        st2 = sb("st2", [PART, 16])
        wcol = sb("wcol", [PART, 1])

        def view(t, at, n, k=None):
            v = t[:, at:at + n]
            return v if k is None else v.rearrange("p (k n) -> p k n", k=k)

        TAIL = NBUF * BUFW
        h1T = view(work, 0, 2048, KD)
        gates = view(work, 2048, 4096, 2 * KD)
        upad = view(work, 6144, KC * 288, KC)
        gsig = view(work, 7296, 1024, KC)
        cacc = view(work, 8320, 1024, KC)
        sqb = view(work, 9344, 1024, KC)
        qk = view(work, 10368, 2048, 2 * KC)
        qksq = view(work, 12416, 2048, 2 * KC)
        v_sb = view(work, 14464, 1024, TH)
        oT = view(work, 15488, 1024, KC)
        router = view(work, 16512, KD * E, KD)
        small = view(work, 17024, 384)
        convrow = work[0:TAPS + 3, 0:CONV]
        qkrow = work[0:2, 512:640]
        crow = work[0:KD, 640:768]
        shift1, G1 = view(ring, TAIL, D), view(ring, TAIL + D, D)
        h1 = view(ring, TAIL + 2 * D, 2 * D, TH)
        gate1, shift2 = view(ring, TAIL, D), view(ring, TAIL + D, D)
        h2 = view(ring, TAIL + 2 * D, 2 * D, TH)
        G2, n2g = view(ring, TAIL + 3 * D, D), view(work, D, D)
        bada = view(iota, 0, 1536, 3)
        adat = ring[:, TAIL + 2 * D:TAIL + 2 * D + W]
        adac = view(work, 7296, 2 * W, 2)
        AU = view(misc, 0, 1024, KC)
        BU = view(misc, 1024, 1024, KC)
        zf = work[0:HEADS, 9344:9600]
        za = work[0:HEADS, 9600:9856]
        zl = work[0:HEADS, 9856:10112]
        cum = small[0:HEADS, 0:256]
        rs16 = sg[0:16, :]
        prob = view(work, 12416, 768, 2)
        probT = view(work, 13184, 768, 2)
        h2T = view(work, 10368, 2048, KD)
        sq2 = view(work, 10368, 2048, TH)
        shT = view(work, 2048, 512, 2)
        shg = view(work, 2560, 512, 2)
        r = {n: work[:, 3072 + 128 * i:3200 + 128 * i].rearrange("p (t e) -> p t e", t=TH)
             for i, n in enumerate(("z", "s", "b", "e", "pre", "m", "rep", "sel"))}
        rbias = work[:, 4096:4096 + E]
        top2 = work[:, 4160:4288].rearrange("p (t g e) -> p t g e", t=TH, g=GROUPS)
        gs = work[:, 4288:4304].rearrange("p (t g) -> p t g", t=TH)
        grank = work[:, 4304:4320].rearrange("p (t g) -> p t g", t=TH)
        gmask = work[:, 4320:4336].rearrange("p (t g) -> p t g", t=TH)
        top8 = work[:, 4336:4352].rearrange("p (t e) -> p t e", t=TH)
        cmp1 = work[:, 4352:4480].rearrange("p (t g h) -> p t g h", t=TH, g=GROUPS)
        cmp2 = work[:, 4480:4608].rearrange("p (t g h) -> p t g h", t=TH, g=GROUPS)
        cnt = work[:, 4608:4672]
        incl = work[:, 4672:4736]
        first = work[:, 4736:4800]
        nit = work[:, 4800:4864]
        cumi = work[:, 4864:4930]
        ecol = work[0:E, 4930:4932]
        ecum = work[0:E, 4932:4934]
        ecol2 = work[0:E, 4934:4938]
        slotT = SI[0:E, :, :].rearrange("p t s -> p (t s)")
        jt = work[0:E, 5200:5200 + 5 * ITEMS].rearrange("p (k j) -> p k j", k=5)
        Emat = ring[0:E, TAIL:TAIL + SLOTS]
        h2r = split[:, 4096:8192].rearrange("p (s t d) -> p s t d", s=2, t=TH)
        SS = y2[:, :, :].rearrange("p b (t s) -> p b t s", t=TH)
        hs = work[:, :].rearrange("p (k s) -> p k s", k=KD)
        act = sg

        bank = [ctx.enter_context(nc.psum_tensor(f"bank{i}", [PART, W], fp32)) for i in range(8)]
        acc = bank[4:8]
        psU, psY, psM = bank[0], bank[1:3], bank[3]

        def cols(w, n):
            return w[0, :, n:n + W].rearrange("(k p) n -> p k n", p=PART)

        pieces = [cols(w_ada, W * j) for j in range(4)]
        pieces += [cols(w_in, n) for n in (CONV, 0, OFF_Q, OFF_Q + ATT, OFF_Q + 2 * ATT)]
        for j in range(4):
            pieces += [cols(w_in, OFF_G + W * j), cols(w_ada, W * (4 + 2 * j)), cols(w_ada, W * (5 + 2 * j))]
        pieces += [w_conv_out[0].rearrange("(k p) n -> p k n", p=PART),
                   w_attn_out[0].rearrange("(k p) n -> p k n", p=PART)]
        pieces += [cols(w_out, 0), cols(w_out, W), cols(w_shared_gate_up, 0),
                   w_shared_down[0].rearrange("(k p) n -> p k n", p=PART)]
        (ADA1, INP, GATEP, COUT, AOUT, WOUT, SHGU, SHD) = (0, 4, 9, 21, 22, 23, 25, 26)
        ADA2 = [GATEP + 3 * (j // 2) + 1 + j % 2 for j in range(8)]

        def used_by():
            users = [(adac_ready, j + 1) for j in range(4)]
            users += [(unit_done, 2 * j + 2) for j in range(5)]
            for j in range(4):
                users += [(unit_done, 2 * (5 + j) + 2), (adac_ready, 5 + j), (adac_pool, j + 1)]
            return users + [(yc_done, 4), (ya_done, 4), (mo_done, 3), (mo_done, 4), (sgu_done, 2), (shared_done, 1)]

        def piece(n):
            k, m = pieces[n].shape[1:]
            return view(ring, (n % NBUF) * BUFW, k * m, k)

        def part(q):
            return (q * QW, QW) if q < 4 else (GU, DN)

        def w_raw(b, q):
            return view(raw, b * SLOTW + part(q)[0], part(q)[1])

        def w_hi(q):
            return view(split, part(q)[0] if q < 4 else 2 * GU, part(q)[1])

        def w_lo(q):
            return view(split, GU + part(q)[0] if q < 4 else 2 * GU + DN, part(q)[1])

        piece_in = [sem(f"piece_in{i}") for i in range(NBUF)]
        gu_in = [sem(f"gu_in{i}") for i in range(2)]
        dn_in = [sem(f"dn_in{i}") for i in range(2)]
        x_in, row_in, n1_in, n2_in, bada_in, wf_in, bf_in, rw_in, rb_in, out_done = map(sem, (
            "x_in", "row_in", "n1_in", "n2_in", "bada_in", "wf_in", "bf_in", "rw_in", "rb_in", "out_done"))
        upad_zero, gates_ready = sem("upad_zero"), sem("gates_ready")
        cst, pool_chain, sel_ready, aug_zero, iota_ready, pad_ready = map(sem, (
            "cst", "pool_chain", "sel_ready", "aug_zero", "iota_ready", "pad_ready"))
        dve_chain, act_chain = sem("dve_chain"), sem("act_chain")
        rowsT, rows_out, sc_ready, adac_ready, adac_pool, cT_in, c_in = map(sem, (
            "rowsT", "rows_out", "sc_ready", "adac_ready", "adac_pool", "cT_in", "c_in"))
        ada_done, ada1_out, ada2_out = map(sem, ("ada_done", "ada1_out", "ada2_out"))
        ss_ready, sqrt_in, sqrt_out, h1_ready, h1T_ps, h1T_ready = map(sem, (
            "ss_ready", "sqrt_in", "sqrt_out", "h1_ready", "h1T_ps", "h1T_ready"))
        unit_done, unit_out_dve, unit_out_act, f_done = map(sem, (
            "unit_done", "unit_out_dve", "unit_out_act", "f_done"))
        qkstat, qkrstd, qkb_done, qk_ready = map(sem, (
            "qkstat", "qkrstd", "qkb_done", "qk_ready"))
        gsig_ready, u_ready, conv_step, f_step = map(sem, ("gsig_ready", "u_ready", "conv_step", "f_step"))
        zf_ready, lf_ready, aug_ready = map(sem, ("zf_ready", "lf_ready", "aug_ready"))
        s_done, max_done, exp_done, p_ready, pT_done, pT_out, o_done, o_out = map(sem, (
            "s_done", "max_done", "exp_done", "p_ready", "pT_done", "pT_out", "o_done", "o_out"))
        mean_done, dmu_ready, csq_ready, var_done, crstd, cb_done, yn_ready, cT_ready = map(sem, (
            "mean_done", "dmu_ready", "csq_ready", "var_done", "crstd", "cb_done", "yn_ready", "cT_ready"))
        yc_done, yc_out, ya_done, ya_out, merged, mo_done, x1_ready = map(sem, (
            "yc_done", "yc_out", "ya_done", "ya_out", "merged", "mo_done", "x1_ready"))
        h2_ready, h2T_ps, h2T_ready, logit_done, sgu_done, shg_ready, shT_ready = map(sem, (
            "h2_ready", "h2T_ps", "h2T_ready", "logit_done", "sgu_done", "shg_ready", "shT_ready"))
        z_ready, ez_ready, sel_out, rank_done, ecol_out, ecum_done, tabs_ps_in, tabs_ps, slotT_ps, slotT_out = map(sem, (
            "z_ready", "ez_ready", "sel_out", "rank_done", "ecol_out", "ecum_done", "tabs_ps_in", "tabs_ps",
            "slotT_ps", "slotT_out"))
        E_ready, m1_done, SS_ready, gather_ps, gather_out_act, gather_out_dve, tabs_ready = map(sem, (
            "E_ready", "m1_done", "SS_ready", "gather_ps", "gather_out_act", "gather_out_dve", "tabs_ready"))
        gu_hi, gu_lo, dn_hi, dn_lo, gu_used, h2r_hi, h2r_lo = map(sem, (
            "gu_hi", "gu_lo", "dn_hi", "dn_lo", "gu_used", "h2r_hi", "h2r_lo"))
        hT_hi, hT_lo, silu_done, act_ready, t_done, aT_hi, aT_lo, si_ready, sit_done, st_ready = map(sem, (
            "hT_hi", "hT_lo", "silu_done", "act_ready", "t_done", "aT_hi", "aT_lo", "si_ready", "sit_done", "st_ready"))
        down_done, y_hi, y_lo, shared_done, all_done, fin = map(sem, (
            "down_done", "y_hi", "y_lo", "shared_done", "all_done", "fin"))

        ADA_B = [1, 2, 3, 4]
        H1T_B = [5, 6, 7, 0]
        UNIT_B = [1, 2, 3, 4]
        UNITS = ["g", "g", "a", "a", "q", "q", "k", "k", "v", "v"] + ["m"] * 8
        S_B, PT_B, O_B, ADA2_B, M_B = [0, 1], [2, 3], 4, 5, [6, 7]

        block = ctx.enter_context(nc.Block())

        @block.sync
        def _(sp):
            sp.dma_start(crow, c[0].rearrange("(k p) -> k p", p=PART)).then_inc(c_in, 16)
            users = used_by()
            for n in range(len(pieces)):
                if n >= NBUF:
                    sp.wait_ge(*users[n - NBUF])
                    sp.wait_ge(piece_in[n % NBUF], 16 * (n // NBUF))
                sp.dma_start(piece(n), pieces[n]).then_inc(piece_in[n % NBUF], 16)
                if n == 0:
                    sp.dma_start(xs[:, :, :], x[0].rearrange("(t p) d -> p t d", p=PART)).then_inc(x_in, 16)

            def load_item(i, b, wait=False):
                e = sp.value_load(tab[0:1, bass.ds(i + (1 + ITEMS), 1)], min_val=0, max_val=E - 1)
                if wait:
                    sp.wait_ge(gu_lo, i * 4 - 4)
                sp.dma_start(view(raw, b * SLOTW, GU, KD), w_experts_gate_up[0, bass.ds(e, 1), :, :].rearrange(
                    "o (k p) n -> p (o k) n", p=PART)).then_inc(gu_in[b], 16)
                if wait:
                    sp.wait_ge(dn_lo, i - 1)
                sp.dma_start(view(raw, b * SLOTW + GU, DN, KF), w_experts_down[0, bass.ds(e, 1), :, :].rearrange(
                    "o (k p) n -> p (o k) n", p=PART)).then_inc(dn_in[b], 16)

            sp.wait_ge(*users[AOUT])
            sp.wait_ge(*users[SHGU])
            sp.wait_ge(*users[SHD])
            sp.wait_ge(tabs_ready, 1)
            more = sp.value_load(tab[0:1, 0:1], min_val=1, max_val=ITEMS // 2 - 1)
            for b in range(2):
                load_item(b, b)
            with sp.Fori(1, more + 1) as g:
                for b in range(2):
                    load_item(g * 2 + b, b, wait=True)
            for t in range(TH):
                for n in range(2):
                    sp.wait_ge(fin, t * 2 + n + 1)
                    sp.dma_start(out[0, t * PART:(t + 1) * PART, n * W:(n + 1) * W],
                                 xs[:, t, n * W:(n + 1) * W]).then_inc(out_done, 16)
            sp.wait_ge(out_done, 16 * TH * 2)

        @block.gpsimd
        def _(pool):
            chain = [0]

            def link(ins):
                chain[0] += 1
                ins.then_inc(pool_chain, 1)
                pool.wait_ge(pool_chain, chain[0])

            link(pool.memset(ident[:, :], 0.0))
            pool.affine_select(out=ident[:, :], in_=ident[:, :], compare_op=ALU.not_equal, fill=1.0, base=0,
                               pattern=[[-1, PART]], channel_multiplier=1).then_inc(cst, 1)
            pool.memset(ones[:, :], 1.0).then_inc(cst, 1)
            link(pool.memset(headsum[:, :, :], 0.0))
            link(pool.memset(headrow[:, :, :], 0.0))
            for half in range(2):
                hr = headrow[:, :, half * HD:(half + 1) * HD]
                link(pool.affine_select(out=headsum[half * HD:(half + 1) * HD, :, :],
                                        in_=headsum[half * HD:(half + 1) * HD, :, :],
                                        compare_op=ALU.not_equal, fill=1.0 / HD, base=half,
                                        pattern=[[2, 8], [-1, 16]], channel_multiplier=0))
                link(pool.affine_select(out=hr, in_=hr, compare_op=ALU.not_equal, fill=1.0, base=-half,
                                        pattern=[[-2, 8], [0, HD]], channel_multiplier=1))
            link(pool.memset(blk[:, :], 0.0))
            for half in range(2):
                link(pool.memset(blk[half * HD:(half + 1) * HD, half * HD:(half + 1) * HD], 1.0 / HD))
            pool.memset(upad[:, :, 0:TAPS - 1], 0.0).then_inc(upad_zero, 1)
            link(pool.memset(causal[:, :], 0.0))
            link(pool.affine_select(out=causal[:, :], in_=causal[:, :], compare_op=ALU.is_ge, fill=NEG, base=PART,
                                    pattern=[[-1, 2 * PART]], channel_multiplier=1))
            link(pool.memset(before[:, :], 0.0))
            link(pool.affine_select(out=before[:, :], in_=before[:, :], compare_op=ALU.is_ge, fill=1.0, base=0,
                                    pattern=[[-1, PART]], channel_multiplier=1))
            link(pool.iota(enum[:, :], pattern=[[0, 1]], base=0, channel_multiplier=1,
                           allow_small_or_imprecise_dtypes=True))
            link(pool.memset(lower8[:, :, :], 0.0))
            pool.affine_select(out=lower8[:, :, :], in_=lower8[:, :, :], compare_op=ALU.is_ge, fill=1.0, base=0,
                               pattern=[[-1, GROUPS], [1, GROUPS]], channel_multiplier=0).then_inc(sel_ready, 1)
            pool.wait_ge(sel_ready, 1)
            link(pool.memset(misc[:, :], 0.0))
            for t, rows in ((AU, 32), (BU, 0)):
                for par in range(2):
                    a = t[64 * par + rows:64 * par + rows + HEADS, :, :]
                    pool.affine_select(out=a, in_=a, compare_op=ALU.not_equal, fill=1.0, base=-par,
                                       pattern=[[-2, KC], [0, SEQ]], channel_multiplier=1).then_inc(aug_zero, 1)
                    pool.wait_ge(aug_zero, (1 if t is BU else 0) * 2 + par + 1)
            pool.wait_ge(sc_ready, 1)
            pool.wait_ge(h1T_ps, 4)
            pool.wait_ge(unit_out_dve, 2)
            for j in range(1, 8, 2):
                n = ADA2[j]
                w = piece(n)
                pool.wait_ge(piece_in[n % NBUF], 16 * (n // NBUF + 1))
                pool.wait_ge(ada_done, 4 + j - 1)
                link(pool.tensor_scalar(adac[:, 1, :], w[:, 0, :], sc[:, 0:1], None, ALU.mult))
                for k in range(1, KD):
                    link(pool.tensor_scalar(adat, w[:, k, :], sc[:, k:k + 1], None, ALU.mult))
                    ins = pool.tensor_tensor(adac[:, 1, :], adac[:, 1, :], adat, ALU.add)
                    if k < KD - 1:
                        link(ins)
                ins.then_inc(adac_pool, 1)
                pool.wait_ge(adac_pool, j // 2 + 1)
            pool.wait_ge(ada_done, 12)
            pool.iota(iota[:, :], pattern=[[1, PADDED]], base=0, channel_multiplier=0,
                      allow_small_or_imprecise_dtypes=True).then_inc(iota_ready, 1)
            pool.wait_ge(iota_ready, 1)
            pool.wait_ge(SS_ready, 8)
            pool.wait_ge(tabs_ready, 1)
            pool.memset(hs[:, :, SLOTS:PADDED], 0.0).then_inc(pad_ready, 1)
            more = pool.value_load(tab[0:1, 0:1], min_val=1, max_val=ITEMS // 2 - 1)
            with pool.Fori(0, more + 1) as g:
                for b in range(2):
                    pool.wait_ge(dn_hi, g * 2 + b + 1)
                    pool.tensor_tensor(w_lo(4), w_raw(b, 4), w_hi(4).bitcast(fp32), ALU.subtract).then_inc(dn_lo, 1)

        @block.scalar
        def _(a):
            chain = [0]

            def link(ins):
                chain[0] += 1
                ins.then_inc(act_chain, 1)
                a.wait_ge(act_chain, chain[0])

            for q in range(4):
                a.dma_start(bada[32 * q:32 * q + 1, :, :],
                            b_ada[0:1, q * 1536:(q + 1) * 1536].rearrange("o (k n) -> o k n", k=3)).then_inc(bada_in, 16)
            a.dma_start(G1, norm1_g.broadcast_to([PART, D])).then_inc(n1_in, 16)
            for i, (src, n) in enumerate(((w_dw[0], TAPS), (b_dw, 1), (conv_gn_g, 1), (conv_gn_b, 1))):
                a.dma_start(convrow[(0, TAPS, TAPS + 1, TAPS + 2)[i]:(0, TAPS, TAPS + 1, TAPS + 2)[i] + n, :],
                            src).then_inc(row_in, 16)
            for i, g in enumerate((q_norm_g, k_norm_g)):
                for half in range(2):
                    a.dma_start(qkrow[i:i + 1, half * HD:(half + 1) * HD], g).then_inc(row_in, 16)
            a.dma_start(bf[:, :], b_forget[0].rearrange("(h o) -> h o", o=1)).then_inc(bf_in, 16)
            with nc.allow_non_contiguous_dma(reason="eight columns of w_in"):
                a.dma_start(wf[:, :, :], w_in[0, :, OFF_F:OFF_F + HEADS].rearrange("(k p) n -> p k n", p=PART)).then_inc(wf_in, 16)
            a.dma_start(router, w_router[0].rearrange("(k p) n -> p k n", p=PART)).then_inc(rw_in, 16)

            a.wait_ge(cT_in, 1)
            a.activation(sc[:, :], bank[5][:, 0:KD], ACT.Silu).then_inc(sc_ready, 1)
            a.wait_ge(x_in, 16)
            for t in range(TH):
                a.activation(h1[:, t, :], xs[:, t, :], ACT.Square, accum_out=st2[:, t:t + 1]).then_inc(ss_ready, 1)
            a.wait_ge(sqrt_in, 1)
            a.activation(st2[:, 4:6], st2[:, 2:4], ACT.Sqrt).then_inc(sqrt_out, 1)
            for i in range(4):
                a.wait_ge(h1T_ps, i + 1)
                a.activation(h1T[:, 2 * i:2 * i + 2, :], bank[H1T_B[i]][:, :].rearrange("p (k n) -> p k n", k=2),
                             ACT.Copy).then_inc(h1T_ready, 1)
            for u, kind in enumerate(UNITS[:10]):
                if kind == "a":
                    continue
                a.wait_ge(unit_done, u + 1)
                ps = bank[UNIT_B[u % 4]]
                ps2 = ps[:, :].rearrange("p (k n) -> p k n", k=2)
                if kind == "g":
                    a.wait_ge(ada_done, 4)
                    ins = a.activation(gsig[:, 2 * u:2 * u + 2, :], ps2, ACT.Sigmoid)
                elif kind in "qk":
                    c0 = 2 * (u - 4)
                    a.activation(qk[:, c0:c0 + 2, :], ps2, ACT.Copy)
                    ins = a.activation(qksq[:, c0:c0 + 2, :], ps2, ACT.Square)
                else:
                    ins = a.activation(v_sb[:, u - 8, :], ps[:, :], ACT.Copy)
                ins.then_inc(unit_out_act, 1)
                if u == 7:
                    a.wait_ge(f_done, 1)
                    a.wait_ge(bf_in, 16)
                    a.activation(zf, bank[5][0:HEADS, 0:SEQ], ACT.Identity, bias=bf[:, 0:1]).then_inc(zf_ready, 1)
                    a.wait_ge(zf_ready, 1)
                    link(a.activation(za, zf, ACT.Abs))
                    link(a.activation(za, za, ACT.Exp, scale=-1.0))
                    a.activation(zl, za, ACT.Ln, bias=1.0).then_inc(lf_ready, 1)
                    a.wait_ge(qkstat, 2)
                    a.activation(rs16[:, :], rs16[:, :], ACT.Sqrt).then_inc(qkrstd, 1)
            def ada_out(j):
                dst = (gate1, shift2, G2, gate2[:, :])[j // 2][:, (j % 2) * W:(j % 2) * W + W]
                a.wait_ge(ada_done, 4 + j + 1)
                a.activation(dst, bank[ADA2_B][:, :], ACT.Identity if j // 2 == 2 else ACT.Copy,
                             bias=1.0 if j // 2 == 2 else 0.0).then_inc(ada2_out, 1)

            def gate_out(h):
                a.wait_ge(unit_done, 10 + h + 1)
                a.activation(gates[:, 2 * h:2 * h + 2, :], bank[M_B[h % 2]][:, :].rearrange("p (k n) -> p k n", k=2),
                             ACT.Copy).then_inc(unit_out_act, 1)

            for h in range(HEADS):
                a.wait_ge(max_done, 2 * h + 2)
                if h >= 2:
                    a.wait_ge(pT_done, h - 1)
                ps = bank[S_B[h % 2]]
                a.activation(prob[:, h % 2, 0:PART], ps[:, 0:PART], ACT.Exp, bias=st2[:, 6:7] if h % 2 == 0 else st2[:, 10:11],
                             accum_out=st2[:, 8:9] if h % 2 == 0 else st2[:, 12:13])
                a.activation(prob[:, h % 2, PART:3 * PART], ps[:, PART:3 * PART], ACT.Exp,
                             bias=st2[:, 7:8] if h % 2 == 0 else st2[:, 11:12],
                             accum_out=st2[:, 9:10] if h % 2 == 0 else st2[:, 13:14]).then_inc(exp_done, 1)
                if h >= 1:
                    gate_out(h - 1)
                    ada_out(h - 1)
            gate_out(HEADS - 1)
            a.wait_ge(unit_out_act, 16)
            for i in (1, 0):
                a.activation(gates[:, i * KD:(i + 1) * KD, :], gates[:, i * KD:(i + 1) * KD, :], ACT.Sigmoid).then_inc(gates_ready, 1)
            ada_out(HEADS - 1)
            a.dma_start(n2g, norm2_g.broadcast_to([PART, D])).then_inc(n2_in, 16)
            a.wait_ge(dmu_ready, 2)
            a.activation(sqb, gsig, ACT.Square).then_inc(csq_ready, 1)
            a.wait_ge(crstd, 1)
            a.activation(rs16[0:8, :], rs16[0:8, :], ACT.Sqrt).then_inc(crstd, 1)
            for k in range(KC):
                a.wait_ge(yn_ready, k // 2 + 1)
                a.activation(cacc[:, k, :], sqb[:, k, :], ACT.Silu, scale=convc[:, k, TAPS + 1:TAPS + 2],
                             bias=convc[:, k, TAPS + 2:TAPS + 3]).then_inc(cT_ready, 1)
            for t in range(TH):
                a.wait_ge(x1_ready, 2 * t + 2)
                a.activation(sq2[:, t, :], xs[:, t, :], ACT.Square, accum_out=st2[:, t:t + 1]).then_inc(ss_ready, 1)
            a.dma_start(rbias, router_bias.broadcast_to([PART, E])).then_inc(rb_in, 16)
            a.wait_ge(sqrt_in, 2)
            a.activation(st2[:, 4:6], st2[:, 2:4], ACT.Sqrt).then_inc(sqrt_out, 1)
            for i in range(4):
                a.wait_ge(h2T_ps, i + 1)
                a.activation(h2T[:, 2 * i:2 * i + 2, :], bank[i][:, :].rearrange("p (k n) -> p k n", k=2),
                             ACT.Copy).then_inc(h2T_ready, 1)
            a.wait_ge(z_ready, 1)
            a.activation(r["e"], r["z"], ACT.Exp, scale=-1.0).then_inc(ez_ready, 1)
            a.wait_ge(sgu_done, 1)
            a.activation(shg[:, :, :], bank[1][:, :].rearrange("p (k n) -> p k n", k=2), ACT.Silu).then_inc(shg_ready, 1)
            a.wait_ge(h2_ready, TH)
            a.wait_ge(mo_done, 4)
            a.activation(h2r[:, 0], h2, ACT.Copy).then_inc(h2r_hi, 1)

            def hi(i, b, q):
                if q < 4:
                    a.activation(w_hi(q), w_raw(b, q), ACT.Copy).then_inc(gu_hi, 1)
                else:
                    a.activation(w_hi(q), w_raw(b, q), ACT.Copy).then_inc(dn_hi, 1)

            for i in range(0, 4 * KD, 2):
                a.wait_ge(gather_ps, i + 1)
                if i == 0:
                    a.wait_ge(tabs_ready, 1)
                a.activation(hs[:, i % KD, (i // KD) * W:(i // KD) * W + W], bank[0][:, :], ACT.Copy).then_inc(gather_out_act, 1)
                if i >= 2 * KD and i % 4 == 2:
                    if i == 2 * KD + 2:
                        a.wait_ge(gu_in[0], 16)
                    hi(0, 0, (i - 2 * KD) // 4)
            a.wait_ge(gather_out_dve, 2 * KD)
            a.wait_ge(gather_out_act, 2 * KD)
            a.wait_ge(pad_ready, 1)
            more = a.value_load(tab[0:1, 0:1], min_val=1, max_val=ITEMS // 2 - 1)

            def next_input(i):
                p = a.value_load(tab[0:1, bass.ds(i + 1, 1)], min_val=0, max_val=SLOTS)
                a.activation(hT2[:, 0], hs[:, :, bass.ds(p, PART)], ACT.Copy).then_inc(hT_hi, 1)

            next_input(0)
            a.wait_ge(dn_in[0], 16)
            a.wait_ge(gather_ps, 4 * KD)
            hi(0, 0, 4)

            def item(i, g, b, last):
                nb = 1 - b
                if not last:
                    a.wait_ge(gu_in[nb], g * 16 + (16 if b == 0 else 32))
                    for q in range(2):
                        a.wait_ge(gu_used, i * 4 + q + 1)
                        hi(i + 1, nb, q)
                a.wait_ge(gu_used, i * 4 + 4)
                a.activation(sg[:, :], psU[:, 0:F], ACT.Silu).then_inc(silu_done, 1)
                if not last:
                    hi(i + 1, nb, 2)
                a.wait_ge(t_done, i + 1)
                a.activation(aT2[:, 0], psM[:, 0:F].rearrange("p (k n) -> p k n", k=KF), ACT.Copy).then_inc(aT_hi, 1)
                if not last:
                    next_input(i + 1)
                    hi(i + 1, nb, 3)
                a.wait_ge(down_done, i + 1)
                a.wait_ge(st_ready, i + 2)
                for n in range(2):
                    a.activation(y2[:, 0, n * W:(n + 1) * W], psY[n][:, :], ACT.Copy, scale=wcol[:, 0:1]).then_inc(y_hi, 1)
                if not last:
                    a.wait_ge(dn_in[nb], g * 16 + (16 if b == 0 else 32))
                    hi(i + 1, nb, 4)

            with a.Fori(0, more) as g:
                for b in range(2):
                    item(g * 2 + b, g, b, False)
            for b in range(2):
                item(more * 2 + b, more, b, b == 1)

        @block.vector
        def _(v):
            chain = [0]

            def link(ins):
                chain[0] += 1
                ins.then_inc(dve_chain, 1)
                v.wait_ge(dve_chain, chain[0])

            def rstd():
                v.tensor_scalar(st2[:, 2:4], st2[:, 0:2], 1.0 / D, EPS, ALU.mult, ALU.add).then_inc(sqrt_in, 1)

            def rstd2(n):
                v.wait_ge(sqrt_out, n)
                link(v.reciprocal(st2[:, 6:8], st2[:, 4:6]))
                link(v.tensor_tensor(st2[:, 8:10], st2[:, 6:8], st2[:, 6:8], ALU.mult))
                link(v.tensor_tensor(st2[:, 8:10], st2[:, 8:10], st2[:, 2:4], ALU.mult))
                link(v.tensor_scalar(st2[:, 8:10], st2[:, 8:10], -0.5, 1.5, ALU.mult, ALU.add))
                link(v.tensor_tensor(st2[:, 14:16], st2[:, 6:8], st2[:, 8:10], ALU.mult))

            v.wait_ge(ss_ready, TH)
            rstd()
            def ada_sum(j, n, ks):
                w = piece(n)
                for k in ks:
                    if k == 0:
                        v.wait_ge(piece_in[n % NBUF], 16 * (n // NBUF + 1))
                        if j >= 2:
                            v.wait_ge(ada_done, j - 1)
                        ins = v.tensor_scalar(adac[:, j % 2, :], w[:, 0, :], sc[:, 0:1], None, ALU.mult)
                    else:
                        ins = v.scalar_tensor_tensor(adac[:, j % 2, :], w[:, k, :], sc[:, k:k + 1], adac[:, j % 2, :],
                                                     ALU.mult, ALU.add)
                    if k < KD - 1:
                        link(ins)
                    else:
                        ins.then_inc(adac_ready, 1)

            v.wait_ge(sc_ready, 1)
            for j in range(4):
                ada_sum(j, ADA1 + j, range(KD))
            v.wait_ge(rowsT, 1)
            v.tensor_copy(convc[:, :, :], bank[0][:, 64:64 + KC * (TAPS + 3)].rearrange("p (k n) -> p k n", k=KC))
            v.tensor_copy(qkg[:, 1:2], bank[0][:, 241:242])
            v.tensor_scalar(qkg[:, 0:1], bank[0][:, 240:241], HD ** -0.5, None, ALU.mult).then_inc(rows_out, 1)

            for j in range(4):
                v.wait_ge(ada_done, j + 1)
                dst = (shift1, G1)[j // 2][:, (j % 2) * W:(j % 2) * W + W]
                if j < 2:
                    v.tensor_copy(dst, bank[ADA_B[j]][:, :]).then_inc(ada1_out, 1)
                else:
                    v.wait_ge(n1_in, 16)
                    v.scalar_tensor_tensor(dst, bank[ADA_B[j]][:, :], 1.0, dst, ALU.add, ALU.mult).then_inc(ada1_out, 1)
            rstd2(1)
            v.wait_ge(ada1_out, 4)
            for t in range(TH):
                link(v.scalar_tensor_tensor(h1[:, t, :], xs[:, t, :], st2[:, 14 + t:15 + t], G1, ALU.mult, ALU.mult))
                v.tensor_tensor(h1[:, t, :], h1[:, t, :], shift1, ALU.add).then_inc(h1_ready, 1)
            v.wait_ge(upad_zero, 1)
            for u in (2, 3):
                v.wait_ge(unit_done, u + 1)
                v.wait_ge(unit_out_act, u - 1)
                k = 2 * (u - 2)
                v.tensor_tensor(upad[:, k:k + 2, TAPS - 1:TAPS - 1 + SEQ],
                                bank[UNIT_B[u % 4]][:, :].rearrange("p (k n) -> p k n", k=2),
                                gsig[:, k:k + 2, :], ALU.mult).then_inc(unit_out_dve, 1)
            v.wait_ge(rows_out, 1)
            v.wait_ge(unit_out_dve, 2)
            for k in range(KC):
                v.tensor_scalar(cacc[:, k, :], upad[:, k, 0:SEQ], convc[:, k, 0:1], convc[:, k, TAPS:TAPS + 1],
                                ALU.mult, ALU.add).then_inc(conv_step, 1)
            taps_done = [1]

            def taps(n):
                first, last = taps_done[0], min(taps_done[0] + n, TAPS)
                taps_done[0] = last
                if first == last:
                    return
                with v.Fori(first, last) as j:
                    for k in range(KC):
                        v.wait_ge(conv_step, (j - 1) * KC + k + 1)
                        v.scalar_tensor_tensor(cacc[:, k, :], upad[:, k, bass.ds(j, SEQ)], convc[:, k, bass.ds(j, 1)],
                                               cacc[:, k, :], ALU.mult, ALU.add).then_inc(conv_step, 1)

            taps(14)
            v.wait_ge(qkstat, 1)
            v.tensor_scalar(rs16[:, :], bank[6][0:16, 0:SEQ], EPS, None, ALU.add).then_inc(qkstat, 1)
            taps(2)
            v.wait_ge(qkrstd, 1)
            v.reciprocal(rs16[:, :], rs16[:, :]).then_inc(qkrstd, 1)
            for i in range(4):
                v.wait_ge(qkb_done, i + 1)
                v.scalar_tensor_tensor(qk[:, 2 * i:2 * i + 2, :], qk[:, 2 * i:2 * i + 2, :],
                                       qkg[:, i // 2:i // 2 + 1],
                                       bank[UNIT_B[i % 4]][:, :].rearrange("p (k n) -> p k n", k=2),
                                       ALU.mult, ALU.mult).then_inc(qk_ready, 1)
            v.wait_ge(lf_ready, 1)
            link(v.tensor_scalar(za, zf, 0.0, None, ALU.min))
            link(v.tensor_tensor(zl, za, zl, ALU.subtract))
            link(v.memset(za, 1.0))
            link(v.tensor_tensor_scan(cum, za, zl, 0.0, ALU.mult, ALU.add))
            v.wait_ge(aug_zero, 4)
            for par in range(2):
                v.tensor_copy(AU[64 * par:64 * par + HEADS, :, :], cum.unsqueeze(1).broadcast_to([HEADS, KC, SEQ]))
                ins = v.tensor_scalar(BU[64 * par + 32:64 * par + 32 + HEADS, :, :],
                                      cum.unsqueeze(1).broadcast_to([HEADS, KC, SEQ]), -1.0, None, ALU.mult)
            ins.then_inc(aug_ready, 1)

            def head_max(h):
                ps = bank[S_B[h % 2]]
                v.wait_ge(s_done, h + 1)
                o = 6 if h % 2 == 0 else 10
                v.tensor_reduce(st2[:, o:o + 1], ps[:, 0:PART], AX, ALU.max, negate=True).then_inc(max_done, 1)
                v.tensor_reduce(st2[:, o + 1:o + 2], ps[:, PART:3 * PART], AX, ALU.max, negate=True).then_inc(max_done, 1)

            def head_norm(h):
                o = 8 if h % 2 == 0 else 12
                v.wait_ge(exp_done, h + 1)
                link(v.reciprocal(st2[:, o:o + 2], st2[:, o:o + 2]))
                v.tensor_scalar(prob[:, h % 2, 0:PART], prob[:, h % 2, 0:PART], st2[:, o:o + 1], None, ALU.mult)
                v.tensor_scalar(prob[:, h % 2, PART:3 * PART], prob[:, h % 2, PART:3 * PART], st2[:, o + 1:o + 2],
                                None, ALU.mult).then_inc(p_ready, 1)

            def head_pT(h):
                v.wait_ge(pT_done, h + 1)
                if h >= 2:
                    v.wait_ge(o_done, h - 1)
                v.tensor_copy(probT[:, h % 2, :], bank[PT_B[h % 2]][:, 0:3 * PART]).then_inc(pT_out, 1)

            def head_out(h):
                if h % 2 == 1:
                    v.wait_ge(o_done, h + 1)
                    v.tensor_copy(oT[:, h // 2, :], bank[O_B][:, 0:SEQ]).then_inc(o_out, 1)

            for step in range(HEADS + 1):
                if step < HEADS:
                    head_max(step)
                taps(1)
                if step >= 1:
                    head_norm(step - 1)
                if step < HEADS and step % 2 == 0:
                    ada_sum(4 + step, ADA2[step], range(KD // 2))
                if step >= 1:
                    head_pT(step - 1)
                if step < HEADS and step % 2 == 0:
                    ada_sum(4 + step, ADA2[step], range(KD // 2, KD))
                else:
                    taps(2)
                if step >= 2:
                    head_out(step - 2)
            head_out(HEADS - 1)
            for i in range(2):
                v.wait_ge(mean_done, i + 1)
                v.tensor_tensor(gsig[:, 2 * i:2 * i + 2, :], cacc[:, 2 * i:2 * i + 2, :],
                                bank[6 + i][:, :].rearrange("p (k n) -> p k n", k=2), ALU.subtract).then_inc(dmu_ready, 1)
            v.wait_ge(var_done, 1)
            v.tensor_scalar(rs16[0:8, :], bank[0][0:8, 0:SEQ], EPS, None, ALU.add).then_inc(crstd, 1)
            v.wait_ge(crstd, 2)
            v.reciprocal(rs16[0:8, :], rs16[0:8, :]).then_inc(crstd, 1)
            for i in range(2):
                v.wait_ge(cb_done, i + 1)
                v.tensor_tensor(sqb[:, 2 * i:2 * i + 2, :], gsig[:, 2 * i:2 * i + 2, :],
                                bank[1 + i][:, :].rearrange("p (k n) -> p k n", k=2), ALU.mult).then_inc(yn_ready, 1)
            for i in range(4):
                v.wait_ge(ya_done, i + 1)
                if i == 0:
                    v.wait_ge(gates_ready, 1)
                v.tensor_tensor(gates[:, KD + 2 * i:KD + 2 * i + 2, :], gates[:, KD + 2 * i:KD + 2 * i + 2, :],
                                bank[3 + i][:, :].rearrange("p (k n) -> p k n", k=2), ALU.mult).then_inc(ya_out, 1)
            for i in range(4):
                v.wait_ge(yc_done, i + 1)
                if i == 0:
                    v.wait_ge(gates_ready, 2)
                g = gates[:, 2 * i:2 * i + 2, :]
                v.tensor_tensor(g, g, bank[3 + i][:, :].rearrange("p (k n) -> p k n", k=2), ALU.mult).then_inc(yc_out, 1)
                v.wait_ge(yc_out, i + 1)
                v.tensor_tensor(g, g, gates[:, KD + 2 * i:KD + 2 * i + 2, :], ALU.add).then_inc(merged, 1)
            v.wait_ge(ada2_out, 8)
            for t in range(TH):
                for n in range(2):
                    i = 2 * t + n
                    v.wait_ge(mo_done, i + 1)
                    link(v.tensor_tensor(cacc[:, 0:2, :].rearrange("p k n -> p (k n)"), bank[i][:, :],
                                         gate1[:, n * W:(n + 1) * W], ALU.mult))
                    v.tensor_tensor(xs[:, t, n * W:(n + 1) * W], xs[:, t, n * W:(n + 1) * W],
                                    cacc[:, 0:2, :].rearrange("p k n -> p (k n)"), ALU.add).then_inc(x1_ready, 1)
                    v.wait_ge(x1_ready, i + 1)
            v.wait_ge(n2_in, 16)
            link(v.tensor_tensor(G2, G2, n2g, ALU.mult))
            v.wait_ge(ss_ready, 2 * TH)
            rstd()
            rstd2(2)
            for t in range(TH):
                link(v.scalar_tensor_tensor(h2[:, t, :], xs[:, t, :], st2[:, 14 + t:15 + t], G2, ALU.mult, ALU.mult))
                v.tensor_tensor(h2[:, t, :], h2[:, t, :], shift2, ALU.add).then_inc(h2_ready, 1)
            v.wait_ge(logit_done, 1)
            v.tensor_scalar(r["z"], bank[0][:, 0:TH * E].rearrange("p (t e) -> p t e", t=TH), LOWEST, None,
                            ALU.max).then_inc(z_ready, 1)
            v.wait_ge(ez_ready, 1)
            link(v.tensor_scalar(r["e"], r["e"], 1.0, None, ALU.add))
            link(v.reciprocal(r["s"], r["e"]))
            v.wait_ge(rb_in, 16)
            link(v.tensor_tensor(r["b"], r["s"], rbias.unsqueeze(1).broadcast_to([PART, TH, E]), ALU.add))
            for t in range(TH):
                for g in range(GROUPS):
                    ins = v.max(top2[:, t, g, :], r["b"][:, t, g * EPG:(g + 1) * EPG])
            link(ins)
            link(v.tensor_tensor(gs, top2[:, :, :, 0], top2[:, :, :, 1], ALU.add))
            mine = gs.unsqueeze(3).broadcast_to([PART, TH, GROUPS, GROUPS])
            theirs = gs.unsqueeze(2).broadcast_to([PART, TH, GROUPS, GROUPS])
            v.wait_ge(sel_ready, 1)
            for t in range(TH):
                v.tensor_tensor(cmp1[:, t], theirs[:, t], mine[:, t], ALU.is_gt)
                ins = v.tensor_tensor(cmp2[:, t], theirs[:, t], mine[:, t], ALU.is_equal)
            link(ins)
            link(v.tensor_tensor(cmp2, cmp2, lower8[:, :, :].unsqueeze(1).broadcast_to([PART, TH, GROUPS, GROUPS]), ALU.mult))
            link(v.tensor_tensor(cmp1, cmp1, cmp2, ALU.add))
            link(v.tensor_reduce(grank, cmp1, AX, ALU.add))
            link(v.tensor_scalar(gmask, grank, float(TOPG), None, ALU.is_lt))
            em = gmask.unsqueeze(3).broadcast_to([PART, TH, GROUPS, EPG])
            grp = {n: r[n].rearrange("p t (g e) -> p t g e", g=GROUPS) for n in ("b", "m", "pre")}
            for t in range(TH):
                v.tensor_tensor(grp["m"][:, t], grp["b"][:, t], em[:, t], ALU.mult)
                ins = v.tensor_scalar(grp["pre"][:, t], em[:, t], -NEG, NEG, ALU.mult, ALU.add)
            link(ins)
            link(v.tensor_tensor(r["m"], r["m"], r["pre"], ALU.add))
            for t in range(TH):
                ins = v.max(top8[:, t, :], r["m"][:, t, :])
            link(ins)
            for t in range(TH):
                ins = v.match_replace(r["rep"][:, t, :], top8[:, t, :], r["m"][:, t, :], 2.0 * NEG)
            link(ins)
            v.tensor_tensor(r["sel"], r["rep"], r["m"], ALU.not_equal).then_inc(sel_out, 1)
            v.wait_ge(sel_out, 1)
            link(v.tensor_tensor(wt[:, :, :], r["s"], r["sel"], ALU.mult))
            link(v.tensor_reduce(st2[:, 0:2], wt[:, :, :], AX, ALU.add))
            link(v.reciprocal(st2[:, 0:2], st2[:, 0:2]))
            for t in range(TH):
                ins = v.tensor_scalar(wt[:, t, :], wt[:, t, :], st2[:, t:t + 1], ROUTED_SCALE, ALU.mult, ALU.mult)
            link(ins)
            v.wait_ge(rank_done, 1)
            link(v.tensor_copy(cnt, bank[0][:, 128:128 + E]))
            link(v.tensor_tensor_scan(incl, ones[:, 0:E], cnt, 0.0, ALU.mult, ALU.add))
            link(v.tensor_tensor(first, incl, cnt, ALU.subtract))
            link(v.tensor_tensor(slotm[:, :, :], bank[0][:, 256:256 + TH * E].rearrange("p (t e) -> p t e", t=TH),
                                 first.unsqueeze(1).broadcast_to([PART, TH, E]), ALU.add))
            link(v.scalar_tensor_tensor(slotm[:, :, :], slotm[:, :, :], 1.0, r["sel"], ALU.add, ALU.mult))
            v.tensor_scalar(slotm[:, :, :], slotm[:, :, :], -1.0, None, ALU.add).then_inc(slotT_out, 1)
            link(v.tensor_copy(ecol[:, 0:1], bank[0][0:E, 448:449]))
            link(v.tensor_scalar(ecol2[:, 0:1], ecol[:, 0:1], 0.0, None, ALU.is_gt))
            link(v.tensor_scalar(ecol2[:, 1:2], ecol[:, 0:1], float(PART), None, ALU.is_gt))
            v.tensor_tensor(ecol[:, 1:2], ecol2[:, 0:1], ecol2[:, 1:2], ALU.add).then_inc(ecol_out, 1)
            v.wait_ge(ecum_done, 1)
            v.wait_ge(slotT_ps, 1)
            link(v.tensor_copy(ecum, bank[3][0:E, 256:258]))
            link(v.tensor_copy(slotT, bank[3][0:E, 0:SEQ]))
            link(v.tensor_tensor(ecol2[:, 2:4], ecum, ecol, ALU.add))
            v.wait_ge(iota_ready, 1)
            v.wait_ge(h2_ready, TH)
            link(v.tensor_scalar(Emat, iota[0:E, 0:SLOTS], ecol2[:, 2:3], None, ALU.is_ge))
            v.scalar_tensor_tensor(Emat, iota[0:E, 0:SLOTS], ecum[:, 0:1], Emat, ALU.is_ge, ALU.subtract).then_inc(E_ready, 1)
            j = iota[0:E, 0:ITEMS]
            link(v.tensor_scalar(jt[:, 0, :], j, ecum[:, 1:2], None, ALU.is_ge))
            link(v.scalar_tensor_tensor(jt[:, 1, :], j, ecol2[:, 3:4], jt[:, 0, :], ALU.is_lt, ALU.mult))
            link(v.tensor_scalar(jt[:, 0, :], j, ecum[:, 1:2], float(PART), ALU.subtract, ALU.mult))
            v.scalar_tensor_tensor(jt[:, 2, :], jt[:, 0, :], ecum[:, 0:1], jt[:, 1, :], ALU.add, ALU.mult).then_inc(tabs_ps_in, 1)
            link(v.tensor_scalar(nit[:, :], cnt, 0.0, None, ALU.is_gt))
            link(v.scalar_tensor_tensor(nit[:, :], cnt, float(PART), nit[:, :], ALU.is_gt, ALU.add))
            link(v.memset(cumi[:, 0:1], 0.0))
            link(v.tensor_tensor_scan(cumi[:, 1:E + 1], ones[:, 0:E], nit[:, :], 0.0, ALU.mult, ALU.add))
            total = cumi[0:1, E:E + 1]
            half = ITEMS // 2
            j = jt[0:1, 3, 0:half]
            link(v.tensor_scalar(j, iota[0:1, 0:half], 2.0, None, ALU.mult))
            link(v.tensor_scalar(j, j, total, None, ALU.is_lt))
            link(v.tensor_reduce(cumi[0:1, 0:1], j, AX, ALU.add))
            link(v.tensor_scalar(tab[0:1, 0:1], cumi[0:1, 0:1], -1.0, None, ALU.add))
            behind = jt[0:1, 4, :]
            link(v.tensor_scalar(behind, iota[0:1, 0:ITEMS], total, float(SLOTS), ALU.is_ge, ALU.mult))
            v.wait_ge(tabs_ps, 1)
            v.tensor_tensor(tab[0:1, 1:1 + ITEMS], bank[3][0:1, 0:ITEMS], behind, ALU.add)
            v.tensor_copy(tab[0:1, 1 + ITEMS:1 + 2 * ITEMS], bank[3][0:1, ITEMS:2 * ITEMS]).then_inc(tabs_ready, 1)
            v.wait_ge(shg_ready, 1)
            v.wait_ge(sgu_done, 2)
            v.tensor_tensor(shT, shg, bank[2][:, :].rearrange("p (k n) -> p k n", k=2), ALU.mult).then_inc(shT_ready, 1)

            v.wait_ge(h2r_hi, 1)
            v.tensor_tensor(h2r[:, 1], h2, h2r[:, 0].bitcast(fp32), ALU.subtract).then_inc(h2r_lo, 1)

            def select(q):
                for t in range(TH):
                    v.wait_ge(m1_done, 2 * q + t + 1)
                    if q >= 2:
                        v.wait_ge(gather_ps, KD * (q - 1))
                    v.tensor_tensor(SS[:, q % 2, t, :], bank[2 + t][:, :], iota[:, q * W:(q + 1) * W],
                                    ALU.is_equal).then_inc(SS_ready, 1)

            select(0)
            for q in range(4):
                if q < 3:
                    select(q + 1)
                for i in range(KD * q + 1, KD * (q + 1), 2):
                    v.wait_ge(gather_ps, i + 1)
                    v.tensor_copy(hs[:, i % KD, q * W:(q + 1) * W], bank[1][:, :]).then_inc(gather_out_dve, 1)
            v.wait_ge(gather_ps, 4 * KD)
            v.tensor_scalar(ST[:, :], iota[:, 0:SEQ], 0.0, None, ALU.mult).then_inc(st_ready, 1)
            v.tensor_scalar(y2[:, :, :], iota[:, 0:2 * D].rearrange("p (s d) -> p s d", s=2), 0.0, None,
                            ALU.mult).then_inc(y_lo, 2)
            more = v.value_load(tab[0:1, 0:1], min_val=1, max_val=ITEMS // 2 - 1)

            def build_si(n):
                p = v.value_load(tab[0:1, bass.ds(n + 1, 1)], min_val=0, max_val=SLOTS)
                e = v.value_load(tab[0:1, bass.ds(n + (1 + ITEMS), 1)], min_val=0, max_val=E - 1)
                for t in range(TH):
                    ins = v.tensor_scalar(SI[:, t, :], iota[:, bass.ds(p, PART)], slotm[:, t, bass.ds(e, 1)],
                                          wt[:, t, bass.ds(e, 1)], ALU.is_equal, ALU.mult)
                ins.then_inc(si_ready, 1)

            def lo(i, b, q):
                v.wait_ge(gu_hi, i * 4 + q + 1)
                v.tensor_tensor(w_lo(q), w_raw(b, q), w_hi(q).bitcast(fp32), ALU.subtract).then_inc(gu_lo, 1)

            def input_lo(i):
                p = v.value_load(tab[0:1, bass.ds(i + 1, 1)], min_val=0, max_val=SLOTS)
                v.wait_ge(hT_hi, i + 1)
                v.tensor_tensor(hT2[:, 1], hs[:, :, bass.ds(p, PART)], hT2[:, 0].bitcast(fp32),
                                ALU.subtract).then_inc(hT_lo, 1)

            build_si(0)
            for q in range(4):
                lo(0, 0, q)
            input_lo(0)

            def item(i, b, last):
                nb = 1 - b
                if not last:
                    lo(i + 1, nb, 0)
                v.wait_ge(silu_done, i + 1)
                v.tensor_tensor(act[:, :], sg[:, :], psU[:, F:2 * F], ALU.mult).then_inc(act_ready, 1)
                v.wait_ge(aT_hi, i + 1)
                v.tensor_tensor(aT2[:, 1], psM[:, 0:F].rearrange("p (k n) -> p k n", k=KF), aT2[:, 0].bitcast(fp32),
                                ALU.subtract).then_inc(aT_lo, 1)
                if not last:
                    lo(i + 1, nb, 1)
                v.wait_ge(sit_done, i + 1)
                v.tensor_scalar(ST[:, :], psU[:, 0:SEQ], 0.0, None, ALU.is_gt)
                v.reduce_sum(wcol[:, 0:1], psU[:, 0:SEQ], AX).then_inc(st_ready, 1)
                if not last:
                    input_lo(i + 1)
                    lo(i + 1, nb, 2)
                    build_si(i + 1)
                    lo(i + 1, nb, 3)
                for n in range(2):
                    v.wait_ge(y_hi, i * 2 + n + 1)
                    v.scalar_tensor_tensor(y2[:, 1, n * W:(n + 1) * W], psY[n][:, :], wcol[:, 0:1],
                                           y2[:, 0, n * W:(n + 1) * W].bitcast(fp32), ALU.mult, ALU.subtract).then_inc(y_lo, 1)

            with v.Fori(0, more) as g:
                for b in range(2):
                    item(g * 2 + b, b, False)
            for b in range(2):
                item(more * 2 + b, b, b == 1)
            v.wait_ge(all_done, 1)
            for t in range(TH):
                for n in range(2):
                    link(v.tensor_tensor(iota[:, 0:W], acc[2 * t + n][:, :], gate2[:, n * W:(n + 1) * W], ALU.mult))
                    xo = xs[:, t, n * W:(n + 1) * W]
                    v.tensor_tensor(xo, xo, iota[:, 0:W], ALU.add).then_inc(fin, 1)
                    v.wait_ge(fin, 2 * t + n + 1)

        @block.tensor
        def _(pe):
            mm, tr = nc.tensor.matmul, nc.tensor.transpose

            def arrived(n):
                pe.wait_ge(piece_in[n % NBUF], 16 * (n // NBUF + 1))
                return piece(n)

            pe.wait_ge(cst, 2)
            pe.wait_ge(c_in, 16)
            tr(bank[5][:, 0:KD], crow, ident[0:KD, 0:KD]).then_inc(cT_in, 1)
            def ada(j, b):
                if j < 4 or j % 2 == 0:
                    pe.wait_ge(adac_ready, j + 1 if j < 4 else j // 2 + 3)
                else:
                    pe.wait_ge(adac_pool, (j - 3) // 2)
                mm(b[:, :], ones[:, :], adac[:, j % 2, :], start=True, stop=False)
                q = j // 3
                mm(b[:, :], ones[32 * q:32 * q + 1, :], bada[32 * q:32 * q + 1, j % 3, :], start=False,
                   stop=True).then_inc(ada_done, 1)

            pe.wait_ge(bada_in, 64)
            for j in range(4):
                ada(j, bank[ADA_B[j]])
            pe.wait_ge(row_in, 16 * 8)
            n = TAPS + 3
            for k in range(KC):
                tr(bank[0][:, 64 + n * k:64 + n * (k + 1)], convrow[:, k * PART:(k + 1) * PART], ident[0:n, 0:n])
            tr(bank[0][:, 240:242], qkrow, ident[0:2, 0:2]).then_inc(rowsT, 1)
            pe.wait_ge(sc_ready, 1)
            for i in range(4):
                for kk in range(2):
                    for t in range(TH):
                        if i == 0 and kk == 0:
                            pe.wait_ge(h1_ready, TH)
                            pe.wait_ge(rows_out, 1)
                        k = 2 * i + kk
                        ins = tr(bank[H1T_B[i]][:, kk * SEQ + t * PART:kk * SEQ + (t + 1) * PART],
                                 h1[:, t, k * PART:(k + 1) * PART], ident[:, :])
                ins.then_inc(h1T_ps, 1)
            pe.wait_ge(h1T_ready, 4)
            pe.wait_ge(ada1_out, 4)
            def project_in(u, halves):
                w = piece(INP + u // 2 if u < 10 else GATEP + 3 * ((u - 10) // 2))
                b = bank[UNIT_B[u % 4] if u < 10 else M_B[u % 2]]
                for kk in halves:
                    m = 2 * (u % 2) + kk
                    for k in range(KD):
                        ins = mm(b[:, kk * SEQ:(kk + 1) * SEQ], w[:, k, m * PART:(m + 1) * PART],
                                 h1T[:, k, :], start=(k == 0), stop=(k == KD - 1))
                if kk == 1:
                    ins.then_inc(unit_done, 1)

            for u, kind in enumerate(UNITS[:10]):
                if u >= 4:
                    p = u - 4
                    if p in (2, 3):
                        pe.wait_ge(unit_out_dve, p - 1)
                    else:
                        pe.wait_ge(unit_out_act, p + 1 if p < 2 else p - 1)
                w = arrived(INP + u // 2)
                if kind == "v":
                    for k in range(KD):
                        ins = mm(bank[UNIT_B[u % 4]][:, :], h1T[:, k, (u % 2) * PART:(u % 2 + 1) * PART], w[:, k, :],
                                 start=(k == 0), stop=(k == KD - 1))
                    ins.then_inc(unit_done, 1)
                else:
                    project_in(u, (0, 1))
                if u == 7:
                    pe.wait_ge(wf_in, 16)
                    for k in range(KD):
                        ins = mm(bank[5][0:HEADS, 0:SEQ], wf[:, k, :], h1T[:, k, :], start=(k == 0), stop=(k == KD - 1))
                    ins.then_inc(f_done, 1)
                if u == 8:
                    pe.wait_ge(unit_out_act, 6)
                    pe.wait_ge(sel_ready, 1)
                    for k in range(2 * KC):
                        ins = mm(bank[6][0:16, 0:SEQ], headsum[:, k, :], qksq[:, k, :], start=(k == 0), stop=(k == 2 * KC - 1))
                    ins.then_inc(qkstat, 1)
            pe.wait_ge(qkrstd, 2)
            pe.wait_ge(unit_out_act, 8)
            for i in range(4):
                for kk in range(2):
                    ins = mm(bank[UNIT_B[i % 4]][:, kk * SEQ:(kk + 1) * SEQ], headrow[:, 2 * i + kk, :], rs16[:, :],
                             start=True, stop=True)
                ins.then_inc(qkb_done, 1)

            def scores(h):
                b, base, j = bank[S_B[h % 2]], 64 * (h % 2), h // 2
                if h >= 2:
                    pe.wait_ge(exp_done, h - 1)
                for q, o, keys in ((0, 0, PART), (1, PART, SEQ)):
                    qs = slice(q * PART, (q + 1) * PART)
                    mm(b[:, o:o + keys], qk[base:base + HD, j, qs], qk[base:base + HD, KC + j, 0:keys], start=True, stop=False)
                    mm(b[:, o:o + keys], AU[base:base + 40, j, qs], BU[base:base + 40, j, 0:keys], start=False, stop=False)
                    ins = mm(b[:, o:o + keys], ident[:, :], causal[:, 2 * PART - keys:], start=False, stop=True)
                ins.then_inc(s_done, 1)

            def transposes(h):
                pe.wait_ge(p_ready, h + 1)
                if h >= 2:
                    pe.wait_ge(pT_out, h - 1)
                for i in range(3):
                    o = (0, 1, 2)[i] * PART
                    ins = tr(bank[PT_B[h % 2]][:, o:o + PART], prob[:, h % 2, o:o + PART], ident[:, :])
                ins.then_inc(pT_done, 1)

            def values(h):
                base, j = 64 * (h % 2), h // 2
                pe.wait_ge(pT_out, h + 1)
                if h % 2 == 0 and h >= 2:
                    pe.wait_ge(o_out, j)
                b = bank[O_B]
                mm(b[base:base + HD, 0:PART], v_sb[:, 0, h * HD:(h + 1) * HD], probT[:, h % 2, 0:PART], start=True, stop=True)
                mm(b[base:base + HD, PART:SEQ], v_sb[:, 0, h * HD:(h + 1) * HD], probT[:, h % 2, PART:SEQ], start=True, stop=False)
                mm(b[base:base + HD, PART:SEQ], v_sb[:, 1, h * HD:(h + 1) * HD], probT[:, h % 2, SEQ:3 * PART],
                   start=False, stop=True).then_inc(o_done, 1)

            pe.wait_ge(qk_ready, 4)
            pe.wait_ge(aug_ready, 1)
            scores(0)
            for h in range(HEADS):
                if h + 1 < HEADS:
                    scores(h + 1)
                arrived(GATEP + 3 * (h // 2))
                if h >= 2:
                    pe.wait_ge(unit_out_act, 8 + h - 1)
                project_in(10 + h, (0,))
                transposes(h)
                project_in(10 + h, (1,))
                values(h)
                if h >= 1:
                    pe.wait_ge(ada2_out, h)
                ada(4 + h, bank[ADA2_B])
            pe.wait_ge(conv_step, TAPS * KC)
            pe.wait_ge(ada2_out, 8)
            pe.wait_ge(unit_out_act, 16)
            for i in range(2):
                for kk in range(2):
                    ins = mm(bank[6 + i][:, kk * SEQ:(kk + 1) * SEQ], blk[:, :], cacc[:, 2 * i + kk, :], start=True, stop=True)
                ins.then_inc(mean_done, 1)
            pe.wait_ge(csq_ready, 1)
            pe.wait_ge(exp_done, HEADS)
            for k in range(KC):
                ins = mm(bank[0][0:8, 0:SEQ], headsum[:, k, 0:8], sqb[:, k, :], start=(k == 0), stop=(k == KC - 1))
            ins.then_inc(var_done, 1)
            w = arrived(COUT)
            wa = arrived(AOUT)
            pe.wait_ge(o_out, 4)
            pe.wait_ge(dmu_ready, 2)

            def project(w, src, done, out_sem):
                for i in range(4):
                    if out_sem is not None:
                        pe.wait_ge(out_sem, i + 1)
                    for kk in range(2):
                        m = 2 * i + kk
                        for k in range(KC):
                            ins = mm(bank[3 + i][:, kk * SEQ:(kk + 1) * SEQ], w[:, k, m * PART:(m + 1) * PART],
                                     src[:, k, :], start=(k == 0), stop=(k == KC - 1))
                    ins.then_inc(done, 1)

            project(wa, oT, ya_done, None)
            pe.wait_ge(crstd, 3)
            for i in range(2):
                for kk in range(2):
                    ins = mm(bank[1 + i][:, kk * SEQ:(kk + 1) * SEQ], headrow[0:8, 2 * i + kk, :], rs16[0:8, :], start=True, stop=True)
                ins.then_inc(cb_done, 1)
            pe.wait_ge(cT_ready, KC)
            project(w, cacc, yc_done, ya_out)
            pe.wait_ge(merged, 4)
            for t in range(TH):
                for n in range(2):
                    w = arrived(WOUT + n)
                    for k in range(KD):
                        ins = mm(bank[2 * t + n][:, :], gates[:, k, t * PART:(t + 1) * PART], w[:, k, :],
                                 start=(k == 0), stop=(k == KD - 1))
                    ins.then_inc(mo_done, 1)
            pe.wait_ge(h2_ready, TH)
            for i in range(4):
                for kk in range(2):
                    for t in range(TH):
                        k = 2 * i + kk
                        ins = tr(bank[i][:, kk * SEQ + t * PART:kk * SEQ + (t + 1) * PART],
                                 h2[:, t, k * PART:(k + 1) * PART], ident[:, :])
                ins.then_inc(h2T_ps, 1)
            pe.wait_ge(h2T_ready, 4)
            pe.wait_ge(rw_in, 16)
            for t in range(TH):
                for k in range(KD):
                    ins = mm(bank[0][:, t * E:(t + 1) * E], h2T[:, k, t * PART:(t + 1) * PART], router[:, k, :],
                             start=(k == 0), stop=(k == KD - 1))
            ins.then_inc(logit_done, 1)
            w = arrived(SHGU)
            for m in range(2 * KF):
                for k in range(KD):
                    ins = mm(bank[1 + m // 2][:, (m % 2) * SEQ:(m % 2 + 1) * SEQ], w[:, k, m * PART:(m + 1) * PART],
                             h2T[:, k, :], start=(k == 0), stop=(k == KD - 1))
                if m % 2 == 1:
                    ins.then_inc(sgu_done, 1)
            pe.wait_ge(sel_out, 1)
            sel = r["sel"]
            for t in range(TH):
                mm(bank[0][:, 128:128 + E], ones[:, :], sel[:, t, :], start=(t == 0), stop=(t == TH - 1))
            for t in range(TH):
                for s in range(t):
                    mm(bank[0][:, 256 + t * E:256 + (t + 1) * E], ones[:, :], sel[:, s, :], start=(s == 0), stop=False)
                mm(bank[0][:, 256 + t * E:256 + (t + 1) * E], before[:, :], sel[:, t, :], start=(t == 0), stop=True)
            for t in range(TH):
                ins = mm(bank[0][0:E, 448:449], sel[:, t, :], ones[:, 0:1], start=(t == 0), stop=(t == TH - 1))
            ins.then_inc(rank_done, 1)
            pe.wait_ge(slotT_out, 1)
            for t in range(TH):
                ins = tr(bank[3][0:E, t * PART:(t + 1) * PART], slotm[:, t, :], ident[:, :])
            ins.then_inc(slotT_ps, 1)
            pe.wait_ge(ecol_out, 1)
            mm(bank[3][0:E, 256:258], before[0:E, 0:E], ecol, start=True, stop=True).then_inc(ecum_done, 1)
            pe.wait_ge(tabs_ps_in, 1)
            mm(bank[3][0:1, 0:ITEMS], ones[0:E, 0:1], jt[:, 2, :], start=True, stop=True)
            mm(bank[3][0:1, ITEMS:2 * ITEMS], enum[:, :], jt[:, 1, :], start=True, stop=True).then_inc(tabs_ps, 1)
            w = arrived(SHD)
            pe.wait_ge(shT_ready, 1)
            for t in range(TH):
                for n in range(2):
                    for k in range(KF):
                        ins = mm(acc[2 * t + n][:, :], shT[:, k, t * PART:(t + 1) * PART], w[:, k, n * W:(n + 1) * W],
                                 start=(k == 0), stop=False)
            ins.then_inc(shared_done, 1)

            pe.wait_ge(E_ready, 1)
            pe.wait_ge(tabs_ready, 1)

            def select(q):
                for t in range(TH):
                    if q >= 1:
                        pe.wait_ge(SS_ready, 2 * (q - 1) + t + 1)
                    mm(bank[2 + t][:, :], slotT[:, t * PART:(t + 1) * PART], Emat[:, q * W:(q + 1) * W],
                       start=True, stop=True).then_inc(m1_done, 1)

            select(0)
            for q in range(4):
                if q < 3:
                    select(q + 1)
                pe.wait_ge(SS_ready, 2 * q + 2)
                if q == 0:
                    pe.wait_ge(h2r_lo, 1)
                for k in range(KD):
                    i = q * KD + k
                    if i >= 2:
                        pe.wait_ge((gather_out_act, gather_out_dve)[i % 2], i // 2)
                    for s in range(2):
                        for t in range(TH):
                            ins = mm(bank[i % 2][:, :], h2r[:, s, t, k * PART:(k + 1) * PART], SS[:, q % 2, t, :],
                                     start=(s == t == 0), stop=(s == 1 and t == TH - 1))
                    ins.then_inc(gather_ps, 1)
            pe.wait_ge(gather_out_act, 2 * KD)
            pe.wait_ge(gather_out_dve, 2 * KD)

            def three(out, a_hi, a_lo, b_hi, b_lo, start, stop):
                mm(out, a_hi, b_hi, start=start, stop=False)
                mm(out, a_hi, b_lo, start=False, stop=False)
                return mm(out, a_lo, b_hi, start=False, stop=stop)

            def scatter(t, stop=False):
                for n in range(2):
                    for s in range(2):
                        ins = mm(acc[2 * t + n][:, :], ST[:, t * PART:(t + 1) * PART], y2[:, s, n * W:(n + 1) * W],
                                 start=False, stop=(stop and s == 1))
                return ins

            def item(i):
                pe.wait_ge(hT_lo, i + 1)
                pe.wait_ge(st_ready, i + 1)
                for q in range(4):
                    pe.wait_ge(gu_lo, i * 4 + q + 1)
                    wh, wl = (w(q).rearrange("p (k n) -> p k n", n=W) for w in (w_hi, w_lo))
                    for kk in range(2):
                        k = 2 * q + kk
                        ins = three(psU[:, :], hT2[:, 0, k], hT2[:, 1, k], wh[:, kk], wl[:, kk], k == 0, k == KD - 1)
                    ins.then_inc(gu_used, 1)
                pe.wait_ge(y_lo, i * 2 + 2)
                scatter(0)
                pe.wait_ge(act_ready, i + 1)
                for k in range(KF):
                    ins = tr(psM[:, k * PART:(k + 1) * PART], act[:, k * PART:(k + 1) * PART], ident[:, :])
                ins.then_inc(t_done, 1)
                scatter(1)
                pe.wait_ge(si_ready, i + 1)
                for t in range(TH):
                    ins = tr(psU[:, t * PART:(t + 1) * PART], SI[:, t, :], ident[:, :])
                ins.then_inc(sit_done, 1)
                pe.wait_ge(aT_lo, i + 1)
                pe.wait_ge(dn_lo, i + 1)
                wh, wl = (w(4).rearrange("p (k n) -> p k n", k=KF) for w in (w_hi, w_lo))
                for n in range(2):
                    cols = slice(n * W, (n + 1) * W)
                    for k in range(KF):
                        ins = three(psY[n][:, :], aT2[:, 0, k], aT2[:, 1, k], wh[:, k, cols], wl[:, k, cols],
                                    k == 0, k == KF - 1)
                ins.then_inc(down_done, 1)

            more = pe.value_load(tab[0:1, 0:1], min_val=1, max_val=ITEMS // 2 - 1)
            with pe.Fori(0, more + 1) as g:
                for b in range(2):
                    item(g * 2 + b)
            pe.wait_ge(st_ready, more * 2 + 3)
            pe.wait_ge(y_lo, more * 4 + 6)
            for t in range(TH):
                ins = scatter(t, stop=True)
            ins.then_inc(all_done, 1)


_INS = ["x", "c", "w_ada", "b_ada", "norm1_g", "w_in", "w_dw", "b_dw", "conv_gn_g", "conv_gn_b", "w_conv_out",
        "q_norm_g", "k_norm_g", "b_forget", "w_attn_out", "w_out", "norm2_g", "w_router", "router_bias",
        "w_experts_gate_up", "w_experts_down", "w_shared_gate_up", "w_shared_down"]


def kernel(**inputs):
    import numpy as _np
    import concourse.bacc as _bacc
    from concourse import mybir as _mybir
    from concourse.bass_utils import run_bass_kernel_spmd as _run

    nc = _bacc.Bacc("TRN2", target_bir_lowering=False, num_devices=1)
    arrays, args = {}, []
    for name in _INS:
        a = _np.ascontiguousarray(inputs[name])
        arrays[f"in_{name}_dram"] = a
        args.append(nc.dram_tensor(f"in_{name}_dram", a.shape, _mybir.dt.from_np(a.dtype), kind="ExternalInput").ap())
    out = nc.dram_tensor("out_dram", inputs["x"].shape, _mybir.dt.float32, kind="ExternalOutput").ap()
    hybrid_conformer_fox_moe_block(nc, *args, out)
    return _run(nc, [arrays], core_ids=[0]).results[0]["out_dram"]
```

```python
import concourse.bass as bass
from concourse import mybir
from contextlib import ExitStack


def hybrid_conformer_fox_moe_block(
    nc, x, c, w_ada, b_ada, norm1_g, w_in, w_dw, b_dw, conv_gn_g, conv_gn_b, w_conv_out, q_norm_g,
    k_norm_g, b_forget, w_attn_out, w_out, norm2_g, w_router, router_bias, w_experts_gate_up,
    w_experts_down, w_shared_gate_up, w_shared_down, out,
):
    fp32, fp32r, i32 = mybir.dt.float32, mybir.dt.float32r, mybir.dt.int32
    ALU = mybir.AluOpType
    ACT = mybir.ActivationFunctionType
    AX = mybir.AxisListType.X

    PART = 128
    SEQ, D = x.shape[1], x.shape[2]
    TH = SEQ // PART
    KD = D // PART
    TAPS, CONV = w_dw.shape[1], w_dw.shape[2]
    KC = CONV // PART
    HEADS, HD = b_forget.shape[1], q_norm_g.shape[1]
    E, F = w_experts_gate_up.shape[1], w_experts_down.shape[2]
    KF = F // PART
    ATT = HEADS * HD
    OFF_Q = 2 * CONV
    OFF_F = OFF_Q + 3 * ATT
    OFF_G = OFF_F + HEADS
    GROUPS, EPG, TOPG, TOPK = 8, 8, 4, 8
    ROUTED_SCALE = 2.5
    EPS = 1e-6
    W = 512
    SLOTS = SEQ * TOPK
    PADDED = SLOTS + PART
    ITEMS = E + SLOTS // PART
    GU, DN = KD * 2 * F, KF * D
    SLOTW = GU + DN
    QW = GU // 4
    NBUF = 5
    BUFW = KD * W
    NEG = -1.0e30
    LOWEST = -87.0

    ctx = ExitStack()
    with ctx:
        def sb(name, shape, dt=fp32):
            return ctx.enter_context(nc.sbuf_tensor(name, shape, dt))

        def sem(name):
            return ctx.enter_context(nc.semaphore(name))

        with nc.sbuf_tensor("ring", [PART, 4 * SLOTW], fp32) as ring:
            pass
        raw = sb("raw", [PART, 2 * SLOTW])
        split = sb("split", [PART, 2 * SLOTW], fp32r)
        with ExitStack() as early:
            def sbe(name, shape):
                return early.enter_context(nc.sbuf_tensor(name, shape, fp32))

            misc = sbe("misc", [PART, 2 * D])
            blk = sbe("blk", [PART, PART])
            causal = sbe("causal", [PART, 2 * PART])
            headsum = sbe("headsum", [PART, 8, 16])
            headrow = sbe("headrow", [16, 8, PART])
            wf = sbe("wf", [PART, KD, HEADS])
            convc = sbe("convc", [PART, KC, TAPS + 3])
            qkg = sbe("qkg", [PART, 2])
            bf = sbe("bf", [HEADS, 1])
            sc = sbe("sc", [PART, KD])
            before = sbe("before", [PART, PART])
            ones = sbe("ones", [PART, PART])
            lower8 = sbe("lower8", [PART, GROUPS, GROUPS])
            enum = sbe("enum", [E, 1])
        y2 = sb("y2", [PART, 2, D], fp32r)
        hT2 = sb("hT2", [PART, 2, KD, PART], fp32r)
        aT2 = sb("aT2", [PART, 2, KF, PART], fp32r)
        work = sb("work", [PART, KD * PADDED])
        xs = sb("xs", [PART, TH, D])
        gate2 = sb("gate2", [PART, D])
        SI = sb("SI", [PART, TH, PART])
        ST = sb("ST", [PART, SEQ], fp32r)
        iota = sb("iota", [PART, PADDED])
        sg = sb("sg", [PART, F])
        ident = sb("ident", [PART, PART])
        slotm = sb("slotm", [PART, TH, E])
        wt = sb("wt", [PART, TH, E])
        tab = sb("tab", [1, 1 + 2 * ITEMS], i32)
        st2 = sb("st2", [PART, 16])
        wcol = sb("wcol", [PART, 1])

        def view(t, at, n, k=None):
            v = t[:, at:at + n]
            return v if k is None else v.rearrange("p (k n) -> p k n", k=k)

        TAIL = NBUF * BUFW
        IN_SPLIT = TAIL - 2 * SLOTW
        h1T = view(work, 0, 2048, KD)
        gates = view(work, 2048, 4096, 2 * KD)
        upad = view(work, 6144, KC * 288, KC)
        gsig = view(work, 7296, 1024, KC)
        cacc = view(work, 8320, 1024, KC)
        sqb = view(work, 9344, 1024, KC)
        qk = view(work, 10368, 2048, 2 * KC)
        qksq = view(work, 12416, 2048, 2 * KC)
        v_sb = view(work, 14464, 1024, TH)
        oT = view(work, 15488, 1024, KC)
        router = view(work, 16512, KD * E, KD)
        small = view(work, 17024, 384)
        convrow = work[0:TAPS + 3, 0:CONV]
        qkrow = work[0:2, 512:640]
        crow = work[0:KD, 640:768]
        shift1, G1 = view(ring, TAIL, D), view(ring, TAIL + D, D)
        h1 = view(ring, TAIL + 2 * D, 2 * D, TH)
        gate1, shift2 = view(ring, TAIL, D), view(ring, TAIL + D, D)
        h2 = view(ring, TAIL + 2 * D, 2 * D, TH)
        G2, n2g = view(ring, TAIL + 3 * D, D), view(work, D, D)
        bada = view(iota, 0, 1536, 3)
        adac = view(work, 7296, 2 * W, 2)
        AU = view(misc, 0, 1024, KC)
        BU = view(misc, 1024, 1024, KC)
        zf = work[0:HEADS, 9344:9600]
        za = work[0:HEADS, 9600:9856]
        zl = work[0:HEADS, 9856:10112]
        cum = small[0:HEADS, 0:256]
        rs16 = sg[0:16, :]
        cdif = view(work, 10368, 1024, KC)
        prob = view(work, 12416, 768, 2)
        probT = view(work, 13184, 768, 2)
        h2T = view(work, 10368, 2048, KD)
        sq2 = view(work, 0, 2 * D, TH)
        shT = view(work, 2048, 512, 2)
        shg = view(work, 2560, 512, 2)
        r = {n: work[:, 3072 + 128 * i:3200 + 128 * i].rearrange("p (t e) -> p t e", t=TH)
             for i, n in enumerate(("z", "s", "b", "e", "pre", "m", "rep", "sel"))}
        rbias = work[:, 4096:4096 + E]
        top2 = work[:, 4160:4288].rearrange("p (t g e) -> p t g e", t=TH, g=GROUPS)
        gs = work[:, 4288:4304].rearrange("p (t g) -> p t g", t=TH)
        grank = work[:, 4304:4320].rearrange("p (t g) -> p t g", t=TH)
        gmask = work[:, 4320:4336].rearrange("p (t g) -> p t g", t=TH)
        top8 = work[:, 4336:4352].rearrange("p (t e) -> p t e", t=TH)
        cmp1 = work[:, 4352:4480].rearrange("p (t g h) -> p t g h", t=TH, g=GROUPS)
        cmp2 = work[:, 4480:4608].rearrange("p (t g h) -> p t g h", t=TH, g=GROUPS)
        cnt = work[:, 4608:4672]
        incl = work[:, 4672:4736]
        first = work[:, 4736:4800]
        nit = work[:, 4800:4864]
        cumi = work[:, 4864:4930]
        ecol = work[0:E, 4930:4932]
        ecum = st2[0:E, 10:12]
        eend = st2[0:E, 12:14]
        ecol2 = work[0:E, 4934:4936]
        slotT = ST[0:E, :]
        jt = work[0:E, 5200:5200 + 5 * ITEMS].rearrange("p (k j) -> p k j", k=5)
        Emat = split[0:E, IN_SPLIT:IN_SPLIT + SLOTS]
        h2r = [y2[:, :, :],
               split[:, IN_SPLIT + 2 * D:].rearrange("p (t d) -> p t d", t=TH)]
        SS = hT2[:, :, :, :].rearrange("p b k n -> p b (k n)").rearrange("p b (t s) -> p b t s", t=TH)
        hs = work[:, :].rearrange("p (k s) -> p k s", k=KD)
        act = sg

        bank = [ctx.enter_context(nc.psum_tensor(f"bank{i}", [PART, W], fp32)) for i in range(8)]
        acc = bank[4:8]
        psU, psY, psM = bank[0], bank[1:3], bank[3]

        def cols(w, n):
            return w[0, :, n:n + W].rearrange("(k p) n -> p k n", p=PART)

        pieces = [cols(w_ada, W * j) for j in range(4)]
        pieces += [cols(w_in, n) for n in (CONV, 0, OFF_Q, OFF_Q + ATT, OFF_Q + 2 * ATT)]
        for j in range(4):
            pieces += [cols(w_in, OFF_G + W * j), cols(w_ada, W * (4 + 2 * j)), cols(w_ada, W * (5 + 2 * j))]
        pieces += [w_attn_out[0].rearrange("(k p) n -> p k n", p=PART),
                   w_conv_out[0].rearrange("(k p) n -> p k n", p=PART)]
        pieces += [cols(w_out, 0), cols(w_out, W), cols(w_shared_gate_up, 0),
                   w_shared_down[0].rearrange("(k p) n -> p k n", p=PART)]
        (ADA1, INP, GATEP, AOUT, COUT, WOUT, SHGU, SHD) = (0, 4, 9, 21, 22, 23, 25, 26)
        ADA2 = [GATEP + 3 * (j // 2) + 1 + j % 2 for j in range(8)]

        def used_by():
            users = [(adac_ready, j + 1) for j in range(4)]
            users += [(unit_done, 2 * j + 2) for j in range(5)]
            for j in range(4):
                users += [(unit_done, 2 * (5 + j) + 2), (adac_ready, 5 + j), (adac_pool, j + 1)]
            return users + [(ya_done, 4), (yc_done, 4), (mo_done, 3), (mo_done, 4), (sgu_done, 2), (shared_done, 1)]

        def piece(n):
            k, m = pieces[n].shape[1:]
            return view(ring, (n % NBUF) * BUFW, k * m, k)

        def part(q):
            return (q * QW, QW) if q < 4 else (GU + (q - 4) * D, D)

        def w_raw(b, q):
            return view(raw, b * SLOTW + part(q)[0], part(q)[1])

        def w_hi(q):
            return view(split, part(q)[0] if q < 4 else GU + part(q)[0], part(q)[1])

        def w_lo(q):
            return view(split, GU + part(q)[0] if q < 4 else GU + DN + part(q)[0], part(q)[1])

        piece_in = [sem(f"piece_in{i}") for i in range(NBUF)]
        gu_in = [sem(f"gu_in{i}") for i in range(2)]
        dn_in = [sem(f"dn_in{i}") for i in range(2)]
        x_in, row_in, n1_in, n2_in, bada_in, wf_in, bf_in, rw_in, rb_in, out_done = map(sem, (
            "x_in", "row_in", "n1_in", "n2_in", "bada_in", "wf_in", "bf_in", "rw_in", "rb_in", "out_done"))
        upad_zero, gates_ready = sem("upad_zero"), sem("gates_ready")
        cst, pool_chain, sel_ready, aug_zero, iota_ready, pad_ready = map(sem, (
            "cst", "pool_chain", "sel_ready", "aug_zero", "iota_ready", "pad_ready"))
        dve_chain, act_chain = sem("dve_chain"), sem("act_chain")
        rowsT, rows_out, sc_ready, adac_ready, adac_pool, ada_scaled, cT_in, c_in = map(sem, (
            "rowsT", "rows_out", "sc_ready", "adac_ready", "adac_pool", "ada_scaled", "cT_in", "c_in"))
        ada_done, ada1_out, ada2_out = map(sem, ("ada_done", "ada1_out", "ada2_out"))
        ss_ready, sqrt_in, sqrt_out, h1_ready, h1T_ps, h1T_ready = map(sem, (
            "ss_ready", "sqrt_in", "sqrt_out", "h1_ready", "h1T_ps", "h1T_ready"))
        unit_done, unit_out_dve, unit_out_act, f_done = map(sem, (
            "unit_done", "unit_out_dve", "unit_out_act", "f_done"))
        qkstat, qkrstd, qkb_done, qk_ready = map(sem, (
            "qkstat", "qkrstd", "qkb_done", "qk_ready"))
        gsig_ready, u_ready, conv_step, f_step = map(sem, ("gsig_ready", "u_ready", "conv_step", "f_step"))
        zf_ready, lf_ready, aug_ready = map(sem, ("zf_ready", "lf_ready", "aug_ready"))
        s_done, max_done, exp_done, p_ready, pT_done, pT_out, o_done, o_out = map(sem, (
            "s_done", "max_done", "exp_done", "p_ready", "pT_done", "pT_out", "o_done", "o_out"))
        mean_done, dmu_ready, csq_ready, var_done, crstd, cb_done, yn_ready, cT_ready = map(sem, (
            "mean_done", "dmu_ready", "csq_ready", "var_done", "crstd", "cb_done", "yn_ready", "cT_ready"))
        yc_done, yc_out, ya_done, ya_out, merged, mo_done, x1_ready = map(sem, (
            "yc_done", "yc_out", "ya_done", "ya_out", "merged", "mo_done", "x1_ready"))
        h2_ready, h2T_ps, h2T_ready, logit_done, sgu_done, shg_ready, shT_ready = map(sem, (
            "h2_ready", "h2T_ps", "h2T_ready", "logit_done", "sgu_done", "shg_ready", "shT_ready"))
        z_ready, ez_ready, sel_out, rank_done, ecol_out, ecum_done, tabs_ps_in, tabs_ps, slotT_ps, slotT_out = map(sem, (
            "z_ready", "ez_ready", "sel_out", "rank_done", "ecol_out", "ecum_done", "tabs_ps_in", "tabs_ps",
            "slotT_ps", "slotT_out"))
        E_ready, m1_done, SS_ready, gather_ps, gather_out_act, gather_out_dve, tabs_ready = map(sem, (
            "E_ready", "m1_done", "SS_ready", "gather_ps", "gather_out_act", "gather_out_dve", "tabs_ready"))
        gu_hi, gu_lo, dn_hi, dn_lo, gu_used, h2r_hi, h2r_lo = map(sem, (
            "gu_hi", "gu_lo", "dn_hi", "dn_lo", "gu_used", "h2r_hi", "h2r_lo"))
        hT_hi, hT_lo, silu_done, act_ready, t_done, aT_hi, aT_lo, si_ready, sit_done, st_ready = map(sem, (
            "hT_hi", "hT_lo", "silu_done", "act_ready", "t_done", "aT_hi", "aT_lo", "si_ready", "sit_done", "st_ready"))
        down_done, y_hi, y_lo, shared_done, all_done, fin = map(sem, (
            "down_done", "y_hi", "y_lo", "shared_done", "all_done", "fin"))

        ADA_B = [1, 2, 3, 4]
        H1T_B = [5, 6, 7, 0]
        UNIT_B = [1, 2, 3, 4]
        UNITS = ["g", "g", "a", "a", "q", "q", "k", "k", "v", "v"] + ["m"] * 8
        S_B, PT_B, O_B, ADA2_B, M_B = [0, 1], [2, 3], 4, 5, [6, 7]

        block = ctx.enter_context(nc.Block())

        @block.sync
        def _(sp):
            sp.dma_start(crow, c[0].rearrange("(k p) -> k p", p=PART)).then_inc(c_in, 16)
            sp.dma_start(bada[0:PART:32, :, :], b_ada[0].rearrange("(q k n) -> q k n", q=4, k=3)).then_inc(bada_in, 16)
            users = used_by()
            for n in range(len(pieces)):
                if n >= NBUF:
                    sp.wait_ge(*users[n - NBUF])
                    sp.wait_ge(piece_in[n % NBUF], 16 * (n // NBUF))
                sp.dma_start(piece(n), pieces[n]).then_inc(piece_in[n % NBUF], 16)
                if n == 0:
                    sp.dma_start(xs[:, :, :], x[0].rearrange("(t p) d -> p t d", p=PART)).then_inc(x_in, 16)

            def load_item(i, b, wait=False):
                e = sp.value_load(tab[0:1, bass.ds(i + (1 + ITEMS), 1)], min_val=0, max_val=E - 1)
                if wait:
                    sp.wait_ge(gu_lo, i * 4 - 4)
                sp.dma_start(view(raw, b * SLOTW, GU, KD), w_experts_gate_up[0, bass.ds(e, 1), :, :].rearrange(
                    "o (k p) n -> p (o k) n", p=PART)).then_inc(gu_in[b], 16)
                if wait:
                    sp.wait_ge(dn_lo, i * 2 - 2)
                sp.dma_start(view(raw, b * SLOTW + GU, DN, KF), w_experts_down[0, bass.ds(e, 1), :, :].rearrange(
                    "o (k p) n -> p (o k) n", p=PART)).then_inc(dn_in[b], 16)

            sp.wait_ge(*users[COUT])
            sp.wait_ge(*users[SHGU])
            sp.wait_ge(*users[SHD])
            sp.wait_ge(tabs_ready, 1)
            more = sp.value_load(tab[0:1, 0:1], min_val=1, max_val=ITEMS // 2 - 1)
            for b in range(2):
                load_item(b, b)
            with sp.Fori(1, more + 1) as g:
                for b in range(2):
                    load_item(g * 2 + b, b, wait=True)
            for t in range(TH):
                for n in range(2):
                    sp.wait_ge(fin, t * 2 + n + 1)
                    sp.dma_start(out[0, t * PART:(t + 1) * PART, n * W:(n + 1) * W],
                                 xs[:, t, n * W:(n + 1) * W]).then_inc(out_done, 16)
            sp.wait_ge(out_done, 16 * TH * 2)

        @block.gpsimd
        def _(pool):
            chain = [0]

            def link(ins):
                chain[0] += 1
                ins.then_inc(pool_chain, 1)
                pool.wait_ge(pool_chain, chain[0])

            link(pool.memset(ident[:, :], 0.0))
            pool.affine_select(out=ident[:, :], in_=ident[:, :], compare_op=ALU.not_equal, fill=1.0, base=0,
                               pattern=[[-1, PART]], channel_multiplier=1).then_inc(cst, 1)
            pool.memset(ones[:, :], 1.0).then_inc(cst, 1)
            link(pool.memset(headsum[:, :, :], 0.0))
            link(pool.memset(headrow[:, :, :], 0.0))
            for half in range(2):
                hr = headrow[:, :, half * HD:(half + 1) * HD]
                link(pool.affine_select(out=headsum[half * HD:(half + 1) * HD, :, :],
                                        in_=headsum[half * HD:(half + 1) * HD, :, :],
                                        compare_op=ALU.not_equal, fill=1.0 / HD, base=half,
                                        pattern=[[2, 8], [-1, 16]], channel_multiplier=0))
                link(pool.affine_select(out=hr, in_=hr, compare_op=ALU.not_equal, fill=1.0, base=-half,
                                        pattern=[[-2, 8], [0, HD]], channel_multiplier=1))
            link(pool.memset(blk[:, :], 0.0))
            for half in range(2):
                link(pool.memset(blk[half * HD:(half + 1) * HD, half * HD:(half + 1) * HD], 1.0 / HD))
            pool.memset(upad[:, :, 0:TAPS - 1], 0.0).then_inc(upad_zero, 1)
            link(pool.memset(causal[:, :], 0.0))
            link(pool.affine_select(out=causal[:, :], in_=causal[:, :], compare_op=ALU.is_ge, fill=NEG, base=PART,
                                    pattern=[[-1, 2 * PART]], channel_multiplier=1))
            link(pool.memset(before[:, :], 0.0))
            link(pool.affine_select(out=before[:, :], in_=before[:, :], compare_op=ALU.is_ge, fill=1.0, base=0,
                                    pattern=[[-1, PART]], channel_multiplier=1))
            link(pool.iota(enum[:, :], pattern=[[0, 1]], base=0, channel_multiplier=1,
                           allow_small_or_imprecise_dtypes=True))
            link(pool.memset(lower8[:, :, :], 0.0))
            pool.affine_select(out=lower8[:, :, :], in_=lower8[:, :, :], compare_op=ALU.is_ge, fill=1.0, base=0,
                               pattern=[[-1, GROUPS], [1, GROUPS]], channel_multiplier=0).then_inc(sel_ready, 1)
            pool.wait_ge(sel_ready, 1)
            link(pool.memset(misc[:, :], 0.0))
            for t, rows in ((AU, 32), (BU, 0)):
                for par in range(2):
                    a = t[64 * par + rows:64 * par + rows + HEADS, :, :]
                    pool.affine_select(out=a, in_=a, compare_op=ALU.not_equal, fill=1.0, base=-par,
                                       pattern=[[-2, KC], [0, SEQ]], channel_multiplier=1).then_inc(aug_zero, 1)
                    pool.wait_ge(aug_zero, (1 if t is BU else 0) * 2 + par + 1)
            pool.wait_ge(unit_out_dve, 2)
            pool.wait_ge(bada_in, 16)
            for j in range(1, 8, 2):
                w = piece(ADA2[j])
                pool.wait_ge(ada_scaled, j // 2 + 1)
                link(pool.tensor_tensor(w[:, 0:4, :], w[:, 0:4, :], w[:, 4:8, :], ALU.add))
                link(pool.tensor_tensor(w[:, 0:2, :], w[:, 0:2, :], w[:, 2:4, :], ALU.add))
                pool.wait_ge(ada_done, 4 + j - 1)
                link(pool.tensor_tensor(adac[:, 1, :], w[:, 0, :], w[:, 1, :], ALU.add))
                row = slice(32 * ((4 + j) // 3), 32 * ((4 + j) // 3) + 1)
                pool.tensor_tensor(adac[row, 1, :], adac[row, 1, :], bada[row, (4 + j) % 3, :], ALU.add).then_inc(adac_pool, 1)
                pool.wait_ge(adac_pool, j // 2 + 1)
            pool.wait_ge(ada_done, 12)
            pool.iota(iota[:, :], pattern=[[1, PADDED]], base=0, channel_multiplier=0,
                      allow_small_or_imprecise_dtypes=True).then_inc(iota_ready, 1)
            pool.wait_ge(iota_ready, 1)
            pool.wait_ge(SS_ready, 8)
            pool.wait_ge(tabs_ready, 1)
            pool.memset(hs[:, :, SLOTS:PADDED], 0.0).then_inc(pad_ready, 1)
            more = pool.value_load(tab[0:1, 0:1], min_val=1, max_val=ITEMS // 2 - 1)
            with pool.Fori(0, more + 1) as g:
                for b in range(2):
                    for k in range(KF):
                        pool.wait_ge(dn_hi, g * 4 + b * 2 + k + 1)
                        pool.tensor_tensor(w_lo(4 + k), w_raw(b, 4 + k), w_hi(4 + k).bitcast(fp32), ALU.subtract).then_inc(dn_lo, 1)

        @block.scalar
        def _(a):
            chain = [0]

            def link(ins):
                chain[0] += 1
                ins.then_inc(act_chain, 1)
                a.wait_ge(act_chain, chain[0])

            a.dma_start(G1, norm1_g.broadcast_to([PART, D])).then_inc(n1_in, 16)
            a.wait_ge(cT_in, 1)
            a.activation(sc[:, :], bank[5][:, 0:KD], ACT.Silu).then_inc(sc_ready, 1)
            for row, src in ((0, w_dw[0]), (TAPS, b_dw), (TAPS + 1, conv_gn_g), (TAPS + 2, conv_gn_b)):
                a.dma_start(convrow[row:row + src.shape[0], :], src).then_inc(row_in, 16)
            for i, g in enumerate((q_norm_g, k_norm_g)):
                for half in range(2):
                    a.dma_start(qkrow[i:i + 1, half * HD:(half + 1) * HD], g).then_inc(row_in, 16)
            a.dma_start(bf[:, :], b_forget[0].rearrange("(h o) -> h o", o=1)).then_inc(bf_in, 16)
            with nc.allow_non_contiguous_dma(reason="eight columns of w_in"):
                a.dma_start(wf[:, :, :], w_in[0, :, OFF_F:OFF_F + HEADS].rearrange("(k p) n -> p k n", p=PART)).then_inc(wf_in, 16)
            a.dma_start(router, w_router[0].rearrange("(k p) n -> p k n", p=PART)).then_inc(rw_in, 16)

            a.wait_ge(x_in, 16)
            for t in range(TH):
                a.activation(h1[:, t, :], xs[:, t, :], ACT.Square, accum_out=st2[:, t:t + 1]).then_inc(ss_ready, 1)
            a.wait_ge(sqrt_in, 1)
            a.activation(st2[:, 4:6], st2[:, 2:4], ACT.Sqrt).then_inc(sqrt_out, 1)
            for i in range(4):
                a.wait_ge(h1T_ps, i + 1)
                a.activation(h1T[:, 2 * i:2 * i + 2, :], bank[H1T_B[i]][:, :].rearrange("p (k n) -> p k n", k=2),
                             ACT.Copy).then_inc(h1T_ready, 1)
            for u, kind in enumerate(UNITS[:10]):
                if kind == "a":
                    continue
                a.wait_ge(unit_done, u + 1)
                ps = bank[UNIT_B[u % 4]]
                ps2 = ps[:, :].rearrange("p (k n) -> p k n", k=2)
                if kind == "g":
                    a.wait_ge(ada_done, 4)
                    ins = a.activation(gsig[:, 2 * u:2 * u + 2, :], ps2, ACT.Sigmoid)
                elif kind in "qk":
                    c0 = 2 * (u - 4)
                    a.activation(qk[:, c0:c0 + 2, :], ps2, ACT.Copy)
                    ins = a.activation(qksq[:, c0:c0 + 2, :], ps2, ACT.Square)
                else:
                    ins = a.activation(v_sb[:, u - 8, :], ps[:, :], ACT.Copy)
                ins.then_inc(unit_out_act, 1)
                if u == 7:
                    a.wait_ge(f_done, 1)
                    a.wait_ge(bf_in, 16)
                    a.activation(zf, bank[5][0:HEADS, 0:SEQ], ACT.Identity, bias=bf[:, 0:1]).then_inc(zf_ready, 1)
                    a.wait_ge(zf_ready, 1)
                    link(a.activation(za, zf, ACT.Abs))
                    link(a.activation(za, za, ACT.Exp, scale=-1.0))
                    a.activation(zl, za, ACT.Ln, bias=1.0).then_inc(lf_ready, 1)
                    a.wait_ge(qkstat, 2)
                    a.activation(rs16[:, :], rs16[:, :], ACT.Sqrt).then_inc(qkrstd, 1)
            def ada_out(j):
                dst = (gate1, shift2, G2, gate2[:, :])[j // 2][:, (j % 2) * W:(j % 2) * W + W]
                a.wait_ge(ada_done, 4 + j + 1)
                a.activation(dst, bank[ADA2_B][:, :], ACT.Identity if j // 2 == 2 else ACT.Copy,
                             bias=1.0 if j // 2 == 2 else 0.0).then_inc(ada2_out, 1)

            def gate_out(h):
                a.wait_ge(unit_done, 10 + h + 1)
                a.activation(gates[:, 2 * h:2 * h + 2, :], bank[M_B[h % 2]][:, :].rearrange("p (k n) -> p k n", k=2),
                             ACT.Copy).then_inc(unit_out_act, 1)

            for h in range(HEADS):
                a.wait_ge(max_done, 2 * h + 2)
                if h >= 2:
                    a.wait_ge(pT_done, h - 1)
                ps = bank[S_B[h % 2]]
                a.activation(prob[:, h % 2, 0:PART], ps[:, 0:PART], ACT.Exp, bias=st2[:, 6:7] if h % 2 == 0 else st2[:, 10:11],
                             accum_out=st2[:, 8:9] if h % 2 == 0 else st2[:, 12:13])
                a.activation(prob[:, h % 2, PART:3 * PART], ps[:, PART:3 * PART], ACT.Exp,
                             bias=st2[:, 7:8] if h % 2 == 0 else st2[:, 11:12],
                             accum_out=st2[:, 9:10] if h % 2 == 0 else st2[:, 13:14]).then_inc(exp_done, 1)
                if h >= 1:
                    gate_out(h - 1)
                    ada_out(h - 1)
                if h % 2 == 0:
                    n = ADA2[h + 1]
                    a.wait_ge(piece_in[n % NBUF], 16 * (n // NBUF + 1))
                    for k in range(KD):
                        ins = a.activation(piece(n)[:, k, :], piece(n)[:, k, :], ACT.Copy, scale=sc[:, k:k + 1])
                    ins.then_inc(ada_scaled, 1)
            gate_out(HEADS - 1)
            a.wait_ge(unit_out_act, 16)
            for i in (1, 0):
                a.activation(gates[:, i * KD:(i + 1) * KD, :], gates[:, i * KD:(i + 1) * KD, :], ACT.Sigmoid).then_inc(gates_ready, 1)
            ada_out(HEADS - 1)
            a.dma_start(n2g, norm2_g.broadcast_to([PART, D])).then_inc(n2_in, 16)
            a.wait_ge(dmu_ready, 2)
            a.activation(sqb, cdif, ACT.Square).then_inc(csq_ready, 1)
            a.wait_ge(crstd, 1)
            a.activation(rs16[0:8, :], rs16[0:8, :], ACT.Sqrt).then_inc(crstd, 1)
            for k in range(KC):
                a.wait_ge(yn_ready, k // 2 + 1)
                a.activation(cacc[:, k, :], sqb[:, k, :], ACT.Silu, scale=convc[:, k, TAPS + 1:TAPS + 2],
                             bias=convc[:, k, TAPS + 2:TAPS + 3]).then_inc(cT_ready, 1)
            for t in range(TH):
                a.wait_ge(x1_ready, 2 * t + 2)
                a.activation(sq2[:, t, :], xs[:, t, :], ACT.Square, accum_out=st2[:, t:t + 1]).then_inc(ss_ready, 1)
                a.wait_ge(sqrt_in, 2 + t)
                a.activation(st2[:, 4 + t:5 + t], st2[:, 2 + t:3 + t], ACT.Sqrt).then_inc(sqrt_out, 1)
                for i in range(2):
                    a.wait_ge(h2T_ps, 2 * t + i + 1)
                    a.activation(h2T[:, 4 * i:4 * i + 4, t * PART:(t + 1) * PART],
                                 bank[4 + 2 * t + i][:, :].rearrange("p (k n) -> p k n", k=4), ACT.Copy).then_inc(h2T_ready, 1)
            a.dma_start(rbias, router_bias.broadcast_to([PART, E])).then_inc(rb_in, 16)
            a.wait_ge(z_ready, 1)
            a.activation(r["e"], r["z"], ACT.Exp, scale=-1.0).then_inc(ez_ready, 1)
            a.wait_ge(sgu_done, 1)
            a.activation(shg[:, :, :], bank[1][:, :].rearrange("p (k n) -> p k n", k=2), ACT.Silu).then_inc(shg_ready, 1)
            a.activation(h2r[0], h2, ACT.Copy).then_inc(h2r_hi, 1)
            def hi(i, b, q):
                a.activation(w_hi(q), w_raw(b, q), ACT.Copy).then_inc(gu_hi if q < 4 else dn_hi, 1)

            a.wait_ge(tabs_ready, 1)
            more = a.value_load(tab[0:1, 0:1], min_val=1, max_val=ITEMS // 2 - 1)
            for i in range(0, 4 * KD, 2):
                a.wait_ge(gather_ps, i + 1)
                a.activation(hs[:, i % KD, (i // KD) * W:(i // KD) * W + W], bank[0][:, :], ACT.Copy).then_inc(gather_out_act, 1)
                if i >= 2 * KD - 4 and i % 4 == 2 and i < 4 * KD - 4:
                    if i == 2 * KD - 2:
                        a.wait_ge(gu_in[0], 16)
                    hi(0, 0, (i - 2 * KD + 4) // 4)
            a.wait_ge(gather_out_dve, 2 * KD)
            a.wait_ge(gather_out_act, 2 * KD)
            a.wait_ge(pad_ready, 1)

            def next_input(i):
                p = a.value_load(tab[0:1, bass.ds(i + 1, 1)], min_val=0, max_val=SLOTS)
                a.activation(hT2[:, 0], hs[:, :, bass.ds(p, PART)], ACT.Copy).then_inc(hT_hi, 1)

            next_input(0)
            a.wait_ge(dn_in[0], 16)
            a.wait_ge(gather_ps, 4 * KD)
            hi(0, 0, 4)
            hi(0, 0, 5)

            def item(i, g, b, last):
                nb = 1 - b
                if not last:
                    a.wait_ge(gu_in[nb], g * 16 + (16 if b == 0 else 32))
                    for q in range(2):
                        a.wait_ge(gu_used, i * 4 + q + 1)
                        hi(i + 1, nb, q)
                a.wait_ge(gu_used, i * 4 + 4)
                a.activation(sg[:, :], psU[:, 0:F], ACT.Silu).then_inc(silu_done, 1)
                if not last:
                    hi(i + 1, nb, 2)
                a.wait_ge(t_done, i + 1)
                a.activation(aT2[:, 0], psM[:, 0:F].rearrange("p (k n) -> p k n", k=KF), ACT.Copy).then_inc(aT_hi, 1)
                if not last:
                    next_input(i + 1)
                    hi(i + 1, nb, 3)
                a.wait_ge(down_done, i + 1)
                if not last:
                    a.wait_ge(dn_in[nb], g * 16 + (16 if b == 0 else 32))
                    hi(i + 1, nb, 4)
                    hi(i + 1, nb, 5)
                a.wait_ge(st_ready, i + 2)
                for n in range(2):
                    a.activation(y2[:, 0, n * W:(n + 1) * W], psY[n][:, :], ACT.Copy, scale=wcol[:, 0:1]).then_inc(y_hi, 1)

            with a.Fori(0, more) as g:
                for b in range(2):
                    item(g * 2 + b, g, b, False)
            for b in range(2):
                item(more * 2 + b, more, b, b == 1)

        @block.vector
        def _(v):
            chain = [0]

            def link(ins):
                chain[0] += 1
                ins.then_inc(dve_chain, 1)
                v.wait_ge(dve_chain, chain[0])

            def rstd(t=0, n=TH):
                v.tensor_scalar(st2[:, 2 + t:2 + t + n], st2[:, t:t + n], 1.0 / D, EPS, ALU.mult, ALU.add).then_inc(sqrt_in, 1)

            def rstd2(done, t=0, n=TH):
                ms, root, r0, e, r1 = (st2[:, c + t:c + t + n] for c in (2, 4, 6, 8, 14))
                v.wait_ge(sqrt_out, done)
                link(v.reciprocal(r0, root))
                link(v.tensor_tensor(e, r0, r0, ALU.mult))
                link(v.tensor_tensor(e, e, ms, ALU.mult))
                link(v.tensor_scalar(e, e, -0.5, 1.5, ALU.mult, ALU.add))
                link(v.tensor_tensor(r1, r0, e, ALU.mult))

            def ada_sum(j, n, ks):
                w = piece(n)
                for k in ks:
                    if k == 0:
                        v.wait_ge(piece_in[n % NBUF], 16 * (n // NBUF + 1))
                        if j >= 2:
                            v.wait_ge(ada_done, j - 1)
                        ins = v.tensor_scalar(adac[:, j % 2, :], w[:, 0, :], sc[:, 0:1], None, ALU.mult)
                    else:
                        ins = v.scalar_tensor_tensor(adac[:, j % 2, :], w[:, k, :], sc[:, k:k + 1], adac[:, j % 2, :],
                                                     ALU.mult, ALU.add)
                    link(ins)
                    if k == KD - 1:
                        if j == 0:
                            v.wait_ge(bada_in, 16)
                        row = slice(32 * (j // 3), 32 * (j // 3) + 1)
                        v.tensor_tensor(adac[row, j % 2, :], adac[row, j % 2, :], bada[row, j % 3, :],
                                        ALU.add).then_inc(adac_ready, 1)

            def ada_row(j):
                v.wait_ge(ada_done, j + 1)
                dst = (shift1, G1)[j // 2][:, (j % 2) * W:(j % 2) * W + W]
                if j < 2:
                    v.tensor_copy(dst, bank[ADA_B[j]][:, :]).then_inc(ada1_out, 1)
                else:
                    v.wait_ge(n1_in, 16)
                    v.scalar_tensor_tensor(dst, bank[ADA_B[j]][:, :], 1.0, dst, ALU.add, ALU.mult).then_inc(ada1_out, 1)

            v.wait_ge(sc_ready, 1)
            for j in range(4):
                ada_sum(j, ADA1 + j, range(KD))
                if j == 1:
                    v.wait_ge(ss_ready, TH)
                    rstd()
                if j == 2:
                    rstd2(1)
                if j >= 1:
                    ada_row(j - 1)
            ada_row(3)
            v.wait_ge(ada1_out, 4)
            for t in range(TH):
                link(v.scalar_tensor_tensor(h1[:, t, :], xs[:, t, :], st2[:, 14 + t:15 + t], G1, ALU.mult, ALU.mult))
                v.tensor_tensor(h1[:, t, :], h1[:, t, :], shift1, ALU.add).then_inc(h1_ready, 1)
            v.wait_ge(rowsT, 1)
            v.tensor_copy(convc[:, :, :], bank[0][:, 64:64 + KC * (TAPS + 3)].rearrange("p (k n) -> p k n", k=KC))
            v.tensor_copy(qkg[:, 1:2], bank[0][:, 241:242])
            v.tensor_scalar(qkg[:, 0:1], bank[0][:, 240:241], HD ** -0.5, None, ALU.mult).then_inc(rows_out, 1)

            v.wait_ge(upad_zero, 1)
            for u in (2, 3):
                v.wait_ge(unit_done, u + 1)
                v.wait_ge(unit_out_act, u - 1)
                k = 2 * (u - 2)
                v.tensor_tensor(upad[:, k:k + 2, TAPS - 1:TAPS - 1 + SEQ],
                                bank[UNIT_B[u % 4]][:, :].rearrange("p (k n) -> p k n", k=2),
                                gsig[:, k:k + 2, :], ALU.mult).then_inc(unit_out_dve, 1)
            v.wait_ge(rows_out, 1)
            v.wait_ge(unit_out_dve, 2)
            for k in range(KC):
                v.tensor_scalar(cacc[:, k, :], upad[:, k, 0:SEQ], convc[:, k, 0:1], convc[:, k, TAPS:TAPS + 1],
                                ALU.mult, ALU.add).then_inc(conv_step, 1)
            taps_done = [1]

            def taps(n):
                first, last = taps_done[0], min(taps_done[0] + n, TAPS)
                taps_done[0] = last
                if first == last:
                    return
                with v.Fori(first, last) as j:
                    for k in range(KC):
                        v.wait_ge(conv_step, (j - 1) * KC + k + 1)
                        v.scalar_tensor_tensor(cacc[:, k, :], upad[:, k, bass.ds(j, SEQ)], convc[:, k, bass.ds(j, 1)],
                                               cacc[:, k, :], ALU.mult, ALU.add).then_inc(conv_step, 1)

            taps(17)
            v.wait_ge(lf_ready, 1)
            link(v.tensor_scalar(za, zf, 0.0, None, ALU.min))
            link(v.tensor_tensor(zl, za, zl, ALU.subtract))
            link(v.memset(za, 1.0))
            link(v.tensor_tensor_scan(cum, za, zl, 0.0, ALU.mult, ALU.add))
            v.wait_ge(aug_zero, 4)
            for par in range(2):
                v.tensor_copy(AU[64 * par:64 * par + HEADS, :, :], cum.unsqueeze(1).broadcast_to([HEADS, KC, SEQ]))
                ins = v.tensor_scalar(BU[64 * par + 32:64 * par + 32 + HEADS, :, :],
                                      cum.unsqueeze(1).broadcast_to([HEADS, KC, SEQ]), -1.0, None, ALU.mult)
            ins.then_inc(aug_ready, 1)

            v.wait_ge(qkstat, 1)
            v.tensor_scalar(rs16[:, :], bank[6][0:16, 0:SEQ], EPS, None, ALU.add).then_inc(qkstat, 1)
            v.wait_ge(qkrstd, 1)
            v.reciprocal(rs16[:, :], rs16[:, :]).then_inc(qkrstd, 1)
            for i in range(4):
                v.wait_ge(qkb_done, i + 1)
                v.scalar_tensor_tensor(qk[:, 2 * i:2 * i + 2, :], qk[:, 2 * i:2 * i + 2, :],
                                       qkg[:, i // 2:i // 2 + 1],
                                       bank[UNIT_B[i % 4]][:, :].rearrange("p (k n) -> p k n", k=2),
                                       ALU.mult, ALU.mult).then_inc(qk_ready, 1)
            def head_max(h):
                ps = bank[S_B[h % 2]]
                v.wait_ge(s_done, h + 1)
                o = 6 if h % 2 == 0 else 10
                v.tensor_reduce(st2[:, o:o + 1], ps[:, 0:PART], AX, ALU.max, negate=True).then_inc(max_done, 1)
                v.tensor_reduce(st2[:, o + 1:o + 2], ps[:, PART:3 * PART], AX, ALU.max, negate=True).then_inc(max_done, 1)

            def head_norm(h):
                o = 8 if h % 2 == 0 else 12
                v.wait_ge(exp_done, h + 1)
                link(v.reciprocal(st2[:, o:o + 2], st2[:, o:o + 2]))
                v.tensor_scalar(prob[:, h % 2, 0:PART], prob[:, h % 2, 0:PART], st2[:, o:o + 1], None, ALU.mult)
                v.tensor_scalar(prob[:, h % 2, PART:3 * PART], prob[:, h % 2, PART:3 * PART], st2[:, o + 1:o + 2],
                                None, ALU.mult).then_inc(p_ready, 1)

            def head_pT(h):
                v.wait_ge(pT_done, h + 1)
                if h >= 2:
                    v.wait_ge(o_done, h - 1)
                v.tensor_copy(probT[:, h % 2, :], bank[PT_B[h % 2]][:, 0:3 * PART]).then_inc(pT_out, 1)

            def head_out(h):
                if h % 2 == 1:
                    v.wait_ge(o_done, h + 1)
                    v.tensor_copy(oT[:, h // 2, :], bank[O_B][:, 0:SEQ]).then_inc(o_out, 1)

            for step in range(HEADS + 1):
                if step < HEADS:
                    head_max(step)
                taps(1)
                if step >= 1:
                    head_norm(step - 1)
                j = {1: 0, 2: 2, 4: 4, 6: 6}.get(step)
                if j is not None:
                    ada_sum(4 + j, ADA2[j], range(KD // 2))
                if step >= 1:
                    head_pT(step - 1)
                if j is not None:
                    ada_sum(4 + j, ADA2[j], range(KD // 2, KD))
                elif step > 0:
                    taps(1)
                if step >= 2:
                    head_out(step - 2)
            head_out(HEADS - 1)
            for i in range(2):
                v.wait_ge(mean_done, i + 1)
                v.tensor_tensor(cdif[:, 2 * i:2 * i + 2, :], cacc[:, 2 * i:2 * i + 2, :],
                                bank[6 + i][:, :].rearrange("p (k n) -> p k n", k=2), ALU.subtract).then_inc(dmu_ready, 1)
            v.wait_ge(var_done, 1)
            v.tensor_scalar(rs16[0:8, :], bank[0][0:8, 0:SEQ], EPS, None, ALU.add).then_inc(crstd, 1)
            v.wait_ge(crstd, 2)
            v.reciprocal(rs16[0:8, :], rs16[0:8, :]).then_inc(crstd, 1)
            for i in range(2):
                v.wait_ge(cb_done, i + 1)
                v.tensor_tensor(sqb[:, 2 * i:2 * i + 2, :], cdif[:, 2 * i:2 * i + 2, :],
                                bank[1 + i][:, :].rearrange("p (k n) -> p k n", k=2), ALU.mult).then_inc(yn_ready, 1)
            for i in range(4):
                v.wait_ge(ya_done, i + 1)
                if i == 0:
                    v.wait_ge(gates_ready, 1)
                v.tensor_tensor(gates[:, KD + 2 * i:KD + 2 * i + 2, :], gates[:, KD + 2 * i:KD + 2 * i + 2, :],
                                bank[3 + i][:, :].rearrange("p (k n) -> p k n", k=2), ALU.mult).then_inc(ya_out, 1)
            for i in range(4):
                v.wait_ge(yc_done, i + 1)
                if i == 0:
                    v.wait_ge(gates_ready, 2)
                g = gates[:, 2 * i:2 * i + 2, :]
                v.tensor_tensor(g, g, bank[3 + i][:, :].rearrange("p (k n) -> p k n", k=2), ALU.mult).then_inc(yc_out, 1)
                v.wait_ge(yc_out, i + 1)
                v.tensor_tensor(g, g, gates[:, KD + 2 * i:KD + 2 * i + 2, :], ALU.add).then_inc(merged, 1)
            v.wait_ge(ada2_out, 8)
            v.wait_ge(n2_in, 16)
            link(v.tensor_tensor(G2, G2, n2g, ALU.mult))
            tmp = cacc[:, 0:2, :].rearrange("p k n -> p (k n)")
            for t in range(TH):
                for n in range(2):
                    i = 2 * t + n
                    v.wait_ge(mo_done, i + 1)
                    link(v.tensor_tensor(tmp, bank[i][:, :], gate1[:, n * W:(n + 1) * W], ALU.mult))
                    v.tensor_tensor(xs[:, t, n * W:(n + 1) * W], xs[:, t, n * W:(n + 1) * W], tmp, ALU.add).then_inc(x1_ready, 1)
                    v.wait_ge(x1_ready, i + 1)
                v.wait_ge(ss_ready, TH + t + 1)
                rstd(t, 1)
                rstd2(2 + t, t, 1)
                link(v.scalar_tensor_tensor(h2[:, t, :], xs[:, t, :], st2[:, 14 + t:15 + t], G2, ALU.mult, ALU.mult))
                v.tensor_tensor(h2[:, t, :], h2[:, t, :], shift2, ALU.add).then_inc(h2_ready, 1)
            v.wait_ge(logit_done, 1)
            v.tensor_scalar(r["z"], bank[0][:, 0:TH * E].rearrange("p (t e) -> p t e", t=TH), LOWEST, None,
                            ALU.max).then_inc(z_ready, 1)
            v.wait_ge(ez_ready, 1)
            link(v.tensor_scalar(r["e"], r["e"], 1.0, None, ALU.add))
            link(v.reciprocal(r["s"], r["e"]))
            v.wait_ge(rb_in, 16)
            link(v.tensor_tensor(r["b"], r["s"], rbias.unsqueeze(1).broadcast_to([PART, TH, E]), ALU.add))
            for t in range(TH):
                for g in range(GROUPS):
                    ins = v.max(top2[:, t, g, :], r["b"][:, t, g * EPG:(g + 1) * EPG])
            link(ins)
            link(v.tensor_tensor(gs, top2[:, :, :, 0], top2[:, :, :, 1], ALU.add))
            mine = gs.unsqueeze(3).broadcast_to([PART, TH, GROUPS, GROUPS])
            theirs = gs.unsqueeze(2).broadcast_to([PART, TH, GROUPS, GROUPS])
            v.wait_ge(sel_ready, 1)
            for t in range(TH):
                v.tensor_tensor(cmp1[:, t], theirs[:, t], mine[:, t], ALU.is_gt)
                ins = v.tensor_tensor(cmp2[:, t], theirs[:, t], mine[:, t], ALU.is_equal)
            link(ins)
            link(v.tensor_tensor(cmp2, cmp2, lower8[:, :, :].unsqueeze(1).broadcast_to([PART, TH, GROUPS, GROUPS]), ALU.mult))
            link(v.tensor_tensor(cmp1, cmp1, cmp2, ALU.add))
            link(v.tensor_reduce(grank, cmp1, AX, ALU.add))
            link(v.tensor_scalar(gmask, grank, float(TOPG), None, ALU.is_lt))
            em = gmask.unsqueeze(3).broadcast_to([PART, TH, GROUPS, EPG])
            grp = {n: r[n].rearrange("p t (g e) -> p t g e", g=GROUPS) for n in ("b", "m", "pre")}
            for t in range(TH):
                v.tensor_tensor(grp["m"][:, t], grp["b"][:, t], em[:, t], ALU.mult)
                ins = v.tensor_scalar(grp["pre"][:, t], em[:, t], -NEG, NEG, ALU.mult, ALU.add)
            link(ins)
            link(v.tensor_tensor(r["m"], r["m"], r["pre"], ALU.add))
            for t in range(TH):
                ins = v.max(top8[:, t, :], r["m"][:, t, :])
            link(ins)
            for t in range(TH):
                ins = v.match_replace(r["rep"][:, t, :], top8[:, t, :], r["m"][:, t, :], 2.0 * NEG)
            link(ins)
            v.tensor_tensor(r["sel"], r["rep"], r["m"], ALU.not_equal).then_inc(sel_out, 1)
            v.wait_ge(sel_out, 1)
            link(v.tensor_tensor(wt[:, :, :], r["s"], r["sel"], ALU.mult))
            link(v.tensor_reduce(st2[:, 0:2], wt[:, :, :], AX, ALU.add))
            link(v.reciprocal(st2[:, 0:2], st2[:, 0:2]))
            for t in range(TH):
                ins = v.tensor_scalar(wt[:, t, :], wt[:, t, :], st2[:, t:t + 1], ROUTED_SCALE, ALU.mult, ALU.mult)
            link(ins)
            v.wait_ge(shg_ready, 1)
            v.wait_ge(sgu_done, 2)
            v.tensor_tensor(shT, shg, bank[2][:, :].rearrange("p (k n) -> p k n", k=2), ALU.mult).then_inc(shT_ready, 1)
            v.wait_ge(rank_done, 1)
            link(v.tensor_copy(cnt, bank[0][:, 128:128 + E]))
            link(v.tensor_tensor_scan(incl, ones[:, 0:E], cnt, 0.0, ALU.mult, ALU.add))
            link(v.tensor_tensor(first, incl, cnt, ALU.subtract))
            link(v.tensor_tensor(slotm[:, :, :], bank[0][:, 256:256 + TH * E].rearrange("p (t e) -> p t e", t=TH),
                                 first.unsqueeze(1).broadcast_to([PART, TH, E]), ALU.add))
            link(v.scalar_tensor_tensor(slotm[:, :, :], slotm[:, :, :], 1.0, r["sel"], ALU.add, ALU.mult))
            v.tensor_scalar(slotm[:, :, :], slotm[:, :, :], -1.0, None, ALU.add).then_inc(slotT_out, 1)
            link(v.tensor_copy(ecol[:, 0:1], bank[0][0:E, 448:449]))
            link(v.tensor_scalar(ecol2[:, 0:1], ecol[:, 0:1], 0.0, None, ALU.is_gt))
            link(v.tensor_scalar(ecol2[:, 1:2], ecol[:, 0:1], float(PART), None, ALU.is_gt))
            v.tensor_tensor(ecol[:, 1:2], ecol2[:, 0:1], ecol2[:, 1:2], ALU.add).then_inc(ecol_out, 1)
            v.wait_ge(ecum_done, 1)
            v.wait_ge(slotT_ps, 1)
            link(v.tensor_copy(ecum, bank[3][0:E, 256:258]))
            link(v.tensor_copy(slotT, bank[3][0:E, 0:SEQ]))
            link(v.tensor_tensor(eend, ecum, ecol, ALU.add))
            v.wait_ge(iota_ready, 1)
            j = iota[0:E, 0:ITEMS]
            link(v.tensor_scalar(jt[:, 0, :], j, ecum[:, 1:2], None, ALU.is_ge))
            link(v.scalar_tensor_tensor(jt[:, 1, :], j, eend[:, 1:2], jt[:, 0, :], ALU.is_lt, ALU.mult))
            link(v.tensor_scalar(jt[:, 0, :], j, ecum[:, 1:2], float(PART), ALU.subtract, ALU.mult))
            v.scalar_tensor_tensor(jt[:, 2, :], jt[:, 0, :], ecum[:, 0:1], jt[:, 1, :], ALU.add, ALU.mult).then_inc(tabs_ps_in, 1)
            def emat(q):
                qs = slice(q * W, (q + 1) * W)
                link(v.tensor_scalar(Emat[:, qs], iota[0:E, qs], eend[:, 0:1], None, ALU.is_ge))
                v.scalar_tensor_tensor(Emat[:, qs], iota[0:E, qs], ecum[:, 0:1], Emat[:, qs].bitcast(fp32),
                                       ALU.is_ge, ALU.subtract).then_inc(E_ready, 1)

            emat(0)
            link(v.tensor_scalar(nit[:, :], cnt, 0.0, None, ALU.is_gt))
            link(v.scalar_tensor_tensor(nit[:, :], cnt, float(PART), nit[:, :], ALU.is_gt, ALU.add))
            link(v.memset(cumi[:, 0:1], 0.0))
            link(v.tensor_tensor_scan(cumi[:, 1:E + 1], ones[:, 0:E], nit[:, :], 0.0, ALU.mult, ALU.add))
            total = cumi[0:1, E:E + 1]
            half = ITEMS // 2
            j = jt[0:1, 3, 0:half]
            link(v.tensor_scalar(j, iota[0:1, 0:half], 2.0, None, ALU.mult))
            link(v.tensor_scalar(j, j, total, None, ALU.is_lt))
            link(v.tensor_reduce(cumi[0:1, 0:1], j, AX, ALU.add))
            link(v.tensor_scalar(tab[0:1, 0:1], cumi[0:1, 0:1], -1.0, None, ALU.add))
            behind = jt[0:1, 4, :]
            link(v.tensor_scalar(behind, iota[0:1, 0:ITEMS], total, float(SLOTS), ALU.is_ge, ALU.mult))
            v.wait_ge(tabs_ps, 1)
            v.tensor_tensor(tab[0:1, 1:1 + ITEMS], bank[3][0:1, 0:ITEMS], behind, ALU.add)
            v.tensor_copy(tab[0:1, 1 + ITEMS:1 + 2 * ITEMS], bank[3][0:1, ITEMS:2 * ITEMS]).then_inc(tabs_ready, 1)
            v.wait_ge(h2r_hi, 1)
            v.wait_ge(h2T_ps, 4)
            v.tensor_tensor(h2r[1], h2, h2r[0].bitcast(fp32), ALU.subtract).then_inc(h2r_lo, 1)
            def lo(i, b, q):
                v.wait_ge(gu_hi, i * 4 + q + 1)
                v.tensor_tensor(w_lo(q), w_raw(b, q), w_hi(q).bitcast(fp32), ALU.subtract).then_inc(gu_lo, 1)

            def select(q):
                for t in range(TH):
                    v.wait_ge(m1_done, 2 * q + t + 1)
                    if q >= 2:
                        v.wait_ge(gather_ps, KD * (q - 1))
                    v.tensor_tensor(SS[:, q % 2, t, :], bank[2 + t][:, :], iota[:, q * W:(q + 1) * W],
                                    ALU.is_equal).then_inc(SS_ready, 1)

            select(0)
            for q in range(4):
                for i in range(KD * q + 1, KD * (q + 1), 2):
                    if i == KD * q + 3 and q < 3:
                        emat(q + 1)
                    if i == KD * q + 5 and q < 3:
                        select(q + 1)
                    v.wait_ge(gather_ps, i + 1)
                    v.tensor_copy(hs[:, i % KD, q * W:(q + 1) * W], bank[1][:, :]).then_inc(gather_out_dve, 1)
                    if i >= 2 * KD and i % 4 == 1:
                        lo(0, 0, (i - 2 * KD) // 4)
            more = v.value_load(tab[0:1, 0:1], min_val=1, max_val=ITEMS // 2 - 1)
            v.wait_ge(gather_ps, 4 * KD)
            v.tensor_scalar(ST[:, :], iota[:, 0:SEQ], 0.0, None, ALU.mult).then_inc(st_ready, 1)

            def build_si(n):
                p = v.value_load(tab[0:1, bass.ds(n + 1, 1)], min_val=0, max_val=SLOTS)
                e = v.value_load(tab[0:1, bass.ds(n + (1 + ITEMS), 1)], min_val=0, max_val=E - 1)
                for t in range(TH):
                    ins = v.tensor_scalar(SI[:, t, :], iota[:, bass.ds(p, PART)], slotm[:, t, bass.ds(e, 1)],
                                          wt[:, t, bass.ds(e, 1)], ALU.is_equal, ALU.mult)
                ins.then_inc(si_ready, 1)

            def input_lo(i):
                p = v.value_load(tab[0:1, bass.ds(i + 1, 1)], min_val=0, max_val=SLOTS)
                v.wait_ge(hT_hi, i + 1)
                v.tensor_tensor(hT2[:, 1], hs[:, :, bass.ds(p, PART)], hT2[:, 0].bitcast(fp32),
                                ALU.subtract).then_inc(hT_lo, 1)

            input_lo(0)
            v.tensor_scalar(y2[:, :, :], iota[:, 0:2 * D].rearrange("p (s d) -> p s d", s=2), 0.0, None,
                            ALU.mult).then_inc(y_lo, 2)
            build_si(0)

            def item(i, b, last):
                nb = 1 - b
                v.wait_ge(silu_done, i + 1)
                v.tensor_tensor(act[:, :], sg[:, :], psU[:, F:2 * F], ALU.mult).then_inc(act_ready, 1)
                if not last:
                    lo(i + 1, nb, 0)
                v.wait_ge(aT_hi, i + 1)
                v.tensor_tensor(aT2[:, 1], psM[:, 0:F].rearrange("p (k n) -> p k n", k=KF), aT2[:, 0].bitcast(fp32),
                                ALU.subtract).then_inc(aT_lo, 1)
                v.wait_ge(sit_done, i + 1)
                v.tensor_scalar(ST[:, :], psU[:, 0:SEQ], 0.0, None, ALU.is_gt)
                v.reduce_sum(wcol[:, 0:1], psU[:, 0:SEQ], AX).then_inc(st_ready, 1)
                if not last:
                    input_lo(i + 1)
                    lo(i + 1, nb, 1)
                    lo(i + 1, nb, 2)
                    build_si(i + 1)
                    lo(i + 1, nb, 3)
                for n in range(2):
                    v.wait_ge(y_hi, i * 2 + n + 1)
                    v.scalar_tensor_tensor(y2[:, 1, n * W:(n + 1) * W], psY[n][:, :], wcol[:, 0:1],
                                           y2[:, 0, n * W:(n + 1) * W].bitcast(fp32), ALU.mult, ALU.subtract).then_inc(y_lo, 1)

            with v.Fori(0, more) as g:
                for b in range(2):
                    item(g * 2 + b, b, False)
            for b in range(2):
                item(more * 2 + b, b, b == 1)
            v.wait_ge(all_done, 1)
            for t in range(TH):
                for n in range(2):
                    link(v.tensor_tensor(iota[:, 0:W], acc[2 * t + n][:, :], gate2[:, n * W:(n + 1) * W], ALU.mult))
                    xo = xs[:, t, n * W:(n + 1) * W]
                    v.tensor_tensor(xo, xo, iota[:, 0:W], ALU.add).then_inc(fin, 1)
                    v.wait_ge(fin, 2 * t + n + 1)

        @block.tensor
        def _(pe):
            mm, tr = nc.tensor.matmul, nc.tensor.transpose

            def arrived(n):
                pe.wait_ge(piece_in[n % NBUF], 16 * (n // NBUF + 1))
                return piece(n)

            pe.wait_ge(cst, 2)
            pe.wait_ge(c_in, 16)
            tr(bank[5][:, 0:KD], crow, ident[0:KD, 0:KD]).then_inc(cT_in, 1)
            def ada(j, b):
                if j < 4 or j % 2 == 0:
                    pe.wait_ge(adac_ready, j + 1 if j < 4 else j // 2 + 3)
                else:
                    pe.wait_ge(adac_pool, (j - 3) // 2)
                mm(b[:, :], ones[:, :], adac[:, j % 2, :], start=True, stop=True).then_inc(ada_done, 1)

            for j in range(4):
                ada(j, bank[ADA_B[j]])
            pe.wait_ge(row_in, 16 * 8)
            n = TAPS + 3
            for k in range(KC):
                tr(bank[0][:, 64 + n * k:64 + n * (k + 1)], convrow[:, k * PART:(k + 1) * PART], ident[0:n, 0:n])
            tr(bank[0][:, 240:242], qkrow, ident[0:2, 0:2]).then_inc(rowsT, 1)
            pe.wait_ge(sc_ready, 1)
            for i in range(4):
                for kk in range(2):
                    for t in range(TH):
                        if i == 0 and kk == 0:
                            pe.wait_ge(h1_ready, t + 1)
                        if i == 3 and kk == 0 and t == 0:
                            pe.wait_ge(rows_out, 1)
                        k = 2 * i + kk
                        ins = tr(bank[H1T_B[i]][:, kk * SEQ + t * PART:kk * SEQ + (t + 1) * PART],
                                 h1[:, t, k * PART:(k + 1) * PART], ident[:, :])
                ins.then_inc(h1T_ps, 1)
            pe.wait_ge(h1T_ready, 4)
            pe.wait_ge(ada1_out, 4)
            def project_in(u, halves):
                w = piece(INP + u // 2 if u < 10 else GATEP + 3 * ((u - 10) // 2))
                b = bank[UNIT_B[u % 4] if u < 10 else M_B[u % 2]]
                for kk in halves:
                    m = 2 * (u % 2) + kk
                    for k in range(KD):
                        ins = mm(b[:, kk * SEQ:(kk + 1) * SEQ], w[:, k, m * PART:(m + 1) * PART],
                                 h1T[:, k, :], start=(k == 0), stop=(k == KD - 1))
                if kk == 1:
                    ins.then_inc(unit_done, 1)

            for u, kind in enumerate(UNITS[:10]):
                if u >= 4:
                    p = u - 4
                    if p in (2, 3):
                        pe.wait_ge(unit_out_dve, p - 1)
                    else:
                        pe.wait_ge(unit_out_act, p + 1 if p < 2 else p - 1)
                w = arrived(INP + u // 2)
                if kind == "v":
                    for k in range(KD):
                        ins = mm(bank[UNIT_B[u % 4]][:, :], h1T[:, k, (u % 2) * PART:(u % 2 + 1) * PART], w[:, k, :],
                                 start=(k == 0), stop=(k == KD - 1))
                    ins.then_inc(unit_done, 1)
                else:
                    project_in(u, (0, 1))
                if u == 7:
                    pe.wait_ge(wf_in, 16)
                    for k in range(KD):
                        ins = mm(bank[5][0:HEADS, 0:SEQ], wf[:, k, :], h1T[:, k, :], start=(k == 0), stop=(k == KD - 1))
                    ins.then_inc(f_done, 1)
                if u == 8:
                    pe.wait_ge(unit_out_act, 6)
                    pe.wait_ge(sel_ready, 1)
                    for k in range(2 * KC):
                        ins = mm(bank[6][0:16, 0:SEQ], headsum[:, k, :], qksq[:, k, :], start=(k == 0), stop=(k == 2 * KC - 1))
                    ins.then_inc(qkstat, 1)
            pe.wait_ge(qkrstd, 2)
            pe.wait_ge(unit_out_act, 8)
            for i in range(4):
                for kk in range(2):
                    ins = mm(bank[UNIT_B[i % 4]][:, kk * SEQ:(kk + 1) * SEQ], headrow[:, 2 * i + kk, :], rs16[:, :],
                             start=True, stop=True)
                ins.then_inc(qkb_done, 1)

            def scores(h):
                b, base, j = bank[S_B[h % 2]], 64 * (h % 2), h // 2
                if h >= 2:
                    pe.wait_ge(exp_done, h - 1)
                for q, o, keys in ((0, 0, PART), (1, PART, SEQ)):
                    qs = slice(q * PART, (q + 1) * PART)
                    mm(b[:, o:o + keys], qk[base:base + HD, j, qs], qk[base:base + HD, KC + j, 0:keys], start=True, stop=False)
                    mm(b[:, o:o + keys], AU[base:base + 40, j, qs], BU[base:base + 40, j, 0:keys], start=False, stop=False)
                    ins = mm(b[:, o:o + keys], ident[:, :], causal[:, 2 * PART - keys:], start=False, stop=True)
                ins.then_inc(s_done, 1)

            def transposes(h):
                pe.wait_ge(p_ready, h + 1)
                if h >= 2:
                    pe.wait_ge(pT_out, h - 1)
                for i in range(3):
                    o = i * PART
                    ins = tr(bank[PT_B[h % 2]][:, o:o + PART], prob[:, h % 2, o:o + PART], ident[:, :])
                ins.then_inc(pT_done, 1)

            def values(h):
                base, j = 64 * (h % 2), h // 2
                pe.wait_ge(pT_out, h + 1)
                if h % 2 == 0 and h >= 2:
                    pe.wait_ge(o_out, j)
                b = bank[O_B]
                mm(b[base:base + HD, 0:PART], v_sb[:, 0, h * HD:(h + 1) * HD], probT[:, h % 2, 0:PART], start=True, stop=True)
                mm(b[base:base + HD, PART:SEQ], v_sb[:, 0, h * HD:(h + 1) * HD], probT[:, h % 2, PART:SEQ], start=True, stop=False)
                mm(b[base:base + HD, PART:SEQ], v_sb[:, 1, h * HD:(h + 1) * HD], probT[:, h % 2, SEQ:3 * PART],
                   start=False, stop=True).then_inc(o_done, 1)

            pe.wait_ge(qk_ready, 4)
            pe.wait_ge(aug_ready, 1)
            scores(0)
            for h in range(HEADS):
                if h + 1 < HEADS:
                    scores(h + 1)
                arrived(GATEP + 3 * (h // 2))
                if h >= 2:
                    pe.wait_ge(unit_out_act, 8 + h - 1)
                project_in(10 + h, (0,))
                transposes(h)
                project_in(10 + h, (1,))
                values(h)
                if h >= 1:
                    pe.wait_ge(ada2_out, h)
                if h + 1 < HEADS:
                    ada(4 + h, bank[ADA2_B])
            def project(w, src, i, done):
                for kk in range(2):
                    m = 2 * i + kk
                    for k in range(KC):
                        ins = mm(bank[3 + i][:, kk * SEQ:(kk + 1) * SEQ], w[:, k, m * PART:(m + 1) * PART],
                                 src[:, k, :], start=(k == 0), stop=(k == KC - 1))
                ins.then_inc(done, 1)

            wa = arrived(AOUT)
            pe.wait_ge(conv_step, TAPS * KC)
            pe.wait_ge(unit_out_act, 16)
            for i in range(2):
                for kk in range(2):
                    ins = mm(bank[6 + i][:, kk * SEQ:(kk + 1) * SEQ], blk[:, :], cacc[:, 2 * i + kk, :], start=True, stop=True)
                ins.then_inc(mean_done, 1)
            pe.wait_ge(o_out, 4)
            project(wa, oT, 0, ya_done)
            ada(3 + HEADS, bank[ADA2_B])
            pe.wait_ge(csq_ready, 1)
            for k in range(KC):
                ins = mm(bank[0][0:8, 0:SEQ], headsum[:, k, 0:8], sqb[:, k, :], start=(k == 0), stop=(k == KC - 1))
            ins.then_inc(var_done, 1)
            project(wa, oT, 1, ya_done)
            pe.wait_ge(ada2_out, 8)
            project(wa, oT, 2, ya_done)
            pe.wait_ge(crstd, 3)
            for i in range(2):
                for kk in range(2):
                    ins = mm(bank[1 + i][:, kk * SEQ:(kk + 1) * SEQ], headrow[0:8, 2 * i + kk, :], rs16[0:8, :], start=True, stop=True)
                ins.then_inc(cb_done, 1)
            pe.wait_ge(dmu_ready, 2)
            project(wa, oT, 3, ya_done)
            w = arrived(COUT)
            pe.wait_ge(cT_ready, KC)
            for i in range(4):
                pe.wait_ge(ya_out, i + 1)
                project(w, cacc, i, yc_done)
            pe.wait_ge(merged, 4)
            for t in range(TH):
                for n in range(2):
                    w = arrived(WOUT + n)
                    for k in range(KD):
                        ins = mm(bank[2 * t + n][:, :], gates[:, k, t * PART:(t + 1) * PART], w[:, k, :],
                                 start=(k == 0), stop=(k == KD - 1))
                    ins.then_inc(mo_done, 1)
            pe.wait_ge(yc_out, 4)
            for t in range(TH):
                ts = slice(t * PART, (t + 1) * PART)
                pe.wait_ge(h2_ready, t + 1)
                for i in range(2):
                    for kk in range(4):
                        k = 4 * i + kk
                        ins = tr(bank[4 + 2 * t + i][:, kk * PART:(kk + 1) * PART], h2[:, t, k * PART:(k + 1) * PART], ident[:, :])
                    ins.then_inc(h2T_ps, 1)
                pe.wait_ge(h2T_ready, 2 * t + 2)
                if t == 0:
                    pe.wait_ge(rw_in, 16)
                    w = arrived(SHGU)
                    pe.wait_ge(x1_ready, 2)
                for k in range(KD):
                    ins = mm(bank[0][:, t * E:(t + 1) * E], h2T[:, k, ts], router[:, k, :], start=(k == 0), stop=(k == KD - 1))
                if t == TH - 1:
                    ins.then_inc(logit_done, 1)
                for m in range(2 * KF):
                    if t == 0 and m == 2:
                        pe.wait_ge(x1_ready, 3)
                    for k in range(KD):
                        ins = mm(bank[1 + m // 2][:, (m % 2) * SEQ + t * PART:(m % 2) * SEQ + (t + 1) * PART],
                                 w[:, k, m * PART:(m + 1) * PART], h2T[:, k, ts], start=(k == 0), stop=(k == KD - 1))
                    if m % 2 == 1 and t == TH - 1:
                        ins.then_inc(sgu_done, 1)
            pe.wait_ge(sel_out, 1)
            sel = r["sel"]
            for t in range(TH):
                mm(bank[0][:, 128:128 + E], ones[:, :], sel[:, t, :], start=(t == 0), stop=(t == TH - 1))
            for t in range(TH):
                for s in range(t):
                    mm(bank[0][:, 256 + t * E:256 + (t + 1) * E], ones[:, :], sel[:, s, :], start=(s == 0), stop=False)
                mm(bank[0][:, 256 + t * E:256 + (t + 1) * E], before[:, :], sel[:, t, :], start=(t == 0), stop=True)
            for t in range(TH):
                ins = mm(bank[0][0:E, 448:449], sel[:, t, :], ones[:, 0:1], start=(t == 0), stop=(t == TH - 1))
            ins.then_inc(rank_done, 1)
            w = arrived(SHD)

            def shared_down(t, n):
                for k in range(KF):
                    ins = mm(acc[2 * t + n][:, :], shT[:, k, t * PART:(t + 1) * PART], w[:, k, n * W:(n + 1) * W],
                             start=(k == 0), stop=False)
                return ins

            pe.wait_ge(shT_ready, 1)
            shared_down(0, 0)
            shared_down(0, 1)
            pe.wait_ge(slotT_out, 1)
            for t in range(TH):
                ins = tr(bank[3][0:E, t * PART:(t + 1) * PART], slotm[:, t, :], ident[:, :])
            ins.then_inc(slotT_ps, 1)
            pe.wait_ge(ecol_out, 1)
            mm(bank[3][0:E, 256:258], before[0:E, 0:E], ecol, start=True, stop=True).then_inc(ecum_done, 1)
            shared_down(1, 0)
            pe.wait_ge(tabs_ps_in, 1)
            mm(bank[3][0:1, 0:ITEMS], ones[0:E, 0:1], jt[:, 2, :], start=True, stop=True)
            mm(bank[3][0:1, ITEMS:2 * ITEMS], enum[:, :], jt[:, 1, :], start=True, stop=True).then_inc(tabs_ps, 1)
            shared_down(1, 1).then_inc(shared_done, 1)
            pe.wait_ge(tabs_ready, 1)

            def select(q):
                pe.wait_ge(E_ready, q + 1)
                for t in range(TH):
                    if q >= 1:
                        pe.wait_ge(SS_ready, 2 * (q - 1) + t + 1)
                    mm(bank[2 + t][:, :], slotT[:, t * PART:(t + 1) * PART], Emat[:, q * W:(q + 1) * W],
                       start=True, stop=True).then_inc(m1_done, 1)

            select(0)
            for q in range(4):
                pe.wait_ge(SS_ready, 2 * q + 2)
                if q == 0:
                    pe.wait_ge(h2r_lo, 1)
                for k in range(KD):
                    i = q * KD + k
                    if k == KD // 2 and q < 3:
                        select(q + 1)
                    if i >= 2:
                        pe.wait_ge((gather_out_act, gather_out_dve)[i % 2], i // 2)
                    for s in range(2):
                        for t in range(TH):
                            ins = mm(bank[i % 2][:, :], h2r[s][:, t, k * PART:(k + 1) * PART], SS[:, q % 2, t, :],
                                     start=(s == t == 0), stop=(s == 1 and t == TH - 1))
                    ins.then_inc(gather_ps, 1)
            pe.wait_ge(gather_out_act, 2 * KD)
            pe.wait_ge(gather_out_dve, 2 * KD)

            def three(out, a_hi, a_lo, b_hi, b_lo, start, stop):
                mm(out, a_hi, b_hi, start=start, stop=False)
                mm(out, a_hi, b_lo, start=False, stop=False)
                return mm(out, a_lo, b_hi, start=False, stop=stop)

            PASSES = [(t, n, s) for t in range(TH) for n in range(2) for s in range(2)]

            def scatter(passes, stop=False):
                for t, n, s in passes:
                    ins = mm(acc[2 * t + n][:, :], ST[:, t * PART:(t + 1) * PART], y2[:, s, n * W:(n + 1) * W],
                             start=False, stop=(stop and s == 1))
                return ins

            def item(i):
                pe.wait_ge(hT_lo, i + 1)
                pe.wait_ge(st_ready, i + 1)
                for q in range(4):
                    pe.wait_ge(gu_lo, i * 4 + q + 1)
                    wh, wl = (w(q).rearrange("p (k n) -> p k n", n=W) for w in (w_hi, w_lo))
                    for kk in range(2):
                        k = 2 * q + kk
                        ins = three(psU[:, :], hT2[:, 0, k], hT2[:, 1, k], wh[:, kk], wl[:, kk], k == 0, k == KD - 1)
                    ins.then_inc(gu_used, 1)
                pe.wait_ge(y_lo, i * 2 + 2)
                scatter(PASSES[:5])
                pe.wait_ge(act_ready, i + 1)
                for k in range(KF):
                    ins = tr(psM[:, k * PART:(k + 1) * PART], act[:, k * PART:(k + 1) * PART], ident[:, :])
                ins.then_inc(t_done, 1)
                scatter(PASSES[5:])
                pe.wait_ge(si_ready, i + 1)
                for t in range(TH):
                    ins = tr(psU[:, t * PART:(t + 1) * PART], SI[:, t, :], ident[:, :])
                ins.then_inc(sit_done, 1)
                pe.wait_ge(aT_hi, i + 1)
                for k in range(KF):
                    pe.wait_ge(dn_lo, i * 2 + k + 1)
                    for n in range(2):
                        for part_of in (w_hi, w_lo):
                            mm(psY[n][:, :], aT2[:, 0, k], part_of(4 + k)[:, n * W:(n + 1) * W],
                               start=(k == 0 and part_of is w_hi), stop=False)
                pe.wait_ge(aT_lo, i + 1)
                for n in range(2):
                    for k in range(KF):
                        ins = mm(psY[n][:, :], aT2[:, 1, k], w_hi(4 + k)[:, n * W:(n + 1) * W], start=False, stop=(k == KF - 1))
                ins.then_inc(down_done, 1)

            more = pe.value_load(tab[0:1, 0:1], min_val=1, max_val=ITEMS // 2 - 1)
            with pe.Fori(0, more + 1) as g:
                for b in range(2):
                    item(g * 2 + b)
            pe.wait_ge(st_ready, more * 2 + 3)
            pe.wait_ge(y_lo, more * 4 + 6)
            ins = scatter(PASSES, stop=True)
            ins.then_inc(all_done, 1)


_INS = ["x", "c", "w_ada", "b_ada", "norm1_g", "w_in", "w_dw", "b_dw", "conv_gn_g", "conv_gn_b", "w_conv_out",
        "q_norm_g", "k_norm_g", "b_forget", "w_attn_out", "w_out", "norm2_g", "w_router", "router_bias",
        "w_experts_gate_up", "w_experts_down", "w_shared_gate_up", "w_shared_down"]


def kernel(**inputs):
    import numpy as _np
    import concourse.bacc as _bacc
    from concourse import mybir as _mybir
    from concourse.bass_utils import run_bass_kernel_spmd as _run

    nc = _bacc.Bacc("TRN2", target_bir_lowering=False, num_devices=1)
    arrays, args = {}, []
    for name in _INS:
        a = _np.ascontiguousarray(inputs[name])
        arrays[f"in_{name}_dram"] = a
        args.append(nc.dram_tensor(f"in_{name}_dram", a.shape, _mybir.dt.from_np(a.dtype), kind="ExternalInput").ap())
    out = nc.dram_tensor("out_dram", inputs["x"].shape, _mybir.dt.float32, kind="ExternalOutput").ap()
    hybrid_conformer_fox_moe_block(nc, *args, out)
    return _run(nc, [arrays], core_ids=[0]).results[0]["out_dram"]
```
